# Optimizing a Trainium2 kernel written in Bass

```python
import math
import jax, jax.numpy as jnp
from jax import lax
import numpy as np

D_MODEL = 1024
BATCH = 1
SEQ = 256
DEPTH = 2

CHUNK = 64
RET_HEADS = 4
RET_DK = 128
RET_DV = 256
CA_HEADS = 8
CA_DH = 64
CA_LEFT_CHUNKS = 8
REL_CLIP = 256
DA_HEADS = 4
DA_DH = 64
Q_BLOCK = 128
FFN_HIDDEN = -(-8 * D_MODEL // (3 * 256)) * 256
ROPE_THETA = 10000.0
LN_EPS = 1e-5
NEG_INF = -1e30
DEEPNORM_ALPHA = (2.0 * DEPTH) ** 0.25
DEEPNORM_BETA = (8.0 * DEPTH) ** -0.25
N_BRANCHES = 3

RET_QK_W = RET_HEADS * RET_DK
RET_V_W = RET_HEADS * RET_DV
CA_W = CA_HEADS * CA_DH
DA_QK_W = 2 * DA_HEADS * DA_DH
DA_V_W = DA_HEADS * 2 * DA_DH
IN_WIDTHS = (RET_QK_W, RET_QK_W, RET_V_W, RET_V_W, CA_W, CA_W, CA_W, DA_QK_W, DA_QK_W, DA_V_W, N_BRANCHES * D_MODEL)
IN_IS_VALUE = (False, False, True, False, False, False, True, False, False, True, False)
IN_TOTAL = sum(IN_WIDTHS)


def _layer_norm(x, g, b):
    xf = x.astype(jnp.float32)
    mu = jnp.mean(xf, axis=-1, keepdims=True)
    var = jnp.mean(jnp.square(xf - mu), axis=-1, keepdims=True)
    return ((xf - mu) * lax.rsqrt(var + LN_EPS) * g.astype(jnp.float32) + b.astype(jnp.float32)).astype(x.dtype)

def _rms_norm(x, g):
    xf = x.astype(jnp.float32)
    y = xf * lax.rsqrt(jnp.mean(xf * xf, axis=-1, keepdims=True) + LN_EPS) * g.astype(jnp.float32)
    return y.astype(x.dtype)

def _rotary(x):
    S, d = x.shape[1], x.shape[-1]
    inv_freq = ROPE_THETA ** (-jnp.arange(0, d, 2, dtype=jnp.float32) / d)
    ang = jnp.arange(S, dtype=jnp.float32)[:, None] * inv_freq[None, :]
    cos = jnp.cos(ang)[None, :, None, :].astype(x.dtype)
    sin = jnp.sin(ang)[None, :, None, :].astype(x.dtype)
    x1, x2 = x[..., : d // 2], x[..., d // 2:]
    return jnp.concatenate([x1 * cos - x2 * sin, x2 * cos + x1 * sin], axis=-1)

def _retention(q, k, v, gate, norm_g):
    B, S, H, dk = q.shape
    dv = v.shape[-1]
    nc = S // CHUNK
    q = _rotary(q)
    k = _rotary(k) * (dk ** -0.5)
    log_gamma = jnp.log1p(-jnp.exp2(-5.0 - jnp.arange(H, dtype=jnp.float32)))
    pos = jnp.arange(CHUNK, dtype=jnp.float32)
    intra_decay = jnp.exp(log_gamma[:, None, None] * jnp.abs(pos[:, None] - pos[None, :]))
    q_decay = jnp.exp(log_gamma[None, :] * (pos[:, None] + 1.0))
    k_decay = jnp.exp(log_gamma[None, :] * (CHUNK - 1.0 - pos[:, None]))
    chunk_decay = jnp.exp(log_gamma * CHUNK)

    qc = q.reshape(B, nc, CHUNK, H, dk)
    kc = k.reshape(B, nc, CHUNK, H, dk)
    vc = v.reshape(B, nc, CHUNK, H, dv)
    scores = jnp.einsum('bcnhd,bcmhd->bchnm', qc, kc) * intra_decay.astype(q.dtype)
    o_intra = jnp.einsum('bchnm,bcmhe->bcnhe', scores, vc)

    def step(state, xs):
        q_i, k_i, v_i = xs
        o = jnp.einsum('bnhd,bhde->bnhe', q_i.astype(jnp.float32) * q_decay[None, :, :, None], state)
        kv = jnp.einsum('bmhd,bmhe->bhde', k_i.astype(jnp.float32) * k_decay[None, :, :, None], v_i.astype(jnp.float32))
        state = state * chunk_decay[None, :, None, None] + kv
        return state, o

    state0 = jnp.zeros((B, H, dk, dv), jnp.float32)
    _, o_inter = lax.scan(step, state0, (jnp.swapaxes(qc, 0, 1), jnp.swapaxes(kc, 0, 1), jnp.swapaxes(vc, 0, 1)))
    o = (o_intra.astype(jnp.float32) + jnp.swapaxes(o_inter, 0, 1)).astype(v.dtype)
    o = _rms_norm(o, norm_g).reshape(B, S, H * dv)
    return jax.nn.silu(gate) * o

def _chunk_attention(q, k, v, rel_bias):
    B, S, H, d = q.shape
    nc = S // CHUNK
    pad = CA_LEFT_CHUNKS * CHUNK
    band = pad + CHUNK
    k_pad = jnp.pad(k, ((0, 0), (pad, 0), (0, 0), (0, 0)))
    v_pad = jnp.pad(v, ((0, 0), (pad, 0), (0, 0), (0, 0)))
    qpos = jnp.arange(CHUNK)
    kpos = jnp.arange(band)
    rel = qpos[:, None] + pad - kpos[None, :]
    idx = jnp.clip(rel, -REL_CLIP, REL_CLIP) + REL_CLIP
    bias = rel_bias[:, idx].astype(jnp.float32)
    q = q * (d ** -0.5)

    def one_chunk(i):
        start = i * CHUNK
        q_i = lax.dynamic_slice_in_dim(q, start, CHUNK, axis=1)
        k_i = lax.dynamic_slice_in_dim(k_pad, start, band, axis=1)
        v_i = lax.dynamic_slice_in_dim(v_pad, start, band, axis=1)
        s = jnp.einsum('bqhd,bkhd->bhqk', q_i, k_i).astype(jnp.float32) + bias[None]
        valid = (start - pad + kpos) >= 0
        s = jnp.where(valid[None, None, None, :], s, NEG_INF)
        p = jax.nn.softmax(s, axis=-1).astype(v.dtype)
        return jnp.einsum('bhqk,bkhd->bqhd', p, v_i)

    o = lax.map(one_chunk, jnp.arange(nc))
    return jnp.transpose(o, (1, 0, 2, 3, 4)).reshape(B, S, H * d)

def _diff_attention(q, k, v, lam, lambda_init, norm_g):
    B, S, H2, d = q.shape
    H = H2 // 2
    q = _rotary(q) * (d ** -0.5)
    k = _rotary(k)
    nb = S // Q_BLOCK
    key_chunk = jnp.arange(S) // CHUNK

    def one_block(i):
        start = i * Q_BLOCK
        q_i = lax.dynamic_slice_in_dim(q, start, Q_BLOCK, axis=1)
        s = jnp.einsum('bqgd,bkgd->bgqk', q_i, k).astype(jnp.float32)
        query_chunk = (start + jnp.arange(Q_BLOCK)) // CHUNK
        allowed = key_chunk[None, :] <= query_chunk[:, None]
        s = jnp.where(allowed[None, None], s, NEG_INF)
        p = jax.nn.softmax(s, axis=-1).reshape(B, H, 2, Q_BLOCK, S)
        p = p[:, :, 0] - lam * p[:, :, 1]
        return jnp.einsum('bhqk,bkhe->bqhe', p.astype(v.dtype), v)

    o = lax.map(one_block, jnp.arange(nb))
    o = jnp.transpose(o, (1, 0, 2, 3, 4)).reshape(B, S, H, 2 * d)
    o = _rms_norm(o, norm_g) * (1.0 - lambda_init)
    return o.reshape(B, S, H * 2 * d)

def first_inputs(seed: int = 0) -> dict:
    key = jax.random.key(seed)
    ks = jax.random.split(key, 24)

    def nrm(k, shape, scale):
        return jax.random.normal(k, shape, jnp.float32) * scale

    beta = DEEPNORM_BETA
    col_scale = jnp.concatenate([
        jnp.full((w,), beta if is_v else 1.0, jnp.float32) for w, is_v in zip(IN_WIDTHS, IN_IS_VALUE)])
    x = nrm(ks[0], (BATCH, SEQ, D_MODEL), 1.0)
    w_in = nrm(ks[1], (DEPTH, D_MODEL, IN_TOTAL), D_MODEL ** -0.5) * col_scale
    ret_norm_g = 1.0 + nrm(ks[2], (DEPTH, RET_DV), 0.02)
    ca_rel_bias = nrm(ks[3], (DEPTH, CA_HEADS, 2 * REL_CLIP + 1), 0.1)
    da_lambda_q1 = nrm(ks[4], (DEPTH, DA_DH), 0.1)
    da_lambda_k1 = nrm(ks[5], (DEPTH, DA_DH), 0.1)
    da_lambda_q2 = nrm(ks[6], (DEPTH, DA_DH), 0.1)
    da_lambda_k2 = nrm(ks[7], (DEPTH, DA_DH), 0.1)
    da_norm_g = 1.0 + nrm(ks[8], (DEPTH, 2 * DA_DH), 0.02)
    w_branch_a = nrm(ks[9], (DEPTH, RET_V_W, D_MODEL), RET_V_W ** -0.5 * beta)
    w_branch_b = nrm(ks[10], (DEPTH, CA_W, D_MODEL), CA_W ** -0.5 * beta)
    w_branch_c = nrm(ks[11], (DEPTH, DA_V_W, D_MODEL), DA_V_W ** -0.5 * beta)
    b_merge = nrm(ks[12], (DEPTH, N_BRANCHES * D_MODEL), 0.1)
    w_out = nrm(ks[13], (DEPTH, D_MODEL, D_MODEL), D_MODEL ** -0.5 * beta)
    ln1_g = 1.0 + nrm(ks[14], (DEPTH, D_MODEL), 0.02)
    ln1_b = nrm(ks[15], (DEPTH, D_MODEL), 0.02)
    w_ffn_in = nrm(ks[16], (DEPTH, D_MODEL, 2 * FFN_HIDDEN), D_MODEL ** -0.5 * beta)
    w_ffn_out = nrm(ks[17], (DEPTH, FFN_HIDDEN, D_MODEL), FFN_HIDDEN ** -0.5 * beta)
    ln2_g = 1.0 + nrm(ks[18], (DEPTH, D_MODEL), 0.02)
    ln2_b = nrm(ks[19], (DEPTH, D_MODEL), 0.02)
    return {
        "x": x, "w_in": w_in, "ret_norm_g": ret_norm_g, "ca_rel_bias": ca_rel_bias,
        "da_lambda_q1": da_lambda_q1, "da_lambda_k1": da_lambda_k1,
        "da_lambda_q2": da_lambda_q2, "da_lambda_k2": da_lambda_k2, "da_norm_g": da_norm_g,
        "w_branch_a": w_branch_a, "w_branch_b": w_branch_b, "w_branch_c": w_branch_c,
        "b_merge": b_merge, "w_out": w_out, "ln1_g": ln1_g, "ln1_b": ln1_b,
        "w_ffn_in": w_ffn_in, "w_ffn_out": w_ffn_out, "ln2_g": ln2_g, "ln2_b": ln2_b,
    }

def first_block(x, w_in, ret_norm_g, ca_rel_bias, da_lambda_q1, da_lambda_k1, da_lambda_q2, da_lambda_k2,
              da_norm_g, w_branch_a, w_branch_b, w_branch_c, b_merge, w_out, ln1_g, ln1_b,
              w_ffn_in, w_ffn_out, ln2_g, ln2_b):
    B, S, D = x.shape
    splits = [int(s) for s in np.cumsum(IN_WIDTHS)[:-1]]
    for l in range(DEPTH):
        h = jnp.einsum('bsd,de->bse', x, w_in[l])
        rq, rk, rv, rg, cq, ck, cv, dq, dk, dv, gates = jnp.split(h, splits, axis=-1)

        o_a = _retention(rq.reshape(B, S, RET_HEADS, RET_DK), rk.reshape(B, S, RET_HEADS, RET_DK),
                         rv.reshape(B, S, RET_HEADS, RET_DV), rg, ret_norm_g[l])
        o_b = _chunk_attention(cq.reshape(B, S, CA_HEADS, CA_DH), ck.reshape(B, S, CA_HEADS, CA_DH),
                               cv.reshape(B, S, CA_HEADS, CA_DH), ca_rel_bias[l])
        lambda_init = 0.8 - 0.6 * math.exp(-0.3 * l)
        lam = (jnp.exp(jnp.sum(da_lambda_q1[l].astype(jnp.float32) * da_lambda_k1[l].astype(jnp.float32)))
               - jnp.exp(jnp.sum(da_lambda_q2[l].astype(jnp.float32) * da_lambda_k2[l].astype(jnp.float32)))
               + lambda_init)
        o_c = _diff_attention(dq.reshape(B, S, 2 * DA_HEADS, DA_DH), dk.reshape(B, S, 2 * DA_HEADS, DA_DH),
                              dv.reshape(B, S, DA_HEADS, 2 * DA_DH), lam, lambda_init, da_norm_g[l])

        g = jax.nn.sigmoid(gates + b_merge[l]).reshape(B, S, N_BRANCHES, D)
        merged = (g[:, :, 0] * jnp.einsum('bse,ed->bsd', o_a, w_branch_a[l])
                  + g[:, :, 1] * jnp.einsum('bse,ed->bsd', o_b, w_branch_b[l])
                  + g[:, :, 2] * jnp.einsum('bse,ed->bsd', o_c, w_branch_c[l]))
        mix = jnp.einsum('bsd,de->bse', merged, w_out[l])
        x = _layer_norm(DEEPNORM_ALPHA * x + mix, ln1_g[l], ln1_b[l])

        u = jnp.einsum('bsd,df->bsf', x, w_ffn_in[l])
        u_gate, u_up = jnp.split(u, 2, axis=-1)
        ffn = jnp.einsum('bsf,fd->bsd', jax.nn.silu(u_gate) * u_up, w_ffn_out[l])
        x = _layer_norm(DEEPNORM_ALPHA * x + ffn, ln2_g[l], ln2_b[l])
    return x


PLE_DIM = 256
D_FF = 2752
M_HEADS = 4
M_HEAD_DIM = 256
M_WIDTH = M_HEADS * M_HEAD_DIM
M_CHUNK = 64
CONV_K = 4
A_Q_HEADS = 16
A_KV_HEADS = 4
A_HEAD_DIM = 64
A_GROUP = A_Q_HEADS // A_KV_HEADS
A_WIDTH = A_Q_HEADS * A_HEAD_DIM
A_KV_WIDTH = A_KV_HEADS * A_HEAD_DIM
WINDOW = 128
A_BLOCK = 128
EPS = 1e-6
N_IN = 4 * M_WIDTH + 2 * M_HEADS + A_WIDTH + 2 * A_KV_WIDTH + 2 * D_MODEL


def rmsnorm(x, g):
    xf = x.astype(jnp.float32)
    y = xf * lax.rsqrt(jnp.mean(xf * xf, axis=-1, keepdims=True) + EPS)
    return (y * g.astype(jnp.float32)).astype(x.dtype)

def head_rmsnorm(x, g):
    xf = x.astype(jnp.float32)
    y = xf * lax.rsqrt(jnp.mean(xf * xf, axis=-1, keepdims=True) + EPS)
    return y * g.astype(jnp.float32)

def swiglu(x, w_gate, w_up, w_down):
    return (jax.nn.silu(x @ w_gate) * (x @ w_up)) @ w_down

def causal_dwconv(x, w, b):
    c = x.shape[-1]
    y = lax.conv_general_dilated(x, w[:, None, :].astype(x.dtype), window_strides=(1,),
                                 padding=[(CONV_K - 1, 0)],
                                 dimension_numbers=("NWC", "WIO", "NWC"),
                                 feature_group_count=c)
    return y + b

def mlstm_chunkwise(q, k, v, ig, lf):
    bsz, t, nh, dh = q.shape
    nc = t // M_CHUNK

    def to_chunks(z):
        return z.reshape(bsz, nc, M_CHUNK, nh, dh).transpose(1, 0, 3, 2, 4)

    def g_chunks(z):
        return z.reshape(bsz, nc, M_CHUNK, nh).transpose(1, 0, 3, 2)

    causal = jnp.tril(jnp.ones((M_CHUNK, M_CHUNK), dtype=bool))

    def step(carry, xs):
        c_st, n_st, m_st = carry
        qc, kc, vc, ic, fc = xs
        b = jnp.cumsum(fc, axis=-1)
        dlog = jnp.where(causal, b[..., :, None] - b[..., None, :] + ic[..., None, :], -jnp.inf)
        inter = b + m_st[..., None]
        m_t = jnp.maximum(inter, jnp.max(dlog, axis=-1))
        w_intra = jnp.exp(dlog - m_t[..., None])
        w_inter = jnp.exp(inter - m_t)
        s = jnp.einsum("bhtk,bhsk->bhts", qc, kc) * w_intra
        num = jnp.einsum("bhts,bhsv->bhtv", s, vc) + w_inter[..., None] * jnp.einsum("bhtk,bhvk->bhtv", qc, c_st)
        den = jnp.sum(s, axis=-1) + w_inter * jnp.einsum("bhtk,bhk->bht", qc, n_st)
        h = num / jnp.maximum(jnp.abs(den), jnp.exp(-m_t))[..., None]
        b_last = b[..., -1]
        a = b_last[..., None] - b + ic
        m_new = jnp.maximum(b_last + m_st, jnp.max(a, axis=-1))
        w_state = jnp.exp(a - m_new[..., None])
        decay = jnp.exp(b_last + m_st - m_new)
        c_new = decay[..., None, None] * c_st + jnp.einsum("bhsv,bhsk->bhvk", vc * w_state[..., None], kc)
        n_new = decay[..., None] * n_st + jnp.einsum("bhs,bhsk->bhk", w_state, kc)
        return (c_new, n_new, m_new), h

    init = (jnp.zeros((bsz, nh, dh, dh), jnp.float32),
            jnp.zeros((bsz, nh, dh), jnp.float32),
            jnp.zeros((bsz, nh), jnp.float32))
    xs = (to_chunks(q), to_chunks(k), to_chunks(v), g_chunks(ig), g_chunks(lf))
    _, hs = lax.scan(step, init, xs)
    return hs.transpose(1, 0, 3, 2, 4).reshape(bsz, t, nh, dh)

def swa_gqa_sinks(q, k, v, sinks):
    bsz, t = q.shape[0], q.shape[1]
    nb = t // A_BLOCK
    qb = q.reshape(bsz, nb, A_BLOCK, A_KV_HEADS, A_GROUP, A_HEAD_DIM)

    def windows(z):
        zp = jnp.pad(z, ((0, 0), (A_BLOCK, 0), (0, 0), (0, 0)))
        zb = zp.reshape(bsz, nb + 1, A_BLOCK, A_KV_HEADS, A_HEAD_DIM)
        return jnp.concatenate([zb[:, :-1], zb[:, 1:]], axis=2)

    kw, vw = windows(k), windows(v)
    scores = jnp.einsum("bnqhgd,bnkhd->bnhgqk", qb, kw).astype(jnp.float32) * (A_HEAD_DIM ** -0.5)
    qi = jnp.arange(A_BLOCK)[:, None]
    kj = jnp.arange(2 * A_BLOCK)[None, :]
    rel = A_BLOCK + qi - kj
    band = (rel >= 0) & (rel < WINDOW)
    key_pos = jnp.arange(nb)[:, None, None] * A_BLOCK + kj[None] - A_BLOCK
    valid = band[None] & (key_pos >= 0)
    scores = jnp.where(valid[None, :, None, None], scores, -jnp.inf)
    sink = sinks.astype(jnp.float32).reshape(A_KV_HEADS, A_GROUP)[None, None, :, :, None, None]
    mx = jnp.maximum(jnp.max(scores, axis=-1, keepdims=True), sink)
    pr = jnp.exp(scores - mx)
    den = jnp.sum(pr, axis=-1, keepdims=True) + jnp.exp(sink - mx)
    attn = (pr / den).astype(v.dtype)
    out = jnp.einsum("bnhgqk,bnkhd->bnqhgd", attn, vw)
    return out.reshape(bsz, t, A_WIDTH)

def hybrid_layer(h, p_i, ffn1_norm, ffn1_w_gate, ffn1_w_up, ffn1_w_down, mix_norm, w_in,
                 m_conv_w, m_conv_b, m_igate_b, m_fgate_b, m_out_norm, a_q_norm, a_k_norm,
                 a_sinks, w_branch_m, w_branch_a, w_out, ffn2_norm, ffn2_w_gate, ffn2_w_up,
                 ffn2_w_down, ple_norm, ple_gate_w, ple_proj_w):
    bsz, t, _ = h.shape
    h = h + 0.5 * swiglu(rmsnorm(h, ffn1_norm), ffn1_w_gate, ffn1_w_up, ffn1_w_down)

    u = rmsnorm(h, mix_norm)
    z = u @ w_in
    sizes = [2 * M_WIDTH, M_WIDTH, M_WIDTH, M_HEADS, M_HEADS, A_WIDTH, A_KV_WIDTH, A_KV_WIDTH, D_MODEL, D_MODEL]
    offs = [int(o) for o in np.cumsum(sizes)[:-1]]
    m_qk, m_v, m_o, m_i, m_f, a_q, a_k, a_v, g_m, g_a = jnp.split(z, offs, axis=-1)

    m_qk = jax.nn.silu(causal_dwconv(m_qk, m_conv_w, m_conv_b))
    m_q, m_k = jnp.split(m_qk, 2, axis=-1)
    mq = m_q.astype(jnp.float32).reshape(bsz, t, M_HEADS, M_HEAD_DIM) * (M_HEAD_DIM ** -0.5)
    mk = m_k.astype(jnp.float32).reshape(bsz, t, M_HEADS, M_HEAD_DIM)
    mv = m_v.astype(jnp.float32).reshape(bsz, t, M_HEADS, M_HEAD_DIM)
    ig = m_i.astype(jnp.float32) + m_igate_b.astype(jnp.float32)
    lf = jax.nn.log_sigmoid(m_f.astype(jnp.float32) + m_fgate_b.astype(jnp.float32))
    hm = mlstm_chunkwise(mq, mk, mv, ig, lf)
    hm = head_rmsnorm(hm, m_out_norm.reshape(M_HEADS, M_HEAD_DIM)).reshape(bsz, t, M_WIDTH)
    hm = (jax.nn.sigmoid(m_o.astype(jnp.float32)) * hm).astype(h.dtype)

    aq = head_rmsnorm(a_q.reshape(bsz, t, A_Q_HEADS, A_HEAD_DIM), a_q_norm).astype(h.dtype)
    ak = head_rmsnorm(a_k.reshape(bsz, t, A_KV_HEADS, A_HEAD_DIM), a_k_norm).astype(h.dtype)
    av = a_v.reshape(bsz, t, A_KV_HEADS, A_HEAD_DIM)
    ha = swa_gqa_sinks(aq, ak, av, a_sinks)

    merged = jax.nn.sigmoid(g_m) * (hm @ w_branch_m) + jax.nn.sigmoid(g_a) * (ha @ w_branch_a)
    h = h + merged @ w_out

    h = h + 0.5 * swiglu(rmsnorm(h, ffn2_norm), ffn2_w_gate, ffn2_w_up, ffn2_w_down)

    h = h + jax.nn.sigmoid(rmsnorm(h, ple_norm) @ ple_gate_w) * (p_i @ ple_proj_w)
    return h

def second_inputs(seed: int = 0) -> dict:
    key = jax.random.key(seed)
    ks = jax.random.split(key, 32)

    def w(k, fan_in, fan_out, scale=1.0):
        return jax.random.normal(k, (DEPTH, fan_in, fan_out), jnp.float32) * (scale * fan_in ** -0.5)

    def gain(k, n):
        return 1.0 + 0.05 * jax.random.normal(k, (DEPTH, n), jnp.float32)

    f_bias = jnp.linspace(3.0, 6.0, M_HEADS, dtype=jnp.float32)[None, :] + 0.1 * jax.random.normal(ks[10], (DEPTH, M_HEADS), jnp.float32)
    return {
        "x": jax.random.normal(ks[0], (BATCH, SEQ, D_MODEL), jnp.float32),
        "p": jax.random.normal(ks[1], (DEPTH, BATCH, SEQ, PLE_DIM), jnp.float32),
        "ffn1_norm": gain(ks[2], D_MODEL),
        "ffn1_w_gate": w(ks[3], D_MODEL, D_FF),
        "ffn1_w_up": w(ks[4], D_MODEL, D_FF),
        "ffn1_w_down": w(ks[5], D_FF, D_MODEL, 0.5),
        "mix_norm": gain(ks[6], D_MODEL),
        "w_in": w(ks[7], D_MODEL, N_IN),
        "m_conv_w": jax.random.normal(ks[8], (DEPTH, CONV_K, 2 * M_WIDTH), jnp.float32) * (CONV_K ** -0.5),
        "m_conv_b": 0.02 * jax.random.normal(ks[9], (DEPTH, 2 * M_WIDTH), jnp.float32),
        "m_igate_b": 0.1 * jax.random.normal(ks[11], (DEPTH, M_HEADS), jnp.float32),
        "m_fgate_b": f_bias,
        "m_out_norm": gain(ks[12], M_WIDTH),
        "a_q_norm": gain(ks[13], A_HEAD_DIM),
        "a_k_norm": gain(ks[14], A_HEAD_DIM),
        "a_sinks": 0.5 * jax.random.normal(ks[15], (DEPTH, A_Q_HEADS), jnp.float32),
        "w_branch_m": w(ks[16], M_WIDTH, D_MODEL),
        "w_branch_a": w(ks[17], A_WIDTH, D_MODEL),
        "w_out": w(ks[18], D_MODEL, D_MODEL, 0.5),
        "ffn2_norm": gain(ks[19], D_MODEL),
        "ffn2_w_gate": w(ks[20], D_MODEL, D_FF),
        "ffn2_w_up": w(ks[21], D_MODEL, D_FF),
        "ffn2_w_down": w(ks[22], D_FF, D_MODEL, 0.5),
        "ple_norm": gain(ks[23], D_MODEL),
        "ple_gate_w": w(ks[24], D_MODEL, D_MODEL),
        "ple_proj_w": w(ks[25], PLE_DIM, D_MODEL, 0.5),
    }

def second_block(x, p, ffn1_norm, ffn1_w_gate, ffn1_w_up, ffn1_w_down, mix_norm, w_in,
              m_conv_w, m_conv_b, m_igate_b, m_fgate_b, m_out_norm, a_q_norm, a_k_norm,
              a_sinks, w_branch_m, w_branch_a, w_out, ffn2_norm, ffn2_w_gate, ffn2_w_up,
              ffn2_w_down, ple_norm, ple_gate_w, ple_proj_w):
    h = x
    for i in range(DEPTH):
        h = hybrid_layer(h, p[i], ffn1_norm[i], ffn1_w_gate[i], ffn1_w_up[i], ffn1_w_down[i],
                         mix_norm[i], w_in[i], m_conv_w[i], m_conv_b[i], m_igate_b[i],
                         m_fgate_b[i], m_out_norm[i], a_q_norm[i], a_k_norm[i], a_sinks[i],
                         w_branch_m[i], w_branch_a[i], w_out[i], ffn2_norm[i], ffn2_w_gate[i],
                         ffn2_w_up[i], ffn2_w_down[i], ple_norm[i], ple_gate_w[i], ple_proj_w[i])
    return h


def setup_inputs(seed=0):
    out = dict(first_inputs(seed))
    for name, value in second_inputs(seed + 1).items():
        if name != "x":
            out[name + "_2"] = value
    return out


def reference(
    x, w_in, ret_norm_g, ca_rel_bias, da_lambda_q1, da_lambda_k1, da_lambda_q2, da_lambda_k2,
    da_norm_g, w_branch_a, w_branch_b, w_branch_c, b_merge, w_out, ln1_g, ln1_b, w_ffn_in,
    w_ffn_out, ln2_g, ln2_b, p_2, ffn1_norm_2, ffn1_w_gate_2, ffn1_w_up_2, ffn1_w_down_2,
    mix_norm_2, w_in_2, m_conv_w_2, m_conv_b_2, m_igate_b_2, m_fgate_b_2, m_out_norm_2,
    a_q_norm_2, a_k_norm_2, a_sinks_2, w_branch_m_2, w_branch_a_2, w_out_2, ffn2_norm_2,
    ffn2_w_gate_2, ffn2_w_up_2, ffn2_w_down_2, ple_norm_2, ple_gate_w_2, ple_proj_w_2,
):
    x = first_block(
        x, w_in, ret_norm_g, ca_rel_bias, da_lambda_q1, da_lambda_k1, da_lambda_q2,
        da_lambda_k2, da_norm_g, w_branch_a, w_branch_b, w_branch_c, b_merge, w_out, ln1_g,
        ln1_b, w_ffn_in, w_ffn_out, ln2_g, ln2_b,
    )
    return second_block(
        x, p_2, ffn1_norm_2, ffn1_w_gate_2, ffn1_w_up_2, ffn1_w_down_2, mix_norm_2, w_in_2,
        m_conv_w_2, m_conv_b_2, m_igate_b_2, m_fgate_b_2, m_out_norm_2, a_q_norm_2, a_k_norm_2,
        a_sinks_2, w_branch_m_2, w_branch_a_2, w_out_2, ffn2_norm_2, ffn2_w_gate_2, ffn2_w_up_2,
        ffn2_w_down_2, ple_norm_2, ple_gate_w_2, ple_proj_w_2,
    )


_drawn_inputs = setup_inputs


def setup_inputs(seed=0):
    import zlib

    import numpy as np

    out = dict(_drawn_inputs(seed))
    spreads = {}
    factors = {'ret_norm_g': 8.0,
     'ca_rel_bias': 8.0,
     'da_lambda_q1': 8.0,
     'da_lambda_k1': 2.721,
     'da_lambda_q2': 7.694,
     'da_lambda_k2': 7.15,
     'da_norm_g': 8.0,
     'w_branch_b': 4.731,
     'b_merge': 8.0,
     'ffn1_norm_2': 3.943,
     'mix_norm_2': 3.29,
     'm_conv_b_2': 54.379,
     'm_igate_b_2': 200.0,
     'm_out_norm_2': 5.442,
     'a_q_norm_2': 8.0,
     'a_k_norm_2': 8.0,
     'a_sinks_2': 27.095,
     'ffn2_norm_2': 4.027,
     'ple_norm_2': 36.626}
    for name, (base, spread) in spreads.items():
        noise = np.random.default_rng([zlib.crc32(name.encode()), seed]).standard_normal(out[name].shape)
        drawn = base * np.exp(spread * noise) if base else spread * noise
        out[name] = __import__('jax').numpy.asarray(drawn.astype(out[name].dtype))
    for name, factor in factors.items():
        out[name] = (out[name] * factor).astype(out[name].dtype)
    return out
```

```python
import math
from contextlib import ExitStack

import concourse.bass as bass
import numpy as np
from concourse import mybir

F32 = mybir.dt.float32
F32R = mybir.dt.float32r
I32 = mybir.dt.int32
ALU = mybir.AluOpType
ACT = mybir.ActivationFunctionType
AXX = mybir.AxisListType.X

P = 128
S = 256
R = S // P
D = 1024
KT = D // P
DEPTH = 2
CHUNK = 64
NEG = -1e30

UNIT = 1024
NRAW = 6
NS = 4

LAG = 2

RH, RDK, RDV = 4, 128, 256
CH, CDH = 8, 64
GH = 8
DH, DDH = 4, 64
F1 = 2816
ALPHA = (2.0 * DEPTH) ** 0.25
LN_EPS = 1e-5
ROPE_THETA = 10000.0

F2 = 2752
EPS = 1e-6
MH, MDH = 4, 256
CONV_K = 4
AH, AKV, ADH = 16, 4, 64
WINDOW = 128
PLE = 256


class Step:

    def __init__(self, after_o=None, after_t=None, b=None, c=None, dst=None, first=None, form=None,
                 g=None, gate=None, h=None, half=None, heads=None, i=None, j=None, kept=None,
                 kg=None, kind=None, kt0=None, last=None, last_chunks=None, lhs=None, m=None,
                 made=None, n=None, new=None, nk=None, nth=None, o=None, of=None, off=None,
                 old=None, pair=None, roped=None, rows=None, s=None, scale=None, slot=None,
                 src=None, t=None, table=None, tile=None, u=None, which=None, width=None):
        self.after_o = after_o
        self.after_t = after_t
        self.b = b
        self.c = c
        self.dst = dst
        self.first = first
        self.form = form
        self.g = g
        self.gate = gate
        self.h = h
        self.half = half
        self.heads = heads
        self.i = i
        self.j = j
        self.kept = kept
        self.kg = kg
        self.kind = kind
        self.kt0 = kt0
        self.last = last
        self.last_chunks = last_chunks
        self.lhs = lhs
        self.m = m
        self.made = made
        self.n = n
        self.new = new
        self.nk = nk
        self.nth = nth
        self.o = o
        self.of = of
        self.off = off
        self.old = old
        self.pair = pair
        self.roped = roped
        self.rows = rows
        self.s = s
        self.scale = scale
        self.slot = slot
        self.src = src
        self.t = t
        self.table = table
        self.tile = tile
        self.u = u
        self.which = which
        self.width = width


class Plan:

    def __init__(self):
        self.steps = []
        self.units = []
        self.t = self.s = self.o = self.rows = self.roped = self.probs = self.n_gate = 0
        self.d = [0, 0]
        self.cc = {}

    def add(self, kind, **kw):
        self.steps.append(Step(kind=kind, **kw))
        return self.steps[-1]

    def begin(self):
        kept, self.steps = self.steps, []
        return kept

    def weave(self, before, dense, side):
        n, done, put = sum(st.kind == "unit" for st in dense), 0, 0
        self.steps = before
        for st in dense:
            if st.kind == "unit":
                while any(sd.t == st.after_t for sd in side[put:]):
                    self.steps.append(side[put])
                    put += 1
            self.steps.append(st)
            if st.kind == "unit":
                done += 1
                upto = max(put, len(side) * done // n)
                self.steps += [sd for sd in side[put:upto] ]
                put = upto

    def pause(self, n):
        for _ in range(n):
            self.add("pause")

    def count(self, name):
        self.cc[name] = self.cc.get(name, 0) + 1
        return self.cc[name]

    def next_t(self):
        self.t += 1
        return self.t - 1

    def next_s(self):
        self.s += 1
        return self.s - 1

    def next_o(self):
        self.o += 1
        return self.o - 1

    def unit(self, w, lhs, kt0, nk, n, pair, nth, first, last, after_t, form="rows"):
        u = len(self.units)
        self.units.append((w, kt0, nk, n))
        self.add("unit", u=u, lhs=lhs, kt0=kt0, nk=nk, n=n, pair=pair, nth=nth, first=first, last=last,
                 after_t=after_t, form=form)
        return u

    def next_d(self, pair):
        self.d[pair] += 1
        return self.d[pair] - 1

    def chunk(self, w, lhs, nkt, n, pair, after_t, form="rows"):
        nth = self.next_d(pair)
        per = UNIT // n
        groups = [(k, min(per, nkt - k)) for k in range(0, nkt, per)]
        for i, (k0, nk) in enumerate(groups):
            u = self.unit(w, lhs, k0, nk, n, pair, nth, i == 0, i == len(groups) - 1, after_t, form)
        return Step(u=u, pair=pair, nth=nth)


def plan_block1():
    p = Plan()

    def split_rows(src, dst, nkt, scale=1.0, rows=0, after_o=0):
        for r in range(R):
            for kg in range(0, nkt, 4):
                last = p.next_t()
                p.add("split", t=last, src=src, dst=dst, tile=r, kg=kg, scale=scale, rows=rows, after_o=after_o)
        return last

    def project(w, cols, name, to_pair):
        c = p.chunk((w, cols), "x", KT, cols[0][1] - cols[0][0], to_pair, t_x)
        return c

    t_x = split_rows("x", "x", KT)
    p.add("lambda")

    q = {}
    for i, name in enumerate(("cq", "ck", "cv")):
        c = p.chunk(("w_in", [(3072 + 512 * i, 3584 + 512 * i)]), "x", KT, 512, i % 2, t_x)
        q[name] = p.add("keep", c=c, dst=name, off=0)

    before = p.begin()
    for i, (name, c0, buf, off) in enumerate([
            ("rq", 0, "rq", 0), ("rk", 512, "rk", 0), ("rv0", 1024, "rv", 0), ("rv1", 1536, "rv", 512)]):
        c = p.chunk(("w_in", [(c0, c0 + 512)]), "x", KT, 512, (i + 1) % 2, t_x)
        q[name] = p.add("keep", c=c, dst=buf, off=off)
        if name in ("rq", "rk"):
            q[name + "_rope"] = p.add("rope", of=q[name], src=buf, heads=RH, half=RDK // 2, table="ret", n=p.count("roped"))
    for j in range(2):
        c = p.chunk(("w_in", [(2048 + 512 * j, 2560 + 512 * j)]), "x", KT, 512, (j + 1) % 2, t_x)
        p.add("ret_gate", c=c, j=j)
    for i, name in enumerate(("dq", "dk", "dv")):
        c = p.chunk(("w_in", [(4608 + 512 * i, 5120 + 512 * i)]), "x", KT, 512, (i + 1) % 2, t_x)
        q[name] = p.add("keep", c=c, dst=name, off=0)
        if name in ("dq", "dk"):
            q[name + "_rope"] = p.add("rope", of=q[name], src=name, heads=GH, half=DDH // 2, table="da",
                                      n=p.count("roped"))

    def gate(b, j, pair):
        c0 = 6144 + b * D + 512 * j
        c = p.chunk(("w_in", [(c0, c0 + 512)]), "x", KT, 512, pair, t_x)
        p.add("gate", c=c, b=b, j=j, n=p.count("gates"))

    def merge(b, j, w, lhs, nkt, t_l, pair):
        c = p.chunk((w, [(512 * j, 512 * j + 512)]), lhs, nkt, 512, pair, t_l)
        p.add("merge", c=c, b=b, j=j, n=2 * b + j + 1, rows=p.count("rows") if b == 2 and j == 1 else None)

    for j in range(2):
        gate(0, j, j)
    dense_a = p.begin()

    for src in ("cq", "ck"):
        for r in range(R):
            t_c = p.next_t()
            p.add("turn", t=t_c, src=src, dst="qT" if src == "cq" else "kT", tile=r, roped=None, kept=q[src])
    tt = {}
    for i in range(CH + LAG + 1):
        if i < CH:
            p.add("ca_s", h=i, s=p.next_s(), after_t=t_c)
        if LAG <= i < CH + LAG:
            h = i - LAG
            tt[h] = p.next_t()
            p.add("probs_T", h=h, t=tt[h], of="ca", n=h + 1, slot=h % 4)
        if i > LAG:
            h = i - LAG - 1
            if h % 4 == 0:
                o = p.next_o()
            p.add("ca_pv", h=h, o=o, t=tt[h], kept=q["cv"])
            if h % 4 == 3:
                p.add("ca_out", h=h, o=o)
    p.pause(2)
    t_b = split_rows("cq", "ob", 4, after_o=o + 1)

    for src in ("rq", "rk"):
        for r in range(R):
            t_r = p.next_t()
            p.add("turn", t=t_r, src=src, dst="qT" if src == "rq" else "kT", tile=r, roped=q[src + "_rope"].n, kept=None)
    for i in range(RH + 1):
        if i < RH:
            q["ret_s", i] = p.add("ret_s", h=i, s=p.next_s(), after_t=t_r)
        if i >= 1:
            p.add("ret_pv", h=i - 1, s=q["ret_s", i - 1].s, o=p.next_o(), kept=(q["rv0"], q["rv1"]))
    p.add("ret_fin", rows=p.count("rows"))
    p.pause(5)
    t_a = split_rows("rg", "oa", KT, rows=p.cc["rows"])

    for src in ("dq", "dk"):
        for r in range(R):
            t_d = p.next_t()
            p.add("turn", t=t_d, src=src, dst="qT" if src == "dq" else "kT", tile=r, roped=q[src + "_rope"].n, kept=None)
    for i in range(DH + 2):
        if i < DH:
            for m in range(2):
                p.add("da_s", g=2 * i + m, s=p.next_s(), after_t=t_d)
            p.add("da_mix", h=i, n=p.count("mixed"))
        if 1 <= i <= DH:
            tt[i - 1] = p.next_t()
            p.add("probs_T", h=i - 1, t=tt[i - 1], of="da", n=i, slot=(2 * (i - 1)) % 4)
        if i >= 2:
            p.add("da_pv", h=i - 2, o=p.next_o(), t=tt[i - 2], kept=q["dv"])
    p.add("da_fin", rows=p.count("rows"))
    p.pause(5)
    t_c2 = split_rows("dq", "oc", 4, rows=p.cc["rows"])
    side = p.begin()
    for j in range(2):
        merge(0, j, "w_branch_a", "oa", KT, t_a, j)
    for b in (1, 2):
        for j in range(2):
            gate(b, j, j)
    for j in range(2):
        merge(1, j, "w_branch_b", "ob", 4, t_b, j)
    p.weave(before, dense_a + p.begin(), side)
    for j in range(2):
        merge(2, j, "w_branch_c", "oc", 4, t_c2, j)
    t_m = split_rows("merged", "x", KT, scale=0.5, rows=p.cc["rows"])
    for j in range(2):
        c = p.chunk(("w_out", [(512 * j, 512 * j + 512)]), "x", KT, 512, j, t_m)
        p.add("resid", c=c, n=j, old=ALPHA, new=1.0)
    p.add("norm", which=0, rows=p.count("rows"))
    t_x2 = split_rows("x", "x", KT, rows=p.cc["rows"])
    plan_ffn(p, "w_ffn_in", "w_ffn_in", "w_ffn_out", F1, F1, t_x2, old=ALPHA, new=1.0)
    p.add("norm", which=1, rows=p.count("rows"))
    return p


def plan_ffn(p, w_gate, w_up, w_down, width, up_at, t_x, old=1.0, new=0.5):
    nch = -(-width // 256)
    turned = None
    for c in range(nch + 1):
        if c < nch:
            w = min(256, width - 256 * c)
            if w_gate == w_up:
                sel = (w_gate, [(256 * c, 256 * c + w), (up_at + 256 * c, up_at + 256 * c + w)])
            else:
                sel = ((w_gate, w_up), [(256 * c, 256 * c + w)])
            ch = p.chunk(sel, "x", KT, 2 * w, c % 2, t_x)
            p.add("swiglu", c=ch, i=c, width=w)
            made = ch
        if c >= 1:
            pw = min(256, width - 256 * (c - 1))
            turned = p.next_t()
            p.add("split_act", t=turned, i=c - 1, width=pw, made=before)
        before = made
    kt = -(-width // P)
    nth = [p.next_d(0), p.next_d(1)]
    ends = [0, 0]
    for k0 in range(0, kt, UNIT // 512):
        nk = min(UNIT // 512, kt - k0)
        for j in range(2):
            ends[j] = p.unit((w_down, [(512 * j, 512 * j + 512)]), "act", k0, nk, 512, j, nth[j], k0 == 0,
                             k0 + nk == kt, turned)
    for j in range(2):
        p.add("resid", c=Step(u=ends[j], pair=j, nth=nth[j]), n=j, old=old, new=new)


def plan_block2():
    p = Plan()

    def split_rows(src, dst, nkt, scale=1.0, rows=0, after_o=0):
        for r in range(R):
            for kg in range(0, nkt, 4):
                last = p.next_t()
                p.add("split", t=last, src=src, dst=dst, tile=r, kg=kg, scale=scale, rows=rows, after_o=after_o)
        return last

    def rms(which):
        p.add("rms", which=which, n=p.count("rms"), rows=p.count("rows"))
        return split_rows("merged", "x", KT, rows=p.cc["rows"])

    def ffn(name, which):
        plan_ffn(p, name + "_w_gate", name + "_w_up", name + "_w_down", F2, None, rms(which))

    p.add("p_split")
    ffn("ffn1", 0)
    t_x = rms(1)

    def kept_rows(name, c0, dst, off, pair):
        c = p.chunk(("w_in", [(c0, c0 + 512)]), "x", KT, 512, pair, t_x)
        q[name] = p.add("keep_kv" if name == "akv" else "keep", c=c, dst=dst, off=off)

    def convolved(i, pair):
        c = p.chunk(("w_in", [(256 * i, 256 * i + 256)]), "x", KT, 256, pair, t_x, form="features")
        p.add("conv", c=c, i=i)
        q["conv", i] = c

    q = {}
    c = p.chunk(("w_in", [(4096, 4104)]), "x", KT, 8, 0, t_x)
    p.add("m_log", c=c)
    for i, (name, c0, dst, off) in enumerate([("aq0", 4104, "aqk", 0), ("aq1", 4616, "aqk", 512),
                                              ("akv", 5128, "aqk", 1024)]):
        kept_rows(name, c0, dst, off, (i + 1) % 2)
    p.add("a_norm", kept=(q["aq0"], q["aq1"], q["akv"]))

    before = p.begin()
    for i in range(4):
        for k in range(2):
            convolved(2 * i + k, k)
            if i or k:
                p.add("conv_silu", i=2 * i + k - 1, c=q["conv", 2 * i + k - 1])
        if i < 2:
            kept_rows(f"mv{i}", 2048 + 512 * i, "mv", 512 * i, 0)
        else:
            c = p.chunk(("w_in", [(3072 + 512 * (i - 2), 3584 + 512 * (i - 2))]), "x", KT, 512, 0, t_x)
            p.add("m_gate", c=c, j=i - 2, which="gt_a")
    p.add("conv_silu", i=7, c=q["conv", 7])
    gates2 = []
    for of, which, c0 in (("hm", "gt", 5640), ("ha", "gt_a", 6664)):
        for j in range(2):
            cg = p.chunk(("w_in", [(c0 + 512 * j, c0 + 512 * j + 512)]), "x", KT, 512, j, t_x)
            p.add("gate2", c=cg, of=of, which=which, j=j)
            gates2.append(cg)
    dense_a = p.begin()

    p.pause(6)
    for r in range(R):
        for half in range(3):
            t_a = p.next_t()
            p.add("a_turn", t=t_a, tile=r, half=half)
    tt = {}
    for i in range(AH + LAG + 1):
        if i < AH:
            p.add("aa_s", h=i, s=p.next_s(), after_t=t_a)
        if LAG <= i < AH + LAG:
            h = i - LAG
            tt[h] = p.next_t()
            p.add("probs_T", h=h, t=tt[h], of="aa", n=h + 1, slot=h % 4)
        if i > LAG:
            h = i - LAG - 1
            if h % 4 == 0:
                q["o"] = p.next_o()
            p.add("aa_pv", h=h, o=q["o"], t=tt[h], kept=q["akv"])
            if h % 4 == 3:
                p.add("aa_out", h=h, o=q["o"])
    p.pause(2)
    t_a2 = split_rows("aqk", "ha", KT, after_o=q["o"] + 1)

    for h in range(MH):
        p.add("m_arow", h=h, s=p.next_s())
    p.add("m_floor")
    for i in range(MH + 2):
        if i < MH:
            p.add("m_s", h=i, s=p.next_s())
        if 1 <= i <= MH:
            tt[i - 1] = p.next_t()
            p.add("probs_T", h=i - 1, t=tt[i - 1], of="m", n=MH + AH + i, slot=i - 1)
        if i >= 2:
            p.add("m_pv", h=i - 2, o=p.next_o(), t=tt[i - 2], kept=(q["mv0"], q["mv1"]))
    p.add("m_fin", rows=p.count("rows"))
    p.pause(5)
    t_m = split_rows("mo", "hm", KT, rows=p.cc["rows"])
    side = p.begin()
    for j in range(2):
        cp = p.chunk(("w_branch_a", [(512 * j, 512 * j + 512)]), "ha", KT, 512, j, t_a2)
        p.add("merge2", c=cp, gate=gates2[2 + j], which="gt_a", j=j, first=True)
    p.weave(before, dense_a + p.begin(), side)
    for j in range(2):
        cp = p.chunk(("w_branch_m", [(512 * j, 512 * j + 512)]), "hm", KT, 512, j, t_m)
        p.add("merge2", c=cp, gate=gates2[j], which="gt", j=j, first=False, rows=p.count("rows") if j == 1 else None)
    t_g = split_rows("merged", "x", KT, scale=0.5, rows=p.cc["rows"])
    for j in range(2):
        c = p.chunk(("w_out", [(512 * j, 512 * j + 512)]), "x", KT, 512, j, t_g)
        p.add("resid", c=c, n=j, old=1.0, new=1.0)

    ffn("ffn2", 2)

    t_p = rms(3)
    for j in range(2):
        cg = p.chunk(("ple_gate_w", [(512 * j, 512 * j + 512)]), "x", KT, 512, 0, t_p)
        p.add("gate2", c=cg, which="gt", j=j)
        nth = p.next_d(1)
        u = p.unit(("ple_proj_w", [(512 * j, 512 * j + 512)]), "p", 0, PLE // P, 512, 1, nth, True, True, None)
        p.add("ple", c=Step(u=u, pair=1, nth=nth), gate=cg, which="gt", j=j)
    return p


class Memory:

    def __init__(self, nc, base, end):
        self.nc, self.base, self.end = nc, base, end

    def at(self, name, offset, shape, dt=F32):
        offset = (offset + 63) // 64 * 64
        size = int(np.prod(shape[1:])) * 4
        assert self.base + offset + size <= self.end, (name, self.base + offset + size - self.end)
        return self.nc.alloc_sbuf_tensor_at(name, list(shape), dt, offset=self.base + offset), offset + size


def build(nc, plan1, plan2, a):
    plans = [plan1, plan2]
    with ExitStack() as ctx:
        def sem(name):
            return ctx.enter_context(nc.semaphore(name))

        psum = [ctx.enter_context(nc.psum_tensor(f"bank{i}", [P, 512], F32)) for i in range(8)]
        DB, TB, SB, OB = psum[0:4], psum[4:6], psum[6], psum[7]

        w_loaded = [sem(f"w_loaded{i}") for i in range(NRAW)]
        c_loaded = sem("c_loaded")
        stored = sem("stored")
        unit_done = sem("unit_done")
        hi_done = sem("hi_done")
        lo_done = sem("lo_done")
        d_done = [sem(f"d_done{i}") for i in range(4)]
        t_ready = [sem(f"t_ready{i}") for i in range(2)]
        t_hi = sem("t_hi")
        t_done = [sem(f"t_done{i}") for i in range(2)]
        s_ready = sem("s_ready")
        s_done = sem("s_done")
        o_ready = sem("o_ready")
        o_done = sem("o_done")
        rows = sem("rows")
        roped = sem("roped")
        tanh_done = sem("tanh_done")
        maxed = sem("maxed")
        soft = sem("soft")
        mixed = sem("mixed")
        gates = sem("gates")
        silu = sem("silu")
        lam_dot = sem("lam_dot")
        lam_exp = sem("lam_exp")
        bias_up = sem("bias_up")
        p_ready = sem("p_ready")
        logs = sem("logs")
        spread_out = sem("spread_out")
        conv_tanh = sem("conv_tanh")
        floored = sem("floored")
        rec_done = sem("rec_done")
        squared = sem("squared")
        summed = sem("summed")
        a_normed = sem("a_normed")
        sumsq = sem("sumsq")
        conv_out = sem("conv_out")
        p_emb = sem("p_emb")
        p_gain = [sem(f"p_gain{i}") for i in range(2)]
        p_conv = sem("p_conv")
        p_bias = sem("p_bias")
        p_vec = sem("p_vec")
        p_gate = sem("p_gate")
        p_norm = sem("p_norm")
        dve_chain = sem("dve_chain")
        act_chain = sem("act_chain")
        pool_chain = sem("pool_chain")
        first_cleared, last_cleared = unit_done.num, pool_chain.num

        fence = nc.alloc_sbuf_tensor("fence", [P, 16], F32)
        mem = Memory(nc, (nc.sbuf_base + 63) // 64 * 64, nc.sbuf_usable_end)
        o = 0
        raw, o = mem.at("raw", o, [P, NRAW, UNIT])
        wh, o = mem.at("wh", o, [P, NS, UNIT], F32R)
        wl, o = mem.at("wl", o, [P, NS, UNIT], F32R)
        xh, o = mem.at("xh", o, [P, KT, S], F32R)
        xl, o = mem.at("xl", o, [P, KT, S], F32R)
        x, o = mem.at("x", o, [P, R, D])
        ident, o = mem.at("ident", o, [P, P])
        scr, o = mem.at("scr", o, [P, 256])
        bst, o = mem.at("bst", o, [P, R, 2, 6])
        bmv, o = mem.at("bmv", o, [P, R, 2])
        shared_end = o

        b = {}
        def buf(name, shape, dt=F32, at=None):
            nonlocal o
            if at is None:
                b[name], o = mem.at(name, o, shape, dt)
            else:
                b[name], end = mem.at(name, at, shape, dt)
                return end

        q0 = o
        for n in ("rq", "rk"):
            buf(n, [P, R, 512])
        buf("rv", [P, R, D])
        buf("rg", [P, R, D])
        c0 = o
        for n in ("cq", "ck", "cv"):
            buf(n, [P, R, 512])
        e0 = o
        for n in ("dq", "dk", "dv"):
            buf(n, [P, R, 512])
        buf("ret_o", [P, R, D], at=q0)
        end = buf("oa_h", [P, KT, S], F32R, at=q0)
        buf("oa_l", [P, KT, S], F32R, at=end)
        buf("gt_c", [P, 2, R, 512], at=q0)
        end = buf("ob_h", [P, 4, S], F32R, at=c0 + 4096)
        buf("ob_l", [P, 4, S], F32R, at=end)
        end = buf("oc_h", [P, 4, S], F32R, at=e0 + 4096)
        buf("oc_l", [P, 4, S], F32R, at=end)
        end = buf("act_h", [P, 22, S], F32R, at=q0)
        buf("act_l", [P, 22, S], F32R, at=end)
        buf("qT", [P, 4, S])
        buf("kT", [P, 4, S])
        buf("Pn", [P, 4, 384])
        buf("PT", [P, 2, 384])
        buf("bias", [P, CH, S])
        buf("decay", [P, RH, 384])
        buf("rope", [P, R, 2, 96])
        buf("dmask", [P, S])
        buf("b_merge", [P, 3 * D])
        buf("ln", [P, 2, D])
        buf("vec", [P, 256 + 128 + 256 + 2])
        buf("rs", [P, 4, 256])
        buf("merged", [P, R, D])
        g0 = o
        buf("gt", [P, 2, R, 512])
        end = buf("ffn_s", [P, 2, R, 256], at=g0)
        buf("ffn_a", [P, 2, R, 256], at=end)
        buf("junk", [P, 256])
        o1, o = o, q0
        buf("mT", [P, 16, S])
        buf("mv", [P, R, D])
        buf("mo", [P, R, D])
        buf("aqk", [P, R, 1280])
        buf("av", [P, R, 256])
        end = buf("hm_h", [P, KT, S], F32R, at=q0)
        buf("hm_l", [P, KT, S], F32R, at=end)
        end = buf("ha_h", [P, KT, S], F32R, at=o)
        buf("ha_l", [P, KT, S], F32R, at=end)
        buf("akd", [P, R, AKV, 2, ADH])
        buf("sq", [P, 1280], at=o)
        buf("aqT", [P, 8, S])
        buf("akT", [P, AKV, S])
        m_o0 = o
        buf("m_o", [P, R, D])
        end = buf("ib", [P, R, MH, P], at=m_o0)
        buf("lfb", [P, R, MH, P], at=end)
        buf("Pn2", [P, 4, 384])
        buf("PT2", [P, 2, 384])
        g0 = o
        buf("gt2", [P, 2, R, 512])
        buf("gt_a", [P, 2, R, 512])
        end = buf("ffn_s2", [P, 2, R, 256], at=g0)
        buf("ffn_a2", [P, 2, R, 256], at=end)
        buf("merged2", [P, R, D])
        buf("gain", [P, 2, D])
        buf("vec2", [P, 64 + 64 + 16 + 8])
        buf("convw", [P, 16, CONV_K + 1])
        buf("p_raw", [P, 2, S])
        buf("p_h", [P, 2, S], F32R)
        buf("p_l", [P, 2, S], F32R)
        buf("masks", [P, 3, S])
        buf("junk2", [P, 256])
        buf("sc2", [P, 384])
        b["act2_h"], b["act2_l"] = b["act_h"], b["act_l"]
        sc2 = b["sc2"]
        ifv, absf, lnf, lf = sc2[:, 0:16], sc2[:, 16:24], sc2[:, 24:32], sc2[:, 32:40]
        mx2, nmx2, sm2 = sc2[:, 40:72], sc2[:, 72:104], sc2[:, 104:136]
        nb, fl, den, rec2, ss2 = sc2[:, 136:144], sc2[:, 144:152], sc2[:, 152:160], sc2[:, 160:168], sc2[:, 168:176]
        es, ssq, rq2 = sc2[:, 176:184], sc2[:, 184:224], sc2[:, 224:264]
        ss, nmx, mx, sm = scr[:, 0:16], scr[:, 16:32], scr[:, 32:48], scr[:, 48:64]
        rc, c1, v, y, tn = scr[:, 64:80], scr[:, 80:84], scr[:, 84:124], scr[:, 124:164], scr[:, 164:204]
        lamv = scr[:, 204:212]

        split_of = {"x": (xh, xl), "oa": (b["oa_h"], b["oa_l"]), "ob": (b["ob_h"], b["ob_l"]),
                    "oc": (b["oc_h"], b["oc_l"]), "act": (b["act_h"], b["act_l"]), "hm": (b["hm_h"], b["hm_l"]),
                    "ha": (b["ha_h"], b["ha_l"]), "p": (b["p_h"], b["p_l"])}
        b["x"] = x
        LAMBDA_DOT, G_RET, G_DA, LAM_INIT = 384, 0, 256, 640

        def slot_counts(u_total):
            return [-(-(u_total - s) // NRAW) for s in range(NRAW)]

        cnt = [slot_counts(len(p.units)) for p in plans]
        slot_base = [[0] * NRAW, [DEPTH * c for c in cnt[0]]]
        unit_base = [0, DEPTH * len(plan1.units)]

        with nc.Block() as block:
            @block.sync
            def _(sp):
                sp.dma_start(x[:, :, :], a["x"].rearrange("(r p) d -> p r d", p=P)).then_inc(c_loaded, 16)
                for u in range(NRAW):
                    sp.dma_start(raw[:, u, :], a["weights"][u]).then_inc(w_loaded[u], 16)

            @block.scalar
            def _(act):
                act.dma_start(ident[:, :], a["ident"]).then_inc(c_loaded, 16)
                act.dma_start(b["decay"][:, :, :], a["decay"]).then_inc(c_loaded, 16)
                act.dma_start(b["rope"][:, :, :, :], a["rope"]).then_inc(c_loaded, 16)
                act.dma_start(b["dmask"][:, :], a["dmask"]).then_inc(c_loaded, 16)
                act.wait_ge(c_loaded, 80)

        for block_no, plan in enumerate(plans):
            if not plan.steps:
                continue
            if block_no == 1:
                for name in ("Pn", "PT", "gt", "ffn_s", "ffn_a", "merged"):
                    b[name] = b[name + "2"]
            steps, U = plan.steps, len(plan.units)
            with nc.Fori(0, DEPTH) as layer:
                with nc.Block() as block:
                    @block.sync
                    def _(sp):
                        for u in range(NRAW, U + NRAW):
                            w = u - NRAW if u < U else NRAW * ((U - 1 - (u - U)) // NRAW) + (u - U)
                            slot = u % NRAW if u < U else u - U
                            sp.wait_ge(lo_done, w + 1)
                            at = unit_base[block_no] + layer * U + u
                            sp.dma_start(raw[:, slot, :],
                                         a["weights"][bass.ds(at, 1)].rearrange("o p n -> p (o n)"))\
                              .then_inc(w_loaded[slot], 16)

                    @block.gpsimd
                    def _(pool):
                        chain = [0]

                        def link(ins):
                            chain[0] += 1
                            ins.then_inc(pool_chain, 1)
                            pool.wait_ge(pool_chain, chain[0])

                        if block_no == 0:
                            pool.wait_ge(p_bias, 16)
                            link(pool.tensor_scalar(b["bias"][:, :, :], b["bias"][:, :, :], CDH ** 0.5, None, ALU.mult))
                            pool.memset(b["bias"][0:CHUNK, :, 192:256], NEG * CDH ** 0.5).then_inc(bias_up, 1)
                        for st in steps:
                            if st.kind == "rope":
                                c = st.of.c
                                if st.n > 1:
                                    pool.wait_ge(roped, st.n - 1)
                                for r in range(R):
                                    pool.wait_ge(d_done[2 * c.pair + r], c.nth + 1)
                                    t = b[st.src][:, r, :].rearrange("p (h a k) -> p h a k", h=st.heads, a=2)
                                    k = st.half
                                    lo = 0 if st.table == "ret" else RDK // 2
                                    cs = [b["rope"][:, r, i, lo:lo + k].unsqueeze(1).broadcast_to([P, st.heads, k])
                                          for i in range(2)]
                                    sc = [b["rs"][:, i, :].rearrange("p (h k) -> p h k", h=st.heads) for i in range(4)]
                                    x1, x2 = t[:, :, 0, :], t[:, :, 1, :]
                                    pool.tensor_tensor(sc[0], x1, cs[0], ALU.mult)
                                    pool.tensor_tensor(sc[1], x2, cs[1], ALU.mult)
                                    pool.tensor_tensor(sc[2], x2, cs[0], ALU.mult)
                                    link(pool.tensor_tensor(sc[3], x1, cs[1], ALU.mult))
                                    link(pool.tensor_tensor(x1, sc[0], sc[1], ALU.subtract))
                                    last = pool.tensor_tensor(x2, sc[2], sc[3], ALU.add)
                                    if r == R - 1:
                                        last.then_inc(roped, 1)
                                    else:
                                        link(last)
                            elif st.kind == "m_log":
                                pool.wait_ge(logs, 4)
                                iv, lv = ifv.rearrange("p (r g) -> p r g", r=R), lf.rearrange("p (r h) -> p r h", r=R)
                                pool.tensor_copy(b["ib"][:, :, :, :], iv[:, :, 0:MH].unsqueeze(3).broadcast_to([P, R, MH, P]))\
                                    .then_inc(spread_out, 1)
                                pool.tensor_copy(b["lfb"][:, :, :, :], lv.unsqueeze(3).broadcast_to([P, R, MH, P]))\
                                    .then_inc(spread_out, 1)
                            elif st.kind == "a_norm":
                                for kept in st.kept:
                                    for r in range(R):
                                        pool.wait_ge(d_done[2 * kept.c.pair + r], kept.c.nth + 1)
                                for r in range(R):
                                    if r:
                                        pool.wait_ge(summed, r)
                                    pool.tensor_tensor(b["sq"][:, :], b["aqk"][:, r, :], b["aqk"][:, r, :], ALU.mult)\
                                        .then_inc(squared, 1)
                                pool.wait_ge(summed, R + 1)
                                pool.wait_ge(p_vec, 16)
                                for r in range(R):
                                    t = b["aqk"][:, r, :].rearrange("p (h k) -> p h k", h=AH + AKV)
                                    link(pool.tensor_tensor(t, t, rq2[:, 20 * r:20 * r + 20].unsqueeze(2)
                                                            .broadcast_to([P, AH + AKV, ADH]), ALU.mult))
                                    pool.tensor_tensor(t[:, 0:AH, :], t[:, 0:AH, :], b["vec2"][:, 0:ADH].unsqueeze(1)
                                                       .broadcast_to([P, AH, ADH]), ALU.mult)
                                    for i in range(2):
                                        last = pool.tensor_tensor(b["akd"][:, r, :, i, :], t[:, AH:, :], b["vec2"][:, ADH:2 * ADH]
                                                                  .unsqueeze(1).broadcast_to([P, AKV, ADH]), ALU.mult)
                                    last.then_inc(a_normed, 1)

                    @block.scalar
                    def _(act):
                        chain = [0]

                        def link(ins):
                            chain[0] += 1
                            ins.then_inc(act_chain, 1)
                            act.wait_ge(act_chain, chain[0])

                        def split_high(u):
                            used = plan.units[u][2] * plan.units[u][3]
                            s = u % NRAW
                            act.wait_ge(w_loaded[s], 16 * (slot_base[block_no][s] + u // NRAW + 1) + layer * (16 * cnt[block_no][s]))
                            act.activation(wh[:, u % NS, 0:used], raw[:, s, 0:used], ACT.Copy).then_inc(hi_done, 1)

                        def row(name):
                            return a[name][bass.ds(layer, 1)].rearrange("o p n -> p (o n)")

                        def param_loads_1():
                            act.dma_start(b["vec"][:, :], row("vec")).then_inc(p_vec, 16)
                            act.dma_start(b["bias"][:, :, :].rearrange("p h n -> p (h n)"), row("bias")).then_inc(p_bias, 16)
                            act.dma_start(b["b_merge"][:, :], row("b_merge")).then_inc(p_gate, 16)
                            act.dma_start(b["ln"][:, :, :].rearrange("p h n -> p (h n)"), row("ln1")).then_inc(p_norm, 16)

                        if block_no == 1:
                            act.dma_start(b["gain"][:, 0, :], row("gain_ffn1")).then_inc(p_gain[0], 16)
                            act.dma_start(b["gain"][:, 1, :], row("gain_mix")).then_inc(p_gain[1], 16)
                            act.dma_start(b["vec2"][:, :], row("vec2")).then_inc(p_vec, 16)
                            act.dma_start(b["convw"][:, :, :].rearrange("p c k -> p (c k)"), row("convw")).then_inc(p_conv, 16)
                            act.dma_start(b["p_raw"][:, :, :].rearrange("p c k -> p (c k)"), row("p")).then_inc(p_emb, 16)
                            act.dma_start(b["masks"][:, :, :], a["masks"]).then_inc(p_bias, 16)
                        else:
                            param_loads_1()
                        for u in range(NS):
                            split_high(u)
                        for st in steps:
                            k = st.kind
                            if k == "unit":
                                if st.u + NS < U:
                                    act.wait_ge(unit_done, st.u + 1)
                                    split_high(st.u + NS)
                            elif k == "split":
                                act.wait_ge(t_ready[st.t % 2], st.t // 2 + 1)
                                act.activation(split_of[st.dst][0][:, st.kg:st.kg + 4, st.tile * P:st.tile * P + P],
                                               TB[st.t % 2][:, :].rearrange("p (k n) -> p k n", k=4), ACT.Copy,
                                               scale=st.scale).then_inc(t_hi, 1)
                            elif k == "split_act":
                                act.wait_ge(t_ready[st.t % 2], st.t // 2 + 1)
                                act.activation(b["act_h"][:, 2 * st.i:2 * st.i + 2, :],
                                               TB[st.t % 2][:, :].rearrange("p (k n) -> p k n", k=2), ACT.Copy)\
                                   .then_inc(t_hi, 1)
                            elif k == "keep":
                                act.wait_ge(unit_done, st.c.u + 1)
                                for r in range(R):
                                    act.activation(b[st.dst][:, r, st.off:st.off + 512], DB[2 * st.c.pair + r][:, :],
                                                   ACT.Copy).then_inc(d_done[2 * st.c.pair + r], 1)
                            elif k == "turn":
                                act.wait_ge(t_ready[st.t % 2], st.t // 2 + 1)
                                act.activation(b[st.dst][:, :, st.tile * P:st.tile * P + P],
                                               TB[st.t % 2][:, :].rearrange("p (k n) -> p k n", k=4), ACT.Copy)\
                                   .then_inc(t_done[st.t % 2], 1)
                            elif k == "ret_gate":
                                act.wait_ge(unit_done, st.c.u + 1)
                                for r in range(R):
                                    act.activation(b["gt"][:, st.j, r, :], DB[2 * st.c.pair + r][:, :], ACT.Tanh,
                                                   scale=0.5).then_inc(tanh_done, 1)
                            elif k == "ret_pv":
                                act.wait_ge(o_ready, st.o + 1)
                                for r in range(R):
                                    link(act.activation(b["junk"][:, :], OB[:, r * RDV:(r + 1) * RDV], ACT.Square,
                                                        accum_out=ss[:, 2 * st.h + r:2 * st.h + r + 1]))
                                act.activation(b["ret_o"][:, :, st.h * RDV:(st.h + 1) * RDV],
                                               OB[:, :].rearrange("p (r n) -> p r n", r=R), ACT.Copy).then_inc(o_done, 1)
                            elif k == "da_pv":
                                act.wait_ge(o_ready, st.o + 1)
                                for r in range(R):
                                    link(act.activation(b["junk"][:, 0:P], OB[:, r * P:(r + 1) * P], ACT.Square,
                                                        accum_out=ss[:, 2 * st.h + r:2 * st.h + r + 1]))
                                act.activation(b["dq"][:, :, st.h * P:(st.h + 1) * P],
                                               OB[:, 0:2 * P].rearrange("p (r n) -> p r n", r=R), ACT.Copy).then_inc(o_done, 1)
                            elif k in ("ca_s", "da_s"):
                                n = st.h if k == "ca_s" else st.g
                                act.wait_ge(maxed, n + 1 + (CH if k == "da_s" else 0))
                                for r in (1, 0):
                                    part = b["Pn"][:, n % 4, 0:256] if r else b["Pn"][:, n % 4, 256:384]
                                    at = r * CH + n if k == "ca_s" else 2 * n + r
                                    last = act.activation(part, part, ACT.Exp, bias=nmx[:, 2 * (n % 8) + r:2 * (n % 8) + r + 1],
                                                          accum_out=sm[:, at:at + 1])
                                last.then_inc(soft, 1)
                            elif k == "probs_T":
                                act.wait_ge(t_ready[st.t % 2], st.t // 2 + 1)
                                act.activation(b["PT"][:, st.h % 2, :], TB[st.t % 2][:, 0:384], ACT.Copy)\
                                   .then_inc(t_done[st.t % 2], 1)
                            elif k == "norm" and st.which == 0:
                                act.wait_ge(rows, st.rows)
                                act.dma_start(b["ln"][:, :, :].rearrange("p h n -> p (h n)"), row("ln2")).then_inc(p_norm, 16)
                            elif k == "lambda":
                                act.wait_ge(lam_dot, 1)
                                act.activation(lamv[:, 2:4], lamv[:, 0:2], ACT.Exp).then_inc(lam_exp, 1)
                            elif k == "gate":
                                for r in range(R):
                                    act.wait_ge(d_done[2 * st.c.pair + r], st.c.nth + 1)
                                g = b["gt_c" if st.b == 2 else "gt"][:, st.j, :, :]
                                act.activation(g, g, ACT.Tanh, scale=0.5).then_inc(gates, 1)
                            elif k == "rms":
                                if st.which:
                                    for bank in range(4):
                                        act.wait_ge(d_done[bank], st.last_chunks[bank // 2] + 1)
                                for r in range(R):
                                    act.activation(b["merged"][:, r, :], x[:, r, :], ACT.Square, accum_out=ss2[:, r:r + 1])\
                                       .then_inc(sumsq, 1)
                                if st.which < 3:
                                    act.wait_ge(rows, st.rows)
                                    if st.which == 0:
                                        act.dma_start(b["gain"][:, 0, :], row("gain_m")).then_inc(p_gain[0], 16)
                                    elif st.which == 1:
                                        act.dma_start(b["gain"][:, 1, :], row("gain_ple")).then_inc(p_gain[1], 16)
                            elif k == "p_split":
                                act.wait_ge(p_emb, 16)
                                act.activation(b["p_h"][:, :, :], b["p_raw"][:, :, :], ACT.Copy).then_inc(p_ready, 1)
                            elif k == "m_log":
                                act.wait_ge(logs, 1)
                                act.activation(lnf, absf, ACT.Exp, scale=-1.0).then_inc(logs, 1)
                                act.wait_ge(logs, 2)
                                act.activation(lnf, lnf, ACT.Ln, bias=1.0).then_inc(logs, 1)
                            elif k == "conv_silu":
                                for ct in range(2):
                                    act.wait_ge(d_done[2 * st.c.pair + ct], st.c.nth + 1)
                                act.activation(b["gt"][:, st.i % 2, :, 0:256], b["mT"][:, 2 * st.i:2 * st.i + 2, :], ACT.Tanh,
                                               scale=0.5).then_inc(conv_tanh, 1)
                            elif k == "keep_kv":
                                act.wait_ge(unit_done, st.c.u + 1)
                                for r in range(R):
                                    bank = DB[2 * st.c.pair + r]
                                    link(act.activation(b["aqk"][:, r, 1024:1280], bank[:, 0:256], ACT.Copy))
                                    act.activation(b["av"][:, r, :], bank[:, 256:512], ACT.Copy)\
                                       .then_inc(d_done[2 * st.c.pair + r], 1)
                            elif k == "m_gate" or k == "gate2":
                                act.wait_ge(unit_done, st.c.u + 1)
                                if st.of == "hm":
                                    act.wait_ge(conv_out, 8)
                                for r in range(R):
                                    act.activation(b[st.which][:, st.j, r, :], DB[2 * st.c.pair + r][:, :], ACT.Tanh,
                                                   scale=0.5).then_inc(d_done[2 * st.c.pair + r], 1)
                            elif k == "m_arow":
                                act.wait_ge(maxed, AH + st.h + 1)
                                for r in (1, 0):
                                    part = b["Pn"][:, st.h, 0:256] if r else b["Pn"][:, st.h, 256:384]
                                    last = act.activation(part, part, ACT.Exp, bias=nmx2[:, 4 * r + st.h:4 * r + st.h + 1])
                                last.then_inc(soft, 1)
                            elif k == "m_floor":
                                act.wait_ge(floored, 1)
                                act.activation(fl, fl, ACT.Exp).then_inc(floored, 1)
                            elif k == "m_pv":
                                act.wait_ge(o_ready, st.o + 1)
                                act.wait_ge(rec_done, st.h + 1)
                                for r in range(R):
                                    scale = rec2[:, 4 * r + st.h:4 * r + st.h + 1]
                                    link(act.activation(b["junk2"][:, :], OB[:, r * MDH:(r + 1) * MDH], ACT.Square, scale=scale,
                                                        accum_out=ss2[:, 2 * st.h + r:2 * st.h + r + 1]))
                                for r in range(R):
                                    scale = rec2[:, 4 * r + st.h:4 * r + st.h + 1]
                                    last = act.activation(b["m_o"][:, r, st.h * MDH:(st.h + 1) * MDH],
                                                          OB[:, r * MDH:(r + 1) * MDH], ACT.Identity, scale=scale)
                                last.then_inc(o_done, 1)
                            elif k == "m_fin":
                                act.wait_ge(rows, st.rows)
                                act.dma_start(b["gain"][:, 0, :], row("gain_ffn2")).then_inc(p_gain[0], 16)
                            elif k == "a_turn":
                                act.wait_ge(t_ready[st.t % 2], st.t // 2 + 1)
                                dst = b["akT"][:, :, :] if st.half == 2 else b["aqT"][:, 4 * st.half:4 * st.half + 4, :]
                                act.activation(dst[:, :, st.tile * P:st.tile * P + P],
                                               TB[st.t % 2][:, :].rearrange("p (k n) -> p k n", k=4), ACT.Copy)\
                                   .then_inc(t_done[st.t % 2], 1)
                            elif k == "aa_s":
                                act.wait_ge(maxed, st.h + 1)
                                for r in (1, 0):
                                    part = b["Pn"][:, st.h % 4, 0:256] if r else b["Pn"][:, st.h % 4, 256:384]
                                    at = 16 * r + st.h
                                    last = act.activation(part, part, ACT.Exp, bias=nmx2[:, at:at + 1],
                                                          accum_out=sm2[:, at:at + 1])
                                if st.h % 4 == 3:
                                    last = act.activation(es, es, ACT.Exp)
                                last.then_inc(soft, 1)
                            elif k == "swiglu":
                                act.wait_ge(unit_done, st.c.u + 1)
                                for r in range(R):
                                    act.activation(b["ffn_s"][:, st.i % 2, r, 0:st.width], DB[2 * st.c.pair + r][:, 0:st.width],
                                                   ACT.Silu).then_inc(silu, 1)

                    @block.vector
                    def _(dve):
                        chain = [0]

                        def link(ins):
                            chain[0] += 1
                            ins.then_inc(dve_chain, 1)
                            dve.wait_ge(dve_chain, chain[0])

                        def split_low(u):
                            used = plan.units[u][2] * plan.units[u][3]
                            dve.wait_ge(hi_done, u + 1)
                            dve.tensor_tensor(wl[:, u % NS, 0:used], raw[:, u % NRAW, 0:used],
                                              wh[:, u % NS, 0:used].bitcast(F32), ALU.subtract).then_inc(lo_done, 1)

                        def rsqrt(n, x_in, scale, eps):
                            vv, yy, tt = v[:, 0:n], y[:, 0:n], tn[:, 0:n]
                            link(dve.tensor_scalar(vv, x_in, scale, eps, ALU.mult, ALU.add))
                            link(dve.tensor_scalar(yy.bitcast(I32), vv.bitcast(I32), 1, None, ALU.arith_shift_right))
                            link(dve.tensor_scalar(yy.bitcast(I32), yy.bitcast(I32), -1.0, float(0x5f3759df),
                                                   ALU.mult, ALU.add))
                            for _ in range(4):
                                link(dve.tensor_tensor(tt, yy, yy, ALU.mult))
                                link(dve.tensor_tensor(tt, tt, vv, ALU.mult))
                                link(dve.tensor_scalar(tt, tt, -0.5, 1.5, ALU.mult, ALU.add))
                                link(dve.tensor_tensor(yy, yy, tt, ALU.mult))
                            return yy

                        for u in range(NS):
                            split_low(u)
                        for st in steps:
                            k = st.kind
                            if k == "unit":
                                if st.u + NS < U:
                                    split_low(st.u + NS)
                            elif k in ("split", "split_act"):
                                dve.wait_ge(t_hi, st.n)
                                bank = TB[st.t % 2][:, :].rearrange("p (k n) -> p k n", k=4 if k == "split" else 2)
                                if k == "split":
                                    h, lo = [w[:, st.kg:st.kg + 4, st.tile * P:st.tile * P + P] for w in split_of[st.dst]]
                                else:
                                    h, lo = [w[:, 2 * st.i:2 * st.i + 2, :] for w in split_of["act"]]
                                if k == "split" and st.scale != 1.0:
                                    ins = dve.scalar_tensor_tensor(lo, bank, st.scale, h.bitcast(F32), ALU.mult, ALU.subtract)
                                else:
                                    ins = dve.tensor_tensor(lo, bank, h.bitcast(F32), ALU.subtract)
                                ins.then_inc(t_done[st.t % 2], 1)
                            elif k == "lambda":
                                dve.wait_ge(p_vec, 16)
                                for i in range(2):
                                    at = LAMBDA_DOT + 128 * i
                                    last = dve.tensor_tensor_reduce(b["junk"][:, 64 * i:64 * i + 64], b["vec"][:, at:at + 64],
                                                                    b["vec"][:, at + 64:at + 128], 1.0, 0.0, ALU.mult,
                                                                    ALU.add, lamv[:, i:i + 1])
                                last.then_inc(lam_dot, 1)
                                dve.wait_ge(lam_exp, 1)
                                link(dve.scalar_tensor_tensor(lamv[:, 4:5], lamv[:, 2:3], lamv[:, 3:4],
                                                              b["vec"][:, LAM_INIT:LAM_INIT + 1], ALU.subtract, ALU.add))
                            elif k == "ret_gate":
                                for r in range(R):
                                    bank = 2 * st.c.pair + r
                                    dve.wait_ge(tanh_done, 2 * st.j + r + 1)
                                    dst = b["rg"][:, r, st.j * 512:(st.j + 1) * 512]
                                    dve.scalar_tensor_tensor(dst, b["gt"][:, st.j, r, :], 1.0, DB[bank][:, :], ALU.add,
                                                             ALU.mult).then_inc(d_done[bank], 1)
                                    dve.wait_ge(d_done[bank], st.c.nth + 1)
                                    d3 = dst.rearrange("p (h n) -> p h n", h=2)
                                    link(dve.tensor_tensor(d3, d3, b["vec"][:, G_RET:G_RET + RDV].unsqueeze(1)
                                                           .broadcast_to([P, 2, RDV]), ALU.mult))
                            elif k == "ret_s":
                                dve.wait_ge(s_ready, st.s + 1)
                                dve.tensor_tensor(b["Pn"][:, st.h % 4, :], SB[:, 0:384], b["decay"][:, st.h, :], ALU.mult)\
                                   .then_inc(s_done, 1)
                            elif k == "ret_fin":
                                dve.wait_ge(o_done, st.o + 1)
                                rs = rsqrt(8, ss[:, 0:8], 1.0 / RDV, LN_EPS)
                                link(dve.tensor_scalar(rs, rs, 0.5, None, ALU.mult))
                                for h in range(RH):
                                    for r in range(R):
                                        part = b["rg"][:, r, h * RDV:(h + 1) * RDV]
                                        last = dve.scalar_tensor_tensor(part, b["ret_o"][:, r, h * RDV:(h + 1) * RDV],
                                                                        rs[:, 2 * h + r:2 * h + r + 1], part,
                                                                        ALU.mult, ALU.mult)
                                last.then_inc(rows, 1)
                            elif k in ("ca_s", "da_s"):
                                n = st.h if k == "ca_s" else st.g
                                dve.wait_ge(s_ready, st.s + 1)
                                if k == "ca_s":
                                    dve.wait_ge(bias_up, 1)
                                add = b["bias"][:, n, :] if k == "ca_s" else b["dmask"][:, :]
                                dve.tensor_tensor_reduce(b["Pn"][:, n % 4, 0:256], SB[:, 0:256], add, 0.125, -3e38,
                                                         ALU.add, ALU.max, mx[:, 2 * (n % 8) + 1:2 * (n % 8) + 2])
                                dve.tensor_tensor_reduce(b["Pn"][:, n % 4, 256:384], SB[:, 256:384], add[:, 128:256],
                                                         0.125, -3e38, ALU.add, ALU.max, mx[:, 2 * (n % 8):2 * (n % 8) + 1])\
                                   .then_inc(s_done, 1)
                                dve.wait_ge(s_done, st.s + 1)
                                dve.tensor_scalar(nmx[:, 2 * (n % 8):2 * (n % 8) + 2], mx[:, 2 * (n % 8):2 * (n % 8) + 2],
                                                  -1.0, None, ALU.mult).then_inc(maxed, 1)
                            elif k == "ca_out":
                                dve.wait_ge(o_ready, st.o + 1)
                                g = st.h // 4
                                for r in range(R):
                                    link(dve.reciprocal(rc[:, 4 * r:4 * r + 4], sm[:, r * CH + 4 * g:r * CH + 4 * g + 4]))
                                for r in range(R):
                                    dst = b["cq"][:, r, 256 * g:256 * g + 256].rearrange("p (h n) -> p h n", h=4)
                                    last = dve.tensor_tensor(dst, OB[:, 256 * r:256 * r + 256].rearrange("p (h n) -> p h n", h=4),
                                                             rc[:, 4 * r:4 * r + 4].unsqueeze(2).broadcast_to([P, 4, CDH]),
                                                             ALU.mult)
                                last.then_inc(o_done, 1)
                            elif k == "da_mix":
                                dve.wait_ge(soft, CH + 2 * st.h + 2)
                                link(dve.reciprocal(rc[:, 0:4], sm[:, 4 * st.h:4 * st.h + 4]))
                                link(dve.tensor_scalar(c1[:, 0:2], rc[:, 2:4], lamv[:, 4:5], None, ALU.mult))
                                s0, s1 = (2 * st.h) % 4, (2 * st.h + 1) % 4
                                for r in range(R):
                                    cols = slice(0, 256) if r else slice(256, 384)
                                    link(dve.tensor_scalar(b["Pn"][:, s1, cols], b["Pn"][:, s1, cols], c1[:, r:r + 1], None,
                                                           ALU.mult))
                                    last = dve.scalar_tensor_tensor(b["Pn"][:, s0, cols], b["Pn"][:, s0, cols],
                                                                    rc[:, r:r + 1], b["Pn"][:, s1, cols], ALU.mult,
                                                                    ALU.subtract)
                                last.then_inc(mixed, 1)
                            elif k == "da_fin":
                                dve.wait_ge(o_done, st.o + 1)
                                rs = rsqrt(8, ss[:, 0:8], 1.0 / P, LN_EPS)
                                link(dve.tensor_scalar(rs, rs, b["vec"][:, LAM_INIT + 1:LAM_INIT + 2], None, ALU.mult))
                                for h in range(DH):
                                    for r in range(R):
                                        part = b["dq"][:, r, h * P:(h + 1) * P]
                                        last = dve.scalar_tensor_tensor(part, part, rs[:, 2 * h + r:2 * h + r + 1],
                                                                        b["vec"][:, G_DA:G_DA + P], ALU.mult, ALU.mult)
                                last.then_inc(rows, 1)
                            elif k == "gate":
                                dve.wait_ge(unit_done, st.c.u + 1)
                                dve.wait_ge(p_gate, 16)
                                at = st.b * D + st.j * 512
                                for r in range(R):
                                    bank = 2 * st.c.pair + r
                                    dve.tensor_tensor(b["gt_c" if st.b == 2 else "gt"][:, st.j, r, :], DB[bank][:, :], b["b_merge"][:, at:at + 512],
                                                      ALU.add).then_inc(d_done[bank], 1)
                            elif k == "merge":
                                dve.wait_ge(unit_done, st.c.u + 1)
                                dve.wait_ge(gates, st.n)
                                for r in range(R):
                                    bank = 2 * st.c.pair + r
                                    g = b["gt_c" if st.b == 2 else "gt"][:, st.j, r, :]
                                    m = b["merged"][:, r, st.j * 512:(st.j + 1) * 512]
                                    dve.scalar_tensor_tensor(m if st.b == 0 else g, g, 1.0, DB[bank][:, :], ALU.add,
                                                             ALU.mult).then_inc(d_done[bank], 1)
                                    if st.b:
                                        dve.wait_ge(d_done[bank], st.c.nth + 1)
                                        last = dve.tensor_tensor(m, m, g, ALU.add)
                                        if st.rows and r == R - 1:
                                            last.then_inc(rows, 1)
                            elif k == "resid":
                                dve.wait_ge(unit_done, st.c.u + 1)
                                for r in range(R):
                                    bank = 2 * st.c.pair + r
                                    xs = x[:, r, 512 * st.n:512 * st.n + 512]
                                    if st.new == 1.0:
                                        ins = dve.scalar_tensor_tensor(xs, xs, st.old, DB[bank][:, :], ALU.mult, ALU.add)
                                    else:
                                        ins = dve.scalar_tensor_tensor(xs, DB[bank][:, :], st.new, xs, ALU.mult, ALU.add)
                                    ins.then_inc(d_done[bank], 1)
                            elif k == "norm":
                                for bank in range(4):
                                    dve.wait_ge(d_done[bank], st.last_chunks[bank // 2] + 1)
                                dve.wait_ge(p_norm, 16 * (st.which + 1))
                                for r in range(R):
                                    for j in range(2):
                                        last = dve.bn_stats(bst[:, r, j, :], x[:, r, 512 * j:512 * j + 512])
                                    link(last)
                                    link(dve.bn_aggr(bmv[:, r, :], bst[:, r, :, :].rearrange("p a b -> p (a b)")))
                                rs = rsqrt(2, bmv[:, :, 1], 1.0, LN_EPS)
                                for r in range(R):
                                    link(dve.tensor_scalar(x[:, r, :], x[:, r, :], bmv[:, r, 0:1], rs[:, r:r + 1],
                                                           ALU.subtract, ALU.mult))
                                    link(dve.tensor_tensor(x[:, r, :], x[:, r, :], b["ln"][:, 0, :], ALU.mult))
                                    last = dve.tensor_tensor(x[:, r, :], x[:, r, :], b["ln"][:, 1, :], ALU.add)
                                    if r < R - 1:
                                        link(last)
                                last.then_inc(rows, 1)
                            elif k == "rms":
                                dve.wait_ge(sumsq, 2 * st.n)
                                rs = rsqrt(R, ss2[:, 0:R], 1.0 / D, EPS)
                                slot, count = {0: (0, 1), 1: (1, 1), 2: (0, 3), 3: (1, 2)}[st.which]
                                dve.wait_ge(p_gain[slot], 16 * count)
                                for r in range(R):
                                    last = dve.scalar_tensor_tensor(b["merged"][:, r, :], x[:, r, :], rs[:, r:r + 1],
                                                                    b["gain"][:, slot, :], ALU.mult, ALU.mult)
                                last.then_inc(rows, 1)
                            elif k == "p_split":
                                dve.wait_ge(p_ready, 1)
                                dve.tensor_tensor(b["p_l"][:, :, :], b["p_raw"][:, :, :], b["p_h"][:, :, :].bitcast(F32),
                                                  ALU.subtract).then_inc(p_ready, 1)
                            elif k == "m_log":
                                dve.wait_ge(unit_done, st.c.u + 1)
                                dve.wait_ge(p_vec, 16)
                                for r in range(R):
                                    bank = 2 * st.c.pair + r
                                    dve.tensor_tensor(ifv[:, 8 * r:8 * r + 8], DB[bank][:, 0:8], b["vec2"][:, 144:152], ALU.add)\
                                       .then_inc(d_done[bank], 1)
                                for r in range(R):
                                    dve.wait_ge(d_done[2 * st.c.pair + r], st.c.nth + 1)
                                f = ifv.rearrange("p (r g) -> p r g", r=R)[:, :, MH:2 * MH]
                                dve.scalar_tensor_tensor(absf.rearrange("p (r h) -> p r h", r=R), f, -1.0, f, ALU.mult, ALU.max)\
                                   .then_inc(logs, 1)
                                l3 = lf.rearrange("p (r h) -> p r h", r=R)
                                link(dve.tensor_scalar(l3, f, 0.0, None, ALU.min))
                                dve.wait_ge(logs, 3)
                                dve.tensor_tensor(lf, lf, lnf, ALU.subtract).then_inc(logs, 1)
                            elif k == "conv":
                                dve.wait_ge(unit_done, st.c.u + 1)
                                dve.wait_ge(p_conv, 16)
                                for ct in range(2):
                                    c = 2 * st.i + ct
                                    bank = 2 * st.c.pair + ct
                                    t, w = b["mT"][:, c, :], b["convw"][:, c, :]
                                    link(dve.tensor_scalar(t, DB[bank][:, 0:S], w[:, 3:4], w[:, 4:5], ALU.mult, ALU.add))
                                    for back in (1, 2, 3):
                                        ins = dve.scalar_tensor_tensor(t[:, back:S], DB[bank][:, 0:S - back],
                                                                       w[:, 3 - back:4 - back], t[:, back:S], ALU.mult, ALU.add)
                                        if back < 3:
                                            link(ins)
                                    ins.then_inc(d_done[bank], 1)
                            elif k == "conv_silu":
                                dve.wait_ge(conv_tanh, st.i + 1)
                                t = b["mT"][:, 2 * st.i:2 * st.i + 2, :]
                                last = dve.scalar_tensor_tensor(t, b["gt"][:, st.i % 2, :, 0:256], 1.0, t, ALU.add, ALU.mult)
                                last.then_inc(conv_out, 1)
                            elif k == "a_norm":
                                for r in range(R):
                                    dve.wait_ge(squared, r + 1)
                                    dve.tensor_reduce(ssq[:, 20 * r:20 * r + 20], b["sq"][:, :].rearrange(
                                        "p (h k) -> p h k", h=AH + AKV), AXX, ALU.add).then_inc(summed, 1)
                                dve.wait_ge(summed, R)
                                rs = rsqrt(40, ssq, 1.0 / ADH, EPS)
                                dve.tensor_copy(rq2, rs).then_inc(summed, 1)
                            elif k == "m_gate":
                                dve.wait_ge(p_gain[0], 32)
                                for r in range(R):
                                    dve.wait_ge(d_done[2 * st.c.pair + r], st.c.nth + 1)
                                    link(dve.scalar_tensor_tensor(b["mo"][:, r, 512 * st.j:512 * st.j + 512], b["gt_a"][:, st.j, r, :],
                                                                  1.0, b["gain"][:, 0, 512 * st.j:512 * st.j + 512], ALU.add,
                                                                  ALU.mult))
                            elif k == "m_arow":
                                dve.wait_ge(s_ready, st.s + 1)
                                dve.wait_ge(p_bias, 16)
                                h = st.h
                                if h == 0:
                                    dve.tensor_copy(nb, SB[:, 256:264])
                                dve.tensor_tensor_reduce(b["Pn"][:, h, 0:256], SB[:, 0:256], b["masks"][:, 0, :], 1.0, 0.0,
                                                         ALU.add, ALU.max, mx2[:, 4 + h:5 + h])
                                dve.tensor_tensor_reduce(b["Pn"][:, h, 256:384], SB[:, 0:128], b["masks"][:, 0, 128:256], 1.0,
                                                         0.0, ALU.add, ALU.max, mx2[:, h:h + 1]).then_inc(s_done, 1)
                                dve.wait_ge(s_done, st.s + 1)
                                dve.tensor_scalar(nmx2[:, h:h + 5:4], mx2[:, h:h + 5:4], -1.0, None, ALU.mult).then_inc(maxed, 1)
                            elif k == "m_floor":
                                dve.wait_ge(maxed, AH + MH)
                                dve.tensor_tensor(fl, nb, nmx2[:, 0:8], ALU.add).then_inc(floored, 1)
                            elif k == "m_s":
                                dve.wait_ge(s_ready, st.s + 1)
                                dve.wait_ge(soft, AH + st.h + 1)
                                h = st.h
                                for r in (1, 0):
                                    part = slice(0, 256) if r else slice(256, 384)
                                    ins = dve.tensor_tensor_reduce(b["Pn"][:, h, part], SB[:, part], b["Pn"][:, h, part],
                                                                   0.25 * MDH ** -0.5, 0.0, ALU.mult, ALU.add,
                                                                   den[:, 4 * r + h:4 * r + h + 1])
                                ins.then_inc(s_done, 1)
                                dve.wait_ge(s_done, st.s + 1)
                                dve.wait_ge(floored, 2)
                                d2 = rec2[:, h:h + 5:4]
                                link(dve.scalar_tensor_tensor(d2, den[:, h:h + 5:4], -1.0, den[:, h:h + 5:4], ALU.mult, ALU.max))
                                link(dve.tensor_tensor(d2, d2, fl[:, h:h + 5:4], ALU.max))
                                dve.reciprocal(d2, d2).then_inc(rec_done, 1)
                            elif k == "m_fin":
                                dve.wait_ge(o_done, st.o + 1)
                                rs = rsqrt(8, ss2[:, 0:8], 1.0 / MDH, EPS)
                                link(dve.tensor_scalar(rs, rs, 0.5, None, ALU.mult))
                                for h in range(MH):
                                    for r in range(R):
                                        part = b["mo"][:, r, h * MDH:(h + 1) * MDH]
                                        last = dve.scalar_tensor_tensor(part, b["m_o"][:, r, h * MDH:(h + 1) * MDH],
                                                                        rs[:, 2 * h + r:2 * h + r + 1], part, ALU.mult, ALU.mult)
                                last.then_inc(rows, 1)
                            elif k == "aa_s":
                                dve.wait_ge(s_ready, st.s + 1)
                                n = st.h
                                if n == 0:
                                    dve.wait_ge(p_bias, 16)
                                sink = b["vec2"][:, 128 + n:129 + n]
                                dve.tensor_tensor_reduce(b["Pn"][:, n % 4, 0:256], SB[:, 0:256], b["masks"][:, 1, :],
                                                         ADH ** -0.5, sink, ALU.add, ALU.max, mx2[:, 16 + n:17 + n])
                                dve.tensor_tensor_reduce(b["Pn"][:, n % 4, 256:384], SB[:, 256:384], b["masks"][:, 1, 128:256],
                                                         ADH ** -0.5, sink, ALU.add, ALU.max, mx2[:, n:n + 1]).then_inc(s_done, 1)
                                dve.wait_ge(s_done, st.s + 1)
                                ins = dve.tensor_scalar(nmx2[:, n:n + 17:16], mx2[:, n:n + 17:16], -1.0, None, ALU.mult)
                                if n % 4 == 3:
                                    link(ins)
                                    g = n - 3
                                    ins = dve.tensor_tensor(es.rearrange("p (r h) -> p r h", r=R),
                                                            nmx2.rearrange("p (r h) -> p r h", r=R)[:, :, g:g + 4],
                                                            b["vec2"][:, 128 + g:132 + g].unsqueeze(1).broadcast_to([P, R, 4]), ALU.add)
                                ins.then_inc(maxed, 1)
                            elif k == "aa_out":
                                dve.wait_ge(o_ready, st.o + 1)
                                g = st.h - 3
                                r3 = rc[:, 0:8].rearrange("p (r h) -> p r h", r=R)
                                dve.wait_ge(soft, st.h + 1)
                                link(dve.tensor_tensor(r3, sm2.rearrange("p (r h) -> p r h", r=R)[:, :, g:g + 4],
                                                       es.rearrange("p (r h) -> p r h", r=R), ALU.add))
                                link(dve.reciprocal(rc[:, 0:8], rc[:, 0:8]))
                                for r in range(R):
                                    dst = b["aqk"][:, r, ADH * g:ADH * g + 256].rearrange("p (h n) -> p h n", h=4)
                                    last = dve.tensor_tensor(dst, OB[:, 256 * r:256 * r + 256].rearrange("p (h n) -> p h n", h=4),
                                                             rc[:, 4 * r:4 * r + 4].unsqueeze(2).broadcast_to([P, 4, ADH]), ALU.mult)
                                last.then_inc(o_done, 1)
                            elif k in ("merge2", "ple"):
                                dve.wait_ge(unit_done, st.c.u + 1)
                                for r in range(R):
                                    dve.wait_ge(d_done[2 * st.gate.pair + r], st.gate.nth + 1)
                                for r in range(R):
                                    bank = 2 * st.c.pair + r
                                    g = b[st.which][:, st.j, r, :]
                                    cols = slice(st.j * 512, (st.j + 1) * 512)
                                    first = st.first
                                    dve.scalar_tensor_tensor(b["merged"][:, r, cols] if first else g, g, 1.0, DB[bank][:, :],
                                                             ALU.add, ALU.mult).then_inc(d_done[bank], 1)
                                    dve.wait_ge(d_done[bank], st.c.nth + 1)
                                    if k == "ple":
                                        link(dve.scalar_tensor_tensor(x[:, r, cols], g, 0.5, x[:, r, cols], ALU.mult, ALU.add))
                                    elif not first:
                                        last = dve.tensor_tensor(b["merged"][:, r, cols], b["merged"][:, r, cols], g, ALU.add)
                                        if st.rows and r == R - 1:
                                            last.then_inc(rows, 1)
                                        else:
                                            link(last)
                            elif k == "swiglu":
                                for r in range(R):
                                    bank = 2 * st.c.pair + r
                                    dve.wait_ge(silu, 2 * st.m + r + 1)
                                    if st.width < 256:
                                        dve.memset(b["ffn_a"][:, st.i % 2, r, st.width:256], 0.0)
                                    dve.tensor_tensor(b["ffn_a"][:, st.i % 2, r, 0:st.width], b["ffn_s"][:, st.i % 2, r, 0:st.width],
                                                      DB[bank][:, st.width:2 * st.width], ALU.mult).then_inc(d_done[bank], 1)

                    @block.tensor
                    def _(pe):
                        def turned(t):
                            pe.wait_ge(t_done[t % 2], t // 2 + 1)
                            if t:
                                pe.wait_ge(t_done[(t - 1) % 2], (t - 1) // 2 + 1)

                        for st in steps:
                            k = st.kind
                            if k == "unit":
                                if st.first and st.nth:
                                    for r in range(R):
                                        pe.wait_ge(d_done[2 * st.pair + r], st.nth)
                                if st.after_t is not None:
                                    turned(st.after_t)
                                pe.wait_ge(lo_done, st.u + 1)
                                if st.lhs == "p":
                                    pe.wait_ge(p_ready, 2)
                                lh, ll = split_of[st.lhs]
                                s = st.u % NS
                                if st.form == "features":
                                    for ct in range(2):
                                        out = DB[2 * st.pair + ct][:, 0:S]
                                        for i in range(st.nk):
                                            kt, at = st.kt0 + i, i * st.n + ct * P
                                            w_h, w_l = wh[:, s, at:at + P], wl[:, s, at:at + P]
                                            pe.matmul(out, w_h, lh[:, kt, :], start=st.first and i == 0, stop=False)
                                            pe.matmul(out, w_h, ll[:, kt, :], start=False, stop=False)
                                            last = pe.matmul(out, w_l, lh[:, kt, :], start=False,
                                                             stop=st.last and i == st.nk - 1)
                                    last.then_inc(unit_done, 1)
                                    continue
                                for r in range(R):
                                    out = DB[2 * st.pair + r][:, 0:st.n]
                                    for i in range(st.nk):
                                        kt = st.kt0 + i
                                        h, lo = lh[:, kt, r * P:r * P + P], ll[:, kt, r * P:r * P + P]
                                        w_h, w_l = wh[:, s, i * st.n:(i + 1) * st.n], wl[:, s, i * st.n:(i + 1) * st.n]
                                        pe.matmul(out, h, w_h, start=st.first and i == 0, stop=False)
                                        pe.matmul(out, h, w_l, start=False, stop=False)
                                        last = pe.matmul(out, lo, w_h, start=False, stop=st.last and i == st.nk - 1)
                                last.then_inc(unit_done, 1)
                            elif k in ("split", "split_act", "turn", "a_turn", "probs_T"):
                                bank = TB[st.t % 2]
                                if st.t >= 2:
                                    pe.wait_ge(t_done[st.t % 2], st.t // 2)
                                if k == "split":
                                    if st.rows:
                                        pe.wait_ge(rows, st.rows)
                                    if st.after_o:
                                        pe.wait_ge(o_done, st.after_o)
                                    src = [b[st.src][:, st.tile, (st.kg + i) * P:(st.kg + i + 1) * P] for i in range(4)]
                                elif k == "split_act":
                                    for r in range(R):
                                        pe.wait_ge(d_done[2 * st.made.pair + r], st.made.nth + 1)
                                    src = [b["ffn_a"][:, st.i % 2, r, i * P:(i + 1) * P] for i in range(2) for r in range(R)]
                                elif k == "a_turn":
                                    pe.wait_ge(a_normed, st.tile + 1)
                                    if st.half == 2:
                                        src = [b["akd"][:, st.tile, i, :, :].rearrange("p a k -> p (a k)") for i in range(AKV)]
                                    else:
                                        src = [b["aqk"][:, st.tile, (4 * st.half + i) * P:(4 * st.half + i + 1) * P] for i in range(4)]
                                elif k == "turn":
                                    if st.roped:
                                        pe.wait_ge(roped, st.roped)
                                    else:
                                        for r in range(R):
                                            pe.wait_ge(d_done[2 * st.kept.c.pair + r], st.kept.c.nth + 1)
                                    src = [b[st.src][:, st.tile, i * P:(i + 1) * P] for i in range(4)]
                                else:
                                    if st.of == "ca" or st.of == "aa":
                                        pe.wait_ge(soft, st.n)
                                    elif st.of == "da":
                                        pe.wait_ge(mixed, st.n)
                                    else:
                                        pe.wait_ge(s_done, st.n)
                                    pn = b["Pn"][:, st.slot, :]
                                    src = [pn[:, 256:384], pn[:, 0:128], pn[:, 128:256]]
                                for i, piece in enumerate(src):
                                    last = pe.transpose(bank[:, i * P:(i + 1) * P], piece, ident[:, :])
                                last.then_inc(t_ready[st.t % 2], 1)
                            elif k == "ret_s":
                                if st.s:
                                    pe.wait_ge(s_done, st.s)
                                turned(st.after_t)
                                h = st.h
                                pe.matmul(SB[:, 0:256], b["kT"][:, h, 0:P], b["qT"][:, h, :], start=True, stop=True)
                                pe.matmul(SB[:, 256:384], b["kT"][:, h, P:S], b["qT"][:, h, P:S], start=True, stop=True)\
                                  .then_inc(s_ready, 1)
                            elif k in ("ca_s", "da_s"):
                                if st.s:
                                    pe.wait_ge(s_done, st.s)
                                turned(st.after_t)
                                n = st.h if k == "ca_s" else st.g
                                p0 = 64 * (n % 2)
                                qT, kT = b["qT"][p0:p0 + 64, n // 2, :], b["kT"][p0:p0 + 64, n // 2, :]
                                pe.matmul(SB[:, 0:256], qT[:, P:S], kT, start=True, stop=True)
                                pe.matmul(SB[:, 256:384], qT[:, 0:P], kT[:, 0:P], start=True, stop=True)\
                                  .then_inc(s_ready, 1)
                            elif k == "m_arow":
                                if st.s:
                                    pe.wait_ge(s_done, st.s)
                                pe.wait_ge(spread_out, 2)
                                pe.wait_ge(p_bias, 16)
                                h, tri = st.h, b["masks"][:, 2, :]
                                lb, ib = b["lfb"], b["ib"]
                                if h == 0:
                                    pe.matmul(SB[:, 256:260], tri[:, 0:P], lf[:, 0:MH], start=True, stop=True)
                                    pe.matmul(SB[:, 260:264], tri[:, P:S], lf[:, 0:MH], start=True, stop=False)
                                    pe.matmul(SB[:, 260:264], tri[:, 0:P], lf[:, MH:2 * MH], start=False, stop=True)
                                pe.matmul(SB[:, 0:P], lb[:, 0, h, :], tri[:, 0:P], start=True, stop=False)
                                pe.matmul(SB[:, 0:P], ib[:, 0, h, :], ident[:, :], start=False, stop=True)
                                pe.matmul(SB[:, P:S], lb[:, 0, h, :], tri[:, P:S], start=True, stop=False)
                                pe.matmul(SB[:, P:S], lb[:, 1, h, :], tri[:, 0:P], start=False, stop=False)
                                pe.matmul(SB[:, P:S], ib[:, 1, h, :], ident[:, :], start=False, stop=True).then_inc(s_ready, 1)
                            elif k == "m_s":
                                if st.s:
                                    pe.wait_ge(s_done, st.s)
                                pe.wait_ge(conv_out, 8)
                                for r, cols in ((1, slice(0, 256)), (0, slice(256, 384))):
                                    for kk in range(2):
                                        ins = pe.matmul(SB[:, cols], b["mT"][:, 2 * st.h + kk, r * P:r * P + P],
                                                        b["mT"][:, 8 + 2 * st.h + kk, 0:(r + 1) * P], start=kk == 0, stop=kk == 1)
                                ins.then_inc(s_ready, 1)
                            elif k == "m_pv":
                                turned(st.t)
                                if st.o:
                                    pe.wait_ge(o_done, st.o)
                                for kept in st.kept:
                                    for r in range(R):
                                        pe.wait_ge(d_done[2 * kept.c.pair + r], kept.c.nth + 1)
                                pt = b["PT"][:, st.h % 2, :]
                                vs = [b["mv"][:, r, st.h * MDH:(st.h + 1) * MDH] for r in range(R)]
                                pe.matmul(OB[:, 0:MDH], pt[:, 0:P], vs[0], start=True, stop=True)
                                pe.matmul(OB[:, MDH:512], pt[:, P:S], vs[0], start=True, stop=False)
                                pe.matmul(OB[:, MDH:512], pt[:, S:384], vs[1], start=False, stop=True).then_inc(o_ready, 1)
                            elif k == "aa_s":
                                if st.s:
                                    pe.wait_ge(s_done, st.s)
                                turned(st.after_t)
                                p0 = 64 * (st.h % 2)
                                qT, kT = b["aqT"][p0:p0 + 64, st.h // 2, :], b["akT"][p0:p0 + 64, st.h // 4, :]
                                pe.matmul(SB[:, 0:256], qT[:, P:S], kT, start=True, stop=True)
                                pe.matmul(SB[:, 256:384], qT[:, 0:P], kT[:, 0:P], start=True, stop=True).then_inc(s_ready, 1)
                            elif k == "aa_pv":
                                turned(st.t)
                                if st.h % 4 == 0:
                                    if st.o:
                                        pe.wait_ge(o_done, st.o)
                                for r in range(R):
                                    pe.wait_ge(d_done[2 * st.kept.c.pair + r], st.kept.c.nth + 1)
                                pt = b["PT"][:, st.h % 2, :]
                                kv = st.h // 4
                                out = [OB[:, 256 * r + ADH * (st.h % 4):256 * r + ADH * (st.h % 4 + 1)] for r in range(R)]
                                vs = [b["av"][:, r, kv * ADH:(kv + 1) * ADH] for r in range(R)]
                                pe.matmul(out[0], pt[:, 0:P], vs[0], start=True, stop=True)
                                pe.matmul(out[1], pt[:, P:S], vs[0], start=True, stop=False)
                                last = pe.matmul(out[1], pt[:, S:384], vs[1], start=False, stop=True)
                                if st.h % 4 == 3:
                                    last.then_inc(o_ready, 1)
                            elif k == "ret_pv":
                                pe.wait_ge(s_done, st.s + 1)
                                if st.o:
                                    pe.wait_ge(o_done, st.o)
                                for kept in st.kept:
                                    for r in range(R):
                                        pe.wait_ge(d_done[2 * kept.c.pair + r], kept.c.nth + 1)
                                pr = b["Pn"][:, st.h % 4, :]
                                vs = [b["rv"][:, r, st.h * RDV:(st.h + 1) * RDV] for r in range(R)]
                                pe.matmul(OB[:, 0:RDV], pr[:, 0:P], vs[0], start=True, stop=True)
                                pe.matmul(OB[:, RDV:512], pr[:, P:S], vs[0], start=True, stop=False)
                                pe.matmul(OB[:, RDV:512], pr[:, S:384], vs[1], start=False, stop=True).then_inc(o_ready, 1)
                            elif k in ("ca_pv", "da_pv"):
                                turned(st.t)
                                if k == "da_pv" or st.h % 4 == 0:
                                    if st.o:
                                        pe.wait_ge(o_done, st.o)
                                for r in range(R):
                                    pe.wait_ge(d_done[2 * st.kept.c.pair + r], st.kept.c.nth + 1)
                                pt = b["PT"][:, st.h % 2, :]
                                if k == "ca_pv":
                                    out = [OB[:, 256 * r + CDH * (st.h % 4):256 * r + CDH * (st.h % 4 + 1)] for r in range(R)]
                                    vs = [b["cv"][:, r, st.h * CDH:(st.h + 1) * CDH] for r in range(R)]
                                else:
                                    out = [OB[:, r * P:(r + 1) * P] for r in range(R)]
                                    vs = [b["dv"][:, r, st.h * P:(st.h + 1) * P] for r in range(R)]
                                pe.matmul(out[0], pt[:, 0:P], vs[0], start=True, stop=True)
                                pe.matmul(out[1], pt[:, P:S], vs[0], start=True, stop=False)
                                last = pe.matmul(out[1], pt[:, S:384], vs[1], start=False, stop=True)
                                if k == "da_pv" or st.h % 4 == 3:
                                    last.then_inc(o_ready, 1)

                nc.all_engine_barrier(sems_to_clear=range(first_cleared, last_cleared + 1))

        with nc.Block() as block:
            @block.sync
            def _(sp):
                last = 1 if plan2.steps else 0
                for s in range(NRAW):
                    sp.wait_ge(w_loaded[s], 16 * (slot_base[last][s] + DEPTH * cnt[last][s] + 1))
                sp.dma_start(a["out"].rearrange("(r p) d -> p r d", p=P), x[:, :, :]).then_inc(stored, 16)
                sp.wait_ge(stored, 16)


def constants():
    f = np.float32
    n = np.arange(S)
    c = {"ident": np.eye(P, dtype=f)}
    lg = np.log1p(-np.exp2(-5.0 - np.arange(RH)))
    dist = n[None, :] - n[:, None]
    same = n[None, :] // CHUNK == n[:, None] // CHUNK
    seen = n[None, :] // CHUNK > n[:, None] // CHUNK
    dec = np.exp(lg[:, None, None] * np.abs(dist)) * (same | seen) * RDK ** -0.5
    c["decay"] = np.concatenate([dec[:, :P, :], dec[:, P:, P:]], 2).transpose(1, 0, 2).astype(f)
    rope = np.zeros((S, 2, 96), f)
    for d, at in ((RDK, 0), (DDH, RDK // 2)):
        inv = (f(ROPE_THETA) ** (-np.arange(0, d, 2, dtype=f) / f(d))).astype(f)
        ang = (n.astype(f)[:, None] * inv[None, :]).astype(f)
        rope[:, 0, at:at + d // 2], rope[:, 1, at:at + d // 2] = np.cos(ang), np.sin(ang)
    c["rope"] = rope.reshape(R, P, 2, 96).transpose(1, 0, 2, 3)
    m = np.zeros((P, S), f)
    m[:CHUNK, 192:] = NEG * DDH ** 0.5
    c["dmask"] = m
    i, j = np.arange(P)[:, None], np.arange(S)[None, :]
    causal = np.where(j <= P + i, 0.0, NEG)
    window = np.where((j <= P + i) & (P + i - j < WINDOW), 0.0, NEG * ADH ** 0.5)
    tri = np.where((j >= i) | (j >= P), -1.0, 0.0)
    c["masks"] = np.stack([causal, window, tri], 1).astype(f)
    return c


def weight_stream(inputs, plans, suffixes):
    total = sum(DEPTH * len(p.units) for p in plans) + NRAW
    out = np.zeros((total, P, UNIT), np.float32)
    at = 0
    for plan, suffix in zip(plans, suffixes):
        for l in range(DEPTH):
            for (names, cols), kt0, nk, n in plan.units:
                names = (names,) if isinstance(names, str) else names
                mats = [inputs[name + suffix][l] for name in names]
                k0, k1 = kt0 * P, min((kt0 + nk) * P, mats[0].shape[0])
                part = np.concatenate([m[k0:k1, c0:c1] for m in mats for c0, c1 in cols], 1)
                full = np.zeros((nk * P, n), np.float32)
                full[:k1 - k0] = part
                out[at, :, :nk * n] = full.reshape(nk, P, n).transpose(1, 0, 2).reshape(P, nk * n)
                at += 1
    return out


def spread(*vectors):
    v = np.concatenate([np.asarray(x, np.float32).reshape(DEPTH, -1) for x in vectors], 1)
    return np.ascontiguousarray(np.broadcast_to(v[:, None, :], (DEPTH, P, v.shape[1])))
def finish_plan(p):
    n = m = g2 = 0
    seen_t = None
    last_chunks = [0, 0]
    o = 0
    p.steps = [st for st in p.steps if st.kind != "pause"]
    for st in p.steps:
        if st.kind in ("split", "split_act"):
            n += 1
            st.n = n
        if st.kind == "resid":
            last_chunks[st.c.pair] = st.c.nth
        if st.kind == "unit":
            if st.after_t == seen_t or st.lhs == "p":
                st.after_t = None
            else:
                seen_t = st.after_t
        if st.kind == "swiglu":
            st.m = m
            m += 1
        if st.kind == "gate2":
            g2 += 1
            st.n = g2
        if st.kind in ("norm", "rms"):
            st.last_chunks = tuple(last_chunks)
        if st.o is not None:
            o = st.o
        if st.kind in ("ret_fin", "da_fin", "m_fin"):
            st.o = o
    return p

def kernel(**inputs):
    import concourse.bacc as bacc
    from concourse.bass_utils import run_bass_kernel_spmd as run
    inputs = {k: np.asarray(v) for k, v in inputs.items()}
    plan1 = finish_plan(plan_block1())
    plan2 = finish_plan(plan_block2())
    f = np.float32
    arrays = dict(constants())
    arrays["x"] = inputs["x"][0]
    arrays["weights"] = weight_stream(inputs, [plan1, plan2], ["", "_2"])
    rb = inputs["ca_rel_bias"]
    idx = 384 + np.arange(P)[:, None] - np.arange(S)[None, :]
    arrays["bias"] = np.ascontiguousarray(rb[:, :, idx].transpose(0, 2, 1, 3)).reshape(DEPTH, P, CH * S)
    li = np.array([[0.8 - 0.6 * math.exp(-0.3 * l), 0.6 * math.exp(-0.3 * l) + 0.2] for l in range(DEPTH)], f)
    arrays["vec"] = spread(inputs["ret_norm_g"], inputs["da_norm_g"], inputs["da_lambda_q1"], inputs["da_lambda_k1"],
                           inputs["da_lambda_q2"], inputs["da_lambda_k2"], li)
    arrays["b_merge"] = spread(inputs["b_merge"])
    arrays["ln1"] = spread(inputs["ln1_g"], inputs["ln1_b"])
    arrays["ln2"] = spread(inputs["ln2_g"], inputs["ln2_b"])
    for key, name in (("gain_ffn1", "ffn1_norm_2"), ("gain_mix", "mix_norm_2"), ("gain_m", "m_out_norm_2"),
                      ("gain_ffn2", "ffn2_norm_2"), ("gain_ple", "ple_norm_2")):
        arrays[key] = spread(inputs[name])
    arrays["vec2"] = spread(inputs["a_q_norm_2"], inputs["a_k_norm_2"], inputs["a_sinks_2"], inputs["m_igate_b_2"],
                            inputs["m_fgate_b_2"])
    taps = np.concatenate([inputs["m_conv_w_2"], inputs["m_conv_b_2"][:, None, :]], 1)
    arrays["convw"] = taps.reshape(DEPTH, CONV_K + 1, 16, P).transpose(0, 3, 2, 1).reshape(DEPTH, P, 16 * (CONV_K + 1))
    pt = inputs["p_2"][:, 0].transpose(0, 2, 1)
    arrays["p"] = pt.reshape(DEPTH, 2, P, S).transpose(0, 2, 1, 3).reshape(DEPTH, P, 2 * S)
    nc = bacc.Bacc("TRN2", target_bir_lowering=False, num_devices=1)
    arrays = {"in_" + k: np.ascontiguousarray(v) for k, v in arrays.items()}
    a = {k[3:]: nc.dram_tensor(k, v.shape, F32, kind="ExternalInput").ap() for k, v in arrays.items()}
    a["out"] = nc.dram_tensor("out", (S, D), F32, kind="ExternalOutput").ap()
    build(nc, plan1, plan2, a)
    r = run(nc, [arrays], core_ids=[0])
    return r.results[0]["out"].reshape(1, S, D)
```

```python
import math
from contextlib import ExitStack

import concourse.bass as bass
import numpy as np
from concourse import mybir

F32 = mybir.dt.float32
F32R = mybir.dt.float32r
I32 = mybir.dt.int32
ALU = mybir.AluOpType
ACT = mybir.ActivationFunctionType
AXX = mybir.AxisListType.X

P = 128
S = 256
R = S // P
D = 1024
KT = D // P
DEPTH = 2
CHUNK = 64
NEG = -1e30

UNIT = 1024
NRAW = 6
NS = 4

CONV_ROOM = 0.75
BEHIND = 1
LAG = 2

RH, RDK, RDV = 4, 128, 256
CH, CDH = 8, 64
GH = 8
DH, DDH = 4, 64
F1 = 2816
ALPHA = (2.0 * DEPTH) ** 0.25
LN_EPS = 1e-5
ROPE_THETA = 10000.0

F2 = 2752
EPS = 1e-6
MH, MDH = 4, 256
CONV_K = 4
AH, AKV, ADH = 16, 4, 64
WINDOW = 128
PLE = 256
HALF = D // 2
GAIN = {0: (0, 1), 1: (1, 1), 2: (0, 3), 3: (1, 2)}


class Step:

    def __init__(self, after_o=None, after_t=None, apply=None, b=None, c=None, dst=None, early=None,
                 end=None, fed=None, first=None, form=None, g=None, gate=None, h=None, half=None,
                 heads=None, i=None, j=None, kept=None, kg=None, kind=None, kt0=None, last=None,
                 last_chunks=None, lhs=None, m=None, made=None, n=None, new=None, nk=None, nth=None,
                 o=None, of=None, off=None, old=None, pair=None, roped=None, rows=None, s=None,
                 scale=None, scaled=None, slot=None, src=None, t=None, table=None, tile=None,
                 tiles=None, u=None, which=None, width=None):
        self.after_o = after_o
        self.after_t = after_t
        self.apply = apply
        self.b = b
        self.c = c
        self.dst = dst
        self.early = early
        self.end = end
        self.fed = fed
        self.first = first
        self.form = form
        self.g = g
        self.gate = gate
        self.h = h
        self.half = half
        self.heads = heads
        self.i = i
        self.j = j
        self.kept = kept
        self.kg = kg
        self.kind = kind
        self.kt0 = kt0
        self.last = last
        self.last_chunks = last_chunks
        self.lhs = lhs
        self.m = m
        self.made = made
        self.n = n
        self.new = new
        self.nk = nk
        self.nth = nth
        self.o = o
        self.of = of
        self.off = off
        self.old = old
        self.pair = pair
        self.roped = roped
        self.rows = rows
        self.s = s
        self.scale = scale
        self.scaled = scaled
        self.slot = slot
        self.src = src
        self.t = t
        self.table = table
        self.tile = tile
        self.tiles = tiles
        self.u = u
        self.which = which
        self.width = width


class Plan:

    def __init__(self):
        self.steps = []
        self.units = []
        self.t = self.s = self.o = self.rows = self.roped = self.probs = self.n_gate = 0
        self.d = [0, 0]
        self.cc = {}
        self.early = 0
        self.lead = None

    def add(self, kind, **kw):
        self.steps.append(Step(kind=kind, **kw))
        return self.steps[-1]

    def begin(self):
        kept, self.steps = self.steps, []
        return kept

    def weave(self, before, dense, side):
        def room(st):
            return 0.0 if st.kind != "unit" else CONV_ROOM if st.form == "features" else 1.0

        n, done, put = sum(room(st) for st in dense), 0, 0
        self.steps = before
        for st in dense:
            if st.kind == "unit":
                while any(sd.t == st.after_t for sd in side[put:]):
                    self.steps.append(side[put])
                    put += 1
            self.steps.append(st)
            if st.kind == "unit":
                done += room(st)
                upto = max(put, int(len(side) * done / n + 1e-6))
                self.steps += side[put:upto]
                put = upto

    def pause(self, n):
        for _ in range(n):
            self.add("pause")

    def count(self, name):
        self.cc[name] = self.cc.get(name, 0) + 1
        return self.cc[name]

    def next_t(self):
        self.t += 1
        return self.t - 1

    def next_s(self):
        self.s += 1
        return self.s - 1

    def next_o(self):
        self.o += 1
        return self.o - 1

    def unit(self, w, lhs, kt0, nk, n, pair, nth, first, last, after_t, form="rows"):
        u = len(self.units)
        self.units.append((w, kt0, nk, n))
        self.add("unit", u=u, lhs=lhs, kt0=kt0, nk=nk, n=n, pair=pair, nth=nth, first=first, last=last,
                 after_t=after_t, form=form)
        return u

    def next_d(self, pair):
        self.d[pair] += 1
        return self.d[pair] - 1

    def chunk(self, w, lhs, nkt, n, pair, after_t, form="rows"):
        nth = self.next_d(pair)
        per = UNIT // n
        groups = [(k, min(per, nkt - k)) for k in range(0, nkt, per)]
        for i, (k0, nk) in enumerate(groups):
            u = self.unit(w, lhs, k0, nk, n, pair, nth, i == 0, i == len(groups) - 1, after_t, form)
        if self.lead:
            (turn, behind, at), self.lead = self.lead, None
            kept = self.steps[:-len(groups)]
            self.steps = self.steps[-len(groups):]
            group = self.first_tiles(len(groups), turn)
            first = self.steps
            self.steps = kept + first[:at] + behind + first[at:] + group
        return Step(u=u, pair=pair, nth=nth)

    def first_tiles(self, k, turn=None):
        group, self.steps = self.steps[-k:], self.steps[:-k]
        for st in group:
            assert st.kind == "unit"
            st.tiles = (1,)
            self.early += 1
            self.add("first_tile", u=st.u, lhs=st.lhs, kt0=st.kt0, nk=st.nk, n=st.n, pair=st.pair, nth=st.nth,
                     first=st.first, last=st.last, after_t=st.after_t if turn is None else turn, tiles=(0,),
                     end=group[-1].u)
        return group

    def turns(self, src, dst, nkt, tile, scale=1.0, rows=0, fed=0):
        for kg in range(0, nkt, 4):
            last = self.next_t()
            self.add("split", t=last, src=src, dst=dst, tile=tile, kg=kg, scale=scale, rows=rows, fed=fed)
        return last

    def tail(self, k, at, finish, turned, behind=3):
        group = self.first_tiles(k)
        finish(0)
        for i, st in enumerate(group):
            self.steps.append(st)
            if i == at:
                turn = turned(0)
        finish(1)
        kept = self.begin()
        last = turned(1)
        self.lead = (turn, self.begin(), behind)
        self.steps = kept
        return last

    def start(self, turned, behind):
        turn = turned(0)
        kept = self.begin()
        last = turned(1)
        self.lead = (turn, self.begin(), behind)
        self.steps = kept
        return last


def plan_block1():
    p = Plan()

    def split_rows(src, dst, nkt, scale=1.0, rows=0, after_o=0):
        for r in range(R):
            for kg in range(0, nkt, 4):
                last = p.next_t()
                p.add("split", t=last, src=src, dst=dst, tile=r, kg=kg, scale=scale, rows=rows, after_o=after_o)
        return last

    t_x = p.start(lambda tile: p.turns("x", "x", KT, tile), 1)

    q = {}
    for i, name in enumerate(("cq", "ck", "cv")):
        c = p.chunk(("w_in", [(3072 + 512 * i, 3584 + 512 * i)]), "x", KT, 512, i % 2, t_x)
        q[name] = p.add("keep", c=c, dst=name, off=0)
    p.add("lambda")

    before = p.begin()
    for i, (name, c0, buf, off) in enumerate([
            ("rq", 0, "rq", 0), ("rk", 512, "rk", 0), ("rv0", 1024, "rv", 0), ("rv1", 1536, "rv", 512)]):
        c = p.chunk(("w_in", [(c0, c0 + 512)]), "x", KT, 512, (i + 1) % 2, t_x)
        q[name] = p.add("keep", c=c, dst=buf, off=off)
        if name in ("rq", "rk"):
            q[name + "_rope"] = p.add("rope", of=q[name], src=buf, heads=RH, half=RDK // 2, table="ret", n=p.count("roped"))
    for j in range(2):
        c = p.chunk(("w_in", [(2048 + 512 * j, 2560 + 512 * j)]), "x", KT, 512, (j + 1) % 2, t_x)
        p.add("ret_gate", c=c, j=j)
    for i, name in enumerate(("dq", "dk", "dv")):
        c = p.chunk(("w_in", [(4608 + 512 * i, 5120 + 512 * i)]), "x", KT, 512, (i + 1) % 2, t_x)
        q[name] = p.add("keep", c=c, dst=name, off=0)
        if name in ("dq", "dk"):
            q[name + "_rope"] = p.add("rope", of=q[name], src=name, heads=GH, half=DDH // 2, table="da",
                                      n=p.count("roped"))

    def gate(b, j, pair):
        c0 = 6144 + b * D + 512 * j
        c = p.chunk(("w_in", [(c0, c0 + 512)]), "x", KT, 512, pair, t_x)
        p.add("gate", c=c, b=b, j=j, n=p.count("gates"))

    def merge(b, j, w, lhs, nkt, t_l, pair):
        c = p.chunk((w, [(512 * j, 512 * j + 512)]), lhs, nkt, 512, pair, t_l)
        p.add("merge", c=c, b=b, j=j, n=2 * b + j + 1)

    for j in range(2):
        gate(0, j, j)
    dense_a = p.begin()

    for src in ("cq", "ck"):
        for r in range(R):
            t_c = p.next_t()
            p.add("turn", t=t_c, src=src, dst="qT" if src == "cq" else "kT", tile=r, roped=None, kept=q[src])
    tt = {}
    for i in range(CH + LAG + 1):
        if i < CH:
            p.add("ca_s", h=i, s=p.next_s(), after_t=t_c)
        if LAG <= i < CH + LAG:
            h = i - LAG
            tt[h] = p.next_t()
            p.add("probs_T", h=h, t=tt[h], of="ca", n=h + 1, slot=h % 4)
        if i > LAG:
            h = i - LAG - 1
            if h % 4 == 0:
                o = p.next_o()
            p.add("ca_pv", h=h, o=o, t=tt[h], kept=q["cv"])
            if h % 4 == 3:
                p.add("ca_out", h=h, o=o)
    p.pause(2)
    t_b = split_rows("cq", "ob", 4, after_o=o + 1)

    for src in ("rq", "rk"):
        for r in range(R):
            t_r = p.next_t()
            p.add("turn", t=t_r, src=src, dst="qT" if src == "rq" else "kT", tile=r, roped=q[src + "_rope"].n, kept=None)
    for i in range(RH + 1):
        if i < RH:
            q["ret_s", i] = p.add("ret_s", h=i, s=p.next_s(), after_t=t_r)
        if i >= 1:
            p.add("ret_pv", h=i - 1, s=q["ret_s", i - 1].s, o=p.next_o(), kept=(q["rv0"], q["rv1"]))
    p.add("ret_fin", rows=p.count("rows"))
    p.pause(8)
    t_a = split_rows("rg", "oa", KT, rows=p.cc["rows"])

    for src in ("dq", "dk"):
        for r in range(R):
            t_d = p.next_t()
            p.add("turn", t=t_d, src=src, dst="qT" if src == "dq" else "kT", tile=r, roped=q[src + "_rope"].n, kept=None)
    for i in range(DH + 2):
        if i >= 2:
            tt[i - 2] = p.next_t()
            p.add("probs_T", h=i - 2, t=tt[i - 2], of="da", n=i - 1, slot=(2 * (i - 2)) % 4)
        if i < DH:
            for m in range(2):
                p.add("da_s", g=2 * i + m, s=p.next_s(), after_t=t_d)
        if 1 <= i <= DH:
            p.add("da_mix", h=i - 1, n=p.count("mixed"))
        if i >= 2:
            p.add("da_pv", h=i - 2, o=p.next_o(), t=tt[i - 2], kept=q["dv"])
    p.add("da_fin", rows=p.count("rows"))
    p.pause(5)
    t_c2 = split_rows("dq", "oc", 4, rows=p.cc["rows"])
    side = p.begin()
    for j in range(2):
        merge(0, j, "w_branch_a", "oa", KT, t_a, j)
    for b in (1, 2):
        for j in range(2):
            gate(b, j, j)
    for j in range(2):
        merge(1, j, "w_branch_b", "ob", 4, t_b, j)
    p.weave(before, dense_a + p.begin(), side)
    cs = [p.chunk(("w_branch_c", [(512 * j, 512 * j + 512)]), "oc", 4, 512, j, t_c2) for j in range(2)]

    done = p.cc["rows"] + 1

    def merged(tile):
        for j in range(2):
            p.add("merge", c=cs[j], b=2, j=j, n=5 + j, tile=tile, early=0 if tile else p.early,
                  rows=p.count("rows") if j == 1 else None)

    t_m = p.tail(4, 2, merged, lambda tile: p.turns("merged", "x", KT, tile, 0.5, rows=done + tile))
    c = p.chunk(("w_out", [(0, 512)]), "x", KT, 512, 0, t_m)
    p.add("resid", c=c, n=0, old=ALPHA, new=1.0)
    c = p.chunk(("w_out", [(512, 1024)]), "x", KT, 512, 1, t_m)

    def rest(tile):
        p.add("resid", c=c, n=1, old=ALPHA, new=1.0, tile=tile, early=0 if tile else p.early)
        p.add("norm", which=0, tile=tile, n=p.count("fed"))

    t_x2 = p.tail(4, 3, rest, lambda tile: p.turns("x", "x", KT, tile, fed=1 + tile), 3)
    plan_ffn(p, "w_ffn_in", "w_ffn_in", "w_ffn_out", F1, F1, t_x2, ALPHA, 1.0,
             lambda tile: p.add("norm", which=1, tile=tile, n=p.count("fed")), None)
    return p


def plan_ffn(p, w_gate, w_up, w_down, width, up_at, t_x, old, new, fresh, turned, scaled=None):
    nch = -(-width // 256)
    turn_of, chunks, widths = [], [], []

    def turn_chunk(i):
        turn_of.append(p.next_t())
        p.add("split_act", t=turn_of[i], i=i, width=widths[i], made=chunks[i])

    for c in range(nch):
        w = min(256, width - 256 * c)
        if w_gate == w_up:
            sel = (w_gate, [(256 * c, 256 * c + w), (up_at + 256 * c, up_at + 256 * c + w)])
        else:
            sel = ((w_gate, w_up), [(256 * c, 256 * c + w)])
        chunks.append(p.chunk(sel, "x", KT, 2 * w, c % 2, t_x))
        widths.append(w)
        p.add("swiglu", c=chunks[c], i=c, width=w, scaled=scaled)
        if c:
            turn_chunk(c - 1)
    kt = -(-width // P)
    per = UNIT // 512
    nth = [p.next_d(0), p.next_d(1)]
    ends = [0, 0]
    free, held = nch % 2, 1 - nch % 2
    order = [(0, free), (per, free), (0, held), (per, held)] + [(k0, j) for k0 in range(2 * per, kt, per) for j in range(2)]
    for i, (k0, j) in enumerate(order):
        nk = min(per, kt - k0)
        ends[j] = p.unit((w_down, [(512 * j, 512 * j + 512)]), "act", k0, nk, 512, j, nth[j], k0 == 0,
                         k0 + nk == kt, turn_of[(k0 + nk - 1) // 2])
        if i == BEHIND:
            turn_chunk(nch - 1)

    def finish(tile):
        for j in range(2):
            p.add("resid", c=Step(u=ends[j], pair=j, nth=nth[j]), n=j, old=old, new=new, tile=tile,
                  early=0 if tile else p.early)
        fresh(tile)

    if turned:
        return p.tail(4, 1, finish, turned)
    group = p.first_tiles(4)
    finish(0)
    p.steps += group
    finish(1)


def plan_block2():
    p = Plan()

    def split_rows(src, dst, nkt, scale=1.0, rows=0, after_o=0):
        for r in range(R):
            for kg in range(0, nkt, 4):
                last = p.next_t()
                p.add("split", t=last, src=src, dst=dst, tile=r, kg=kg, scale=scale, rows=rows, after_o=after_o)
        return last

    def rms(which, tile):
        p.add("rms", which=which, tile=tile, n=p.count("fed"))
        if which == 1:
            p.add("root", tile=tile, n=p.cc["fed"], rows=p.count("rows"), apply=True)

    def turned(which):
        def add(tile):
            if which == 1:
                return p.turns("merged", "x", KT, tile, rows=1 + tile)
            last = p.turns("merged", "x", KT, tile, fed=2 * which + 1 + tile)
            if tile:
                p.add("root", n=p.cc["fed"], scaled=p.count("scaled"))
            return last
        return add

    def ffn(name, which, t_x):
        return plan_ffn(p, name + "_w_gate", name + "_w_up", name + "_w_down", F2, None, t_x, 1.0, 0.5,
                        lambda tile: rms(which + 1, tile), turned(which + 1), scaled=p.cc["scaled"])

    for tile in range(R):
        rms(0, tile)
    t_x = ffn("ffn1", 0, p.start(turned(0), 3))

    def kept_rows(name, c0, dst, off, pair):
        c = p.chunk(("w_in", [(c0, c0 + 512)]), "x", KT, 512, pair, t_x)
        q[name] = p.add("keep_kv" if name == "akv" else "keep", c=c, dst=dst, off=off)

    def convolved(i, pair):
        c = p.chunk(("w_in", [(256 * i, 256 * i + 256)]), "x", KT, 256, pair, t_x, form="features")
        p.add("conv", c=c, i=i)
        q["conv", i] = c

    q = {}
    for i, (name, c0, dst, off) in enumerate([("aq0", 4104, "aqk", 0), ("aq1", 4616, "aqk", 512),
                                              ("akv", 5128, "aqk", 1024)]):
        kept_rows(name, c0, dst, off, (i + 1) % 2)
    c = p.chunk(("w_in", [(4096, 4104)]), "x", KT, 8, 0, t_x)
    p.add("m_log", c=c)
    p.add("p_split")
    p.add("a_norm", kept=(q["aq0"], q["aq1"], q["akv"]))

    before = p.begin()
    for i in range(4):
        for k in range(2):
            convolved(2 * i + k, k)
            if i or k:
                p.add("conv_silu", i=2 * i + k - 1, c=q["conv", 2 * i + k - 1])
        if i < 2:
            kept_rows(f"mv{i}", 2048 + 512 * i, "mv", 512 * i, 0)
        else:
            c = p.chunk(("w_in", [(3072 + 512 * (i - 2), 3584 + 512 * (i - 2))]), "x", KT, 512, 0, t_x)
            p.add("m_gate", c=c, j=i - 2, which="gt_a")
    p.add("conv_silu", i=7, c=q["conv", 7])
    gates2 = []
    for of, which, c0 in (("hm", "gt", 5640), ("ha", "gt_a", 6664)):
        for j in range(2):
            cg = p.chunk(("w_in", [(c0 + 512 * j, c0 + 512 * j + 512)]), "x", KT, 512, j, t_x)
            p.add("gate2", c=cg, of=of, which=which, j=j)
            gates2.append(cg)
    dense_a = p.begin()

    for r in range(R):
        p.pause(4)
        p.add("a_sum", tile=r)
    p.pause(9)
    for r in range(R):
        for half in range(3):
            t_a = p.next_t()
            p.add("a_turn", t=t_a, tile=r, half=half)
    tt = {}
    for i in range(AH + LAG + 1):
        if i < AH:
            p.add("aa_s", h=i, s=p.next_s(), after_t=t_a)
        if LAG <= i < AH + LAG:
            h = i - LAG
            tt[h] = p.next_t()
            p.add("probs_T", h=h, t=tt[h], of="aa", n=h + 1, slot=h % 4)
        if i > LAG:
            h = i - LAG - 1
            if h % 4 == 0:
                q["o"] = p.next_o()
            p.add("aa_pv", h=h, o=q["o"], t=tt[h], kept=q["akv"])
            if h % 4 == 3:
                p.add("aa_out", h=h, o=q["o"])
    p.pause(2)
    t_a2 = split_rows("aqk", "ha", KT, after_o=q["o"] + 1)

    for h in range(MH):
        p.add("m_arow", h=h, s=p.next_s())
    p.add("m_floor")
    for i in range(MH + 2):
        if i < MH:
            p.add("m_s", h=i, s=p.next_s())
        if 1 <= i <= MH:
            tt[i - 1] = p.next_t()
            p.add("probs_T", h=i - 1, t=tt[i - 1], of="m", n=MH + AH + i, slot=i - 1)
        if i >= 2:
            p.add("m_pv", h=i - 2, o=p.next_o(), t=tt[i - 2], kept=(q["mv0"], q["mv1"]))
    p.add("m_fin", rows=p.count("rows"))
    p.pause(8)
    t_m = split_rows("mo", "hm", KT, rows=p.cc["rows"])
    side = p.begin()
    for j in range(2):
        cp = p.chunk(("w_branch_a", [(512 * j, 512 * j + 512)]), "ha", KT, 512, j, t_a2)
        p.add("merge2", c=cp, gate=gates2[2 + j], which="gt_a", j=j, first=True)
    p.weave(before, dense_a + p.begin(), side)
    c = p.chunk(("w_branch_m", [(0, 512)]), "hm", KT, 512, 0, t_m)
    p.add("merge2", c=c, gate=gates2[0], which="gt", j=0, first=False)
    c = p.chunk(("w_branch_m", [(512, 1024)]), "hm", KT, 512, 1, t_m)
    done = p.cc["rows"] + 1
    t_g = p.tail(4, 2, lambda tile: p.add("merge2", c=c, gate=gates2[1], which="gt", j=1, first=False, tile=tile,
                                          early=0 if tile else p.early, rows=p.count("rows")),
                 lambda tile: p.turns("merged", "x", KT, tile, 0.5, rows=done + tile))
    c = p.chunk(("w_out", [(0, 512)]), "x", KT, 512, 0, t_g)
    p.add("resid", c=c, n=0, old=1.0, new=1.0)
    cw = p.chunk(("w_out", [(512, 1024)]), "x", KT, 512, 1, t_g)

    def rest(tile):
        p.add("resid", c=cw, n=1, old=1.0, new=1.0, tile=tile, early=0 if tile else p.early)
        rms(2, tile)

    t_x = p.tail(4, 1, rest, turned(2))
    t_p = ffn("ffn2", 2, t_x)
    for j in range(2):
        cg = p.chunk(("ple_gate_w", [(512 * j, 512 * j + 512)]), "x", KT, 512, 0, t_p)
        p.add("gate2", c=cg, which="gt", j=j, scaled=p.cc["scaled"])
        nth = p.next_d(1)
        u = p.unit(("ple_proj_w", [(512 * j, 512 * j + 512)]), "p", 0, PLE // P, 512, 1, nth, True, True, None)
        p.add("ple", c=Step(u=u, pair=1, nth=nth), gate=cg, which="gt", j=j)
    return p


class Memory:

    def __init__(self, nc, base, end):
        self.nc, self.base, self.end = nc, base, end

    def at(self, name, offset, shape, dt=F32):
        offset = (offset + 63) // 64 * 64
        size = int(np.prod(shape[1:])) * 4
        assert self.base + offset + size <= self.end, (name, self.base + offset + size - self.end)
        return self.nc.alloc_sbuf_tensor_at(name, list(shape), dt, offset=self.base + offset), offset + size


def build(nc, plan1, plan2, a):
    plans = [plan1, plan2]
    with ExitStack() as ctx:
        def sem(name):
            return ctx.enter_context(nc.semaphore(name))

        psum = [ctx.enter_context(nc.psum_tensor(f"bank{i}", [P, 512], F32)) for i in range(8)]
        DB, TB, SB, OB = psum[0:4], psum[4:6], psum[6], psum[7]

        w_loaded = [sem(f"w_loaded{i}") for i in range(NRAW)]
        x_loaded = sem("x_loaded")
        c_loaded = sem("c_loaded")
        stored = sem("stored")
        unit_done = sem("unit_done")
        hi_done = sem("hi_done")
        lo_done = sem("lo_done")
        d_done = [sem(f"d_done{i}") for i in range(4)]
        t_ready = [sem(f"t_ready{i}") for i in range(2)]
        t_hi = sem("t_hi")
        t_done = [sem(f"t_done{i}") for i in range(2)]
        s_ready = sem("s_ready")
        s_done = sem("s_done")
        o_ready = sem("o_ready")
        o_done = sem("o_done")
        rows = sem("rows")
        fed_left = sem("fed_left")
        fed = sem("fed")
        scaled = sem("scaled")
        gained = sem("gained")
        first_done = sem("first_done")
        roped = sem("roped")
        tanh_done = sem("tanh_done")
        maxed = sem("maxed")
        soft = sem("soft")
        mixed = sem("mixed")
        gates = sem("gates")
        silu = sem("silu")
        lam_dot = sem("lam_dot")
        lam_exp = sem("lam_exp")
        bias_up = sem("bias_up")
        p_ready = sem("p_ready")
        logs = sem("logs")
        spread_out = sem("spread_out")
        tapped = sem("tapped")
        conv_tanh = sem("conv_tanh")
        floored = sem("floored")
        rec_done = sem("rec_done")
        squared = sem("squared")
        summed = sem("summed")
        a_normed = sem("a_normed")
        sumsq = sem("sumsq")
        conv_out = sem("conv_out")
        p_emb = sem("p_emb")
        p_gain = [sem(f"p_gain{i}") for i in range(2)]
        p_conv = sem("p_conv")
        p_bias = sem("p_bias")
        p_vec = sem("p_vec")
        p_gate = sem("p_gate")
        p_norm = sem("p_norm")
        dve_chain = sem("dve_chain")
        act_chain = sem("act_chain")
        pool_chain = sem("pool_chain")
        first_cleared, last_cleared = unit_done.num, pool_chain.num

        fence = nc.alloc_sbuf_tensor("fence", [P, 16], F32)
        mem = Memory(nc, (nc.sbuf_base + 63) // 64 * 64, nc.sbuf_usable_end)
        o = 0
        raw, o = mem.at("raw", o, [P, NRAW, UNIT])
        wh, o = mem.at("wh", o, [P, NS, UNIT], F32R)
        wl, o = mem.at("wl", o, [P, NS, UNIT], F32R)
        xh, o = mem.at("xh", o, [P, KT, S], F32R)
        xl, o = mem.at("xl", o, [P, KT, S], F32R)
        x, o = mem.at("x", o, [P, R, D])
        ident, o = mem.at("ident", o, [P, P])
        scr, o = mem.at("scr", o, [P, 256])
        bst, o = mem.at("bst", o, [P, R, 2, 6])
        bmv, o = mem.at("bmv", o, [P, R, 2])

        b = {}
        def buf(name, shape, dt=F32, at=None):
            nonlocal o
            if at is None:
                b[name], o = mem.at(name, o, shape, dt)
            else:
                b[name], end = mem.at(name, at, shape, dt)
                return end

        q0 = o
        for n in ("rq", "rk"):
            buf(n, [P, R, 512])
        buf("rv", [P, R, D])
        buf("rg", [P, R, D])
        c0 = o
        for n in ("cq", "ck", "cv"):
            buf(n, [P, R, 512])
        e0 = o
        for n in ("dq", "dk", "dv"):
            buf(n, [P, R, 512])
        buf("ret_o", [P, R, D], at=q0)
        end = buf("oa_h", [P, KT, S], F32R, at=q0)
        buf("oa_l", [P, KT, S], F32R, at=end)
        buf("gt_c", [P, 2, R, 512], at=q0)
        end = buf("ob_h", [P, 4, S], F32R, at=c0 + 4096)
        buf("ob_l", [P, 4, S], F32R, at=end)
        end = buf("oc_h", [P, 4, S], F32R, at=e0 + 4096)
        buf("oc_l", [P, 4, S], F32R, at=end)
        end = buf("act_h", [P, 22, S], F32R, at=q0)
        buf("act_l", [P, 22, S], F32R, at=end)
        buf("qT", [P, 4, S])
        buf("kT", [P, 4, S])
        buf("Pn", [P, 4, 384])
        buf("PT", [P, 2, 384])
        buf("bias", [P, CH, S])
        buf("decay", [P, RH, 384])
        buf("rope", [P, R, 2, 96])
        buf("dmask", [P, S])
        buf("b_merge", [P, 3 * D])
        buf("ln", [P, 2, D])
        buf("vec", [P, 256 + 128 + 256 + 2])
        buf("rs", [P, 4, 256])
        buf("merged", [P, R, D])
        g0 = o
        buf("gt", [P, 2, R, 512])
        end = buf("ffn_s", [P, 2, R, 256], at=g0)
        buf("ffn_a", [P, 2, R, 256], at=end)
        buf("junk", [P, 256])
        o1, o = o, q0
        buf("mT", [P, 16, S])
        buf("mv", [P, R, D])
        buf("mo", [P, R, D])
        buf("aqk", [P, R, 1280])
        buf("av", [P, R, 256])
        end = buf("hm_h", [P, KT, S], F32R, at=q0)
        buf("hm_l", [P, KT, S], F32R, at=end)
        end = buf("ha_h", [P, KT, S], F32R, at=o)
        buf("ha_l", [P, KT, S], F32R, at=end)
        buf("akd", [P, R, AKV, 2, ADH])
        buf("sq", [P, 1280], at=o)
        buf("aqT", [P, 8, S])
        buf("akT", [P, AKV, S])
        m_o0 = o
        buf("m_o", [P, R, D])
        end = buf("ib", [P, R, MH, P], at=m_o0)
        buf("lfb", [P, R, MH, P], at=end)
        buf("Pn2", [P, 4, 384])
        buf("PT2", [P, 2, 384])
        g0 = o
        buf("gt2", [P, 2, R, 512])
        buf("gt_a", [P, 2, R, 512])
        end = buf("ffn_s2", [P, 2, R, 256], at=g0)
        buf("ffn_a2", [P, 2, R, 256], at=end)
        buf("merged2", [P, R, D])
        buf("gain", [P, 2, D])
        buf("vec2", [P, 64 + 64 + 16 + 8])
        buf("convw", [P, 16, CONV_K + 1])
        buf("p_raw", [P, 2, S])
        buf("p_h", [P, 2, S], F32R)
        buf("p_l", [P, 2, S], F32R)
        buf("masks", [P, 3, S])
        buf("junk2", [P, 256])
        buf("sc2", [P, 384])
        b["act2_h"], b["act2_l"] = b["act_h"], b["act_l"]
        sc2 = b["sc2"]
        ifv, absf, lnf, lf = sc2[:, 0:16], sc2[:, 16:24], sc2[:, 24:32], sc2[:, 32:40]
        mx2, nmx2, sm2 = sc2[:, 40:72], sc2[:, 72:104], sc2[:, 104:136]
        nb, fl, den, rec2, ss2 = sc2[:, 136:144], sc2[:, 144:152], sc2[:, 152:160], sc2[:, 160:168], sc2[:, 168:176]
        root = sc2[:, 264:268]
        es, ssq, rq2 = sc2[:, 176:184], sc2[:, 184:224], sc2[:, 224:264]
        ss, nmx, mx, sm = scr[:, 0:16], scr[:, 16:32], scr[:, 32:48], scr[:, 48:64]
        rc, c1, v, y, tn = scr[:, 64:80], scr[:, 80:84], scr[:, 84:124], scr[:, 124:164], scr[:, 164:204]
        lamv = scr[:, 204:212]

        split_of = {"x": (xh, xl), "oa": (b["oa_h"], b["oa_l"]), "ob": (b["ob_h"], b["ob_l"]),
                    "oc": (b["oc_h"], b["oc_l"]), "act": (b["act_h"], b["act_l"]), "hm": (b["hm_h"], b["hm_l"]),
                    "ha": (b["ha_h"], b["ha_l"]), "p": (b["p_h"], b["p_l"])}
        b["x"] = x
        LAMBDA_DOT, G_RET, G_DA, LAM_INIT = 384, 0, 256, 640

        def slot_counts(u_total):
            return [-(-(u_total - s) // NRAW) for s in range(NRAW)]

        cnt = [slot_counts(len(p.units)) for p in plans]
        slot_base = [[0] * NRAW, [DEPTH * c for c in cnt[0]]]
        unit_base = [0, DEPTH * len(plan1.units)]

        with nc.Block() as block:
            @block.sync
            def _(sp):
                sp.dma_start(x[:, :, :], a["x"].rearrange("(r p) d -> p r d", p=P)).then_inc(x_loaded, 16)
                for u in range(NRAW):
                    sp.dma_start(raw[:, u, :], a["weights"][u]).then_inc(w_loaded[u], 16)

            @block.scalar
            def _(act):
                act.dma_start(ident[:, :], a["ident"]).then_inc(x_loaded, 16)
                act.dma_start(b["decay"][:, :, :], a["decay"]).then_inc(c_loaded, 16)
                act.dma_start(b["rope"][:, :, :, :], a["rope"]).then_inc(c_loaded, 16)
                act.dma_start(b["dmask"][:, :], a["dmask"]).then_inc(c_loaded, 16)

        for block_no, plan in enumerate(plans):
            if not plan.steps:
                continue
            if block_no == 1:
                for name in ("Pn", "PT", "gt", "ffn_s", "ffn_a", "merged"):
                    b[name] = b[name + "2"]
            steps, U = plan.steps, len(plan.units)
            with nc.Fori(0, DEPTH) as layer:
                with nc.Block() as block:
                    @block.sync
                    def _(sp):
                        def row(name):
                            return a[name][bass.ds(layer, 1)].rearrange("o p n -> p (o n)")

                        if block_no == 1:
                            sp.dma_start(b["gain"][:, 0, :], row("gain_ffn1")).then_inc(p_gain[0], 16)
                            sp.dma_start(b["gain"][:, 1, :], row("gain_mix")).then_inc(p_gain[1], 16)
                            sp.dma_start(b["vec2"][:, :], row("vec2")).then_inc(p_vec, 16)
                            sp.dma_start(b["convw"][:, :, :].rearrange("p c k -> p (c k)"), row("convw")).then_inc(p_conv, 16)
                            sp.dma_start(b["p_raw"][:, :, :].rearrange("p c k -> p (c k)"), row("p")).then_inc(p_emb, 16)
                            sp.dma_start(b["masks"][:, :, :], a["masks"]).then_inc(p_bias, 16)
                        else:
                            sp.dma_start(b["vec"][:, :], row("vec")).then_inc(p_vec, 16)
                            sp.dma_start(b["bias"][:, :, :].rearrange("p h n -> p (h n)"), row("bias")).then_inc(p_bias, 16)
                            sp.dma_start(b["b_merge"][:, :], row("b_merge")).then_inc(p_gate, 16)
                            sp.dma_start(b["ln"][:, :, :].rearrange("p h n -> p (h n)"), row("ln1")).then_inc(p_norm, 16)
                        for u in range(NRAW, U + NRAW):
                            w = u - NRAW if u < U else NRAW * ((U - 1 - (u - U)) // NRAW) + (u - U)
                            slot = u % NRAW if u < U else u - U
                            sp.wait_ge(lo_done, w + 1)
                            at = unit_base[block_no] + layer * U + u
                            sp.dma_start(raw[:, slot, :],
                                         a["weights"][bass.ds(at, 1)].rearrange("o p n -> p (o n)"))\
                              .then_inc(w_loaded[slot], 16)

                    @block.gpsimd
                    def _(pool):
                        chain = [0]

                        def link(ins):
                            chain[0] += 1
                            ins.then_inc(pool_chain, 1)
                            pool.wait_ge(pool_chain, chain[0])

                        if block_no == 0:
                            pool.wait_ge(p_bias, 16)
                            link(pool.tensor_scalar(b["bias"][:, :, :], b["bias"][:, :, :], CDH ** 0.5, None, ALU.mult))
                            pool.memset(b["bias"][0:CHUNK, :, 192:256], NEG * CDH ** 0.5).then_inc(bias_up, 1)
                        for st in steps:
                            if st.kind == "rope":
                                c = st.of.c
                                pool.wait_ge(c_loaded, 48)
                                if st.n > 1:
                                    pool.wait_ge(roped, st.n - 1)
                                for r in range(R):
                                    pool.wait_ge(d_done[2 * c.pair + r], c.nth + 1)
                                    t = b[st.src][:, r, :].rearrange("p (h a k) -> p h a k", h=st.heads, a=2)
                                    k = st.half
                                    lo = 0 if st.table == "ret" else RDK // 2
                                    cs = [b["rope"][:, r, i, lo:lo + k].unsqueeze(1).broadcast_to([P, st.heads, k])
                                          for i in range(2)]
                                    sc = [b["rs"][:, i, :].rearrange("p (h k) -> p h k", h=st.heads) for i in range(4)]
                                    x1, x2 = t[:, :, 0, :], t[:, :, 1, :]
                                    pool.tensor_tensor(sc[0], x1, cs[0], ALU.mult)
                                    pool.tensor_tensor(sc[1], x2, cs[1], ALU.mult)
                                    pool.tensor_tensor(sc[2], x2, cs[0], ALU.mult)
                                    link(pool.tensor_tensor(sc[3], x1, cs[1], ALU.mult))
                                    link(pool.tensor_tensor(x1, sc[0], sc[1], ALU.subtract))
                                    last = pool.tensor_tensor(x2, sc[2], sc[3], ALU.add)
                                    if r == R - 1:
                                        last.then_inc(roped, 1)
                                    else:
                                        link(last)
                            elif st.kind == "norm":
                                pool.wait_ge(gained, st.n)
                                xs = x[:, st.tile, HALF:D]
                                pool.tensor_tensor(xs, xs, b["ln"][:, 1, HALF:D], ALU.add).then_inc(fed, 1)
                            elif st.kind == "rms":
                                r = st.tile
                                slot, count = GAIN[st.which]
                                pool.wait_ge(p_gain[slot], 16 * count)
                                if st.which:
                                    for j in range(2):
                                        pool.wait_ge(d_done[2 * j + r], st.last_chunks[j] + 1)
                                pool.tensor_tensor(b["merged"][:, r, HALF:D], x[:, r, HALF:D], b["gain"][:, slot, HALF:D], ALU.mult)\
                                    .then_inc(fed, 1)
                            elif st.kind == "m_log":
                                pool.wait_ge(logs, 4)
                                iv, lv = ifv.rearrange("p (r g) -> p r g", r=R), lf.rearrange("p (r h) -> p r h", r=R)
                                pool.tensor_copy(b["ib"][:, :, :, :], iv[:, :, 0:MH].unsqueeze(3).broadcast_to([P, R, MH, P]))\
                                    .then_inc(spread_out, 1)
                                pool.tensor_copy(b["lfb"][:, :, :, :], lv.unsqueeze(3).broadcast_to([P, R, MH, P]))\
                                    .then_inc(spread_out, 1)
                            elif st.kind == "a_norm":
                                for kept in st.kept:
                                    for r in range(R):
                                        pool.wait_ge(d_done[2 * kept.c.pair + r], kept.c.nth + 1)
                                for r in range(R):
                                    if r:
                                        pool.wait_ge(summed, r)
                                    pool.tensor_tensor(b["sq"][:, :], b["aqk"][:, r, :], b["aqk"][:, r, :], ALU.mult)\
                                        .then_inc(squared, 1)
                                pool.wait_ge(summed, R + 1)
                                pool.wait_ge(p_vec, 16)
                                for r in range(R):
                                    t = b["aqk"][:, r, :].rearrange("p (h k) -> p h k", h=AH + AKV)
                                    link(pool.tensor_tensor(t, t, rq2[:, 20 * r:20 * r + 20].unsqueeze(2)
                                                            .broadcast_to([P, AH + AKV, ADH]), ALU.mult))
                                    pool.tensor_tensor(t[:, 0:AH, :], t[:, 0:AH, :], b["vec2"][:, 0:ADH].unsqueeze(1)
                                                       .broadcast_to([P, AH, ADH]), ALU.mult)
                                    for i in range(2):
                                        last = pool.tensor_tensor(b["akd"][:, r, :, i, :], t[:, AH:, :], b["vec2"][:, ADH:2 * ADH]
                                                                  .unsqueeze(1).broadcast_to([P, AKV, ADH]), ALU.mult)
                                    last.then_inc(a_normed, 1)

                    @block.scalar
                    def _(act):
                        chain = [0]

                        def link(ins):
                            chain[0] += 1
                            ins.then_inc(act_chain, 1)
                            act.wait_ge(act_chain, chain[0])

                        def split_high(u):
                            used = plan.units[u][2] * plan.units[u][3]
                            s = u % NRAW
                            act.wait_ge(w_loaded[s], 16 * (slot_base[block_no][s] + u // NRAW + 1) + layer * (16 * cnt[block_no][s]))
                            act.activation(wh[:, u % NS, 0:used], raw[:, s, 0:used], ACT.Copy).then_inc(hi_done, 1)

                        def row(name):
                            return a[name][bass.ds(layer, 1)].rearrange("o p n -> p (o n)")

                        split_high(0)
                        high = 1
                        for st in steps:
                            k = st.kind
                            if k == "first_tile":
                                if high <= st.end:
                                    split_high(high)
                                    high += 1
                            elif k == "unit":
                                if st.u + NS < U:
                                    act.wait_ge(unit_done, st.u + 1)
                                    split_high(high)
                                    high += 1
                            elif k == "split":
                                act.wait_ge(t_ready[st.t % 2], st.t // 2 + 1)
                                act.activation(split_of[st.dst][0][:, st.kg:st.kg + 4, st.tile * P:st.tile * P + P],
                                               TB[st.t % 2][:, :].rearrange("p (k n) -> p k n", k=4), ACT.Copy,
                                               scale=st.scale).then_inc(t_hi, 1)
                            elif k == "split_act":
                                act.wait_ge(t_ready[st.t % 2], st.t // 2 + 1)
                                act.activation(b["act_h"][:, 2 * st.i:2 * st.i + 2, :],
                                               TB[st.t % 2][:, :].rearrange("p (k n) -> p k n", k=2), ACT.Copy)\
                                   .then_inc(t_hi, 1)
                            elif k == "keep":
                                act.wait_ge(unit_done, st.c.u + 1)
                                for r in range(R):
                                    act.activation(b[st.dst][:, r, st.off:st.off + 512], DB[2 * st.c.pair + r][:, :],
                                                   ACT.Copy).then_inc(d_done[2 * st.c.pair + r], 1)
                            elif k == "turn":
                                act.wait_ge(t_ready[st.t % 2], st.t // 2 + 1)
                                act.activation(b[st.dst][:, :, st.tile * P:st.tile * P + P],
                                               TB[st.t % 2][:, :].rearrange("p (k n) -> p k n", k=4), ACT.Copy)\
                                   .then_inc(t_done[st.t % 2], 1)
                            elif k == "ret_gate":
                                act.wait_ge(unit_done, st.c.u + 1)
                                for r in range(R):
                                    act.activation(b["gt"][:, st.j, r, :], DB[2 * st.c.pair + r][:, :], ACT.Tanh,
                                                   scale=0.5).then_inc(tanh_done, 1)
                            elif k == "ret_pv":
                                act.wait_ge(o_ready, st.o + 1)
                                for r in range(R):
                                    link(act.activation(b["junk"][:, :], OB[:, r * RDV:(r + 1) * RDV], ACT.Square,
                                                        accum_out=ss[:, 2 * st.h + r:2 * st.h + r + 1]))
                                act.activation(b["ret_o"][:, :, st.h * RDV:(st.h + 1) * RDV],
                                               OB[:, :].rearrange("p (r n) -> p r n", r=R), ACT.Copy).then_inc(o_done, 1)
                            elif k == "da_pv":
                                act.wait_ge(o_ready, st.o + 1)
                                for r in range(R):
                                    link(act.activation(b["junk"][:, 0:P], OB[:, r * P:(r + 1) * P], ACT.Square,
                                                        accum_out=ss[:, 2 * st.h + r:2 * st.h + r + 1]))
                                act.activation(b["dq"][:, :, st.h * P:(st.h + 1) * P],
                                               OB[:, 0:2 * P].rearrange("p (r n) -> p r n", r=R), ACT.Copy).then_inc(o_done, 1)
                            elif k in ("ca_s", "da_s"):
                                n = st.h if k == "ca_s" else st.g
                                act.wait_ge(maxed, n + 1 + (CH if k == "da_s" else 0))
                                for r in (1, 0):
                                    part = b["Pn"][:, n % 4, 0:256] if r else b["Pn"][:, n % 4, 256:384]
                                    at = r * CH + n if k == "ca_s" else 2 * n + r
                                    last = act.activation(part, part, ACT.Exp, bias=nmx[:, 2 * (n % 8) + r:2 * (n % 8) + r + 1],
                                                          accum_out=sm[:, at:at + 1])
                                last.then_inc(soft, 1)
                            elif k == "probs_T":
                                act.wait_ge(t_ready[st.t % 2], st.t // 2 + 1)
                                act.activation(b["PT"][:, st.h % 2, :], TB[st.t % 2][:, 0:384], ACT.Copy)\
                                   .then_inc(t_done[st.t % 2], 1)
                            elif k == "norm" and st.which == 0 and st.tile == 1:
                                act.wait_ge(fed, st.n)
                                act.wait_ge(fed_left, st.n)
                                act.dma_start(b["ln"][:, :, :].rearrange("p h n -> p (h n)"), row("ln2")).then_inc(p_norm, 16)
                            elif k == "lambda":
                                act.wait_ge(lam_dot, 1)
                                act.activation(lamv[:, 2:4], lamv[:, 0:2], ACT.Exp).then_inc(lam_exp, 1)
                            elif k == "gate":
                                for r in range(R):
                                    act.wait_ge(d_done[2 * st.c.pair + r], st.c.nth + 1)
                                g = b["gt_c" if st.b == 2 else "gt"][:, st.j, :, :]
                                act.activation(g, g, ACT.Tanh, scale=0.5).then_inc(gates, 1)
                            elif k == "rms":
                                r = st.tile
                                if st.which:
                                    for j in range(2):
                                        act.wait_ge(d_done[2 * j + r], st.last_chunks[j] + 1)
                                act.activation(b["m_o"][:, r, :], x[:, r, :], ACT.Square, accum_out=ss2[:, r:r + 1])\
                                   .then_inc(sumsq, 1)
                                if st.which < 3 and r == 1:
                                    act.wait_ge(fed, st.n)
                                    act.wait_ge(fed_left, st.n)
                                    if st.which == 0:
                                        act.dma_start(b["gain"][:, 0, :], row("gain_m")).then_inc(p_gain[0], 16)
                                    elif st.which == 1:
                                        act.dma_start(b["gain"][:, 1, :], row("gain_ple")).then_inc(p_gain[1], 16)
                            elif k == "p_split":
                                act.wait_ge(p_emb, 16)
                                act.activation(b["p_h"][:, :, :], b["p_raw"][:, :, :], ACT.Copy).then_inc(p_ready, 1)
                            elif k == "m_log":
                                act.wait_ge(logs, 1)
                                act.activation(lnf, absf, ACT.Exp, scale=-1.0).then_inc(logs, 1)
                                act.wait_ge(logs, 2)
                                act.activation(lnf, lnf, ACT.Ln, bias=1.0).then_inc(logs, 1)
                            elif k == "conv":
                                act.wait_ge(unit_done, st.c.u + 1)
                                act.wait_ge(p_conv, 16)
                                for ct in range(2):
                                    c = 2 * st.i + ct
                                    w = b["convw"][:, c, :]
                                    act.activation(b["mT"][:, c, :], DB[2 * st.c.pair + ct][:, 0:S], ACT.Identity,
                                                   scale=w[:, 3:4], bias=w[:, 4:5]).then_inc(tapped, 1)
                            elif k == "conv_silu":
                                for ct in range(2):
                                    act.wait_ge(d_done[2 * st.c.pair + ct], st.c.nth + 1)
                                act.activation(b["gt"][:, st.i % 2, :, 0:256], b["mT"][:, 2 * st.i:2 * st.i + 2, :], ACT.Tanh,
                                               scale=0.5).then_inc(conv_tanh, 1)
                            elif k == "keep_kv":
                                act.wait_ge(unit_done, st.c.u + 1)
                                for r in range(R):
                                    bank = DB[2 * st.c.pair + r]
                                    link(act.activation(b["aqk"][:, r, 1024:1280], bank[:, 0:256], ACT.Copy))
                                    act.activation(b["av"][:, r, :], bank[:, 256:512], ACT.Copy)\
                                       .then_inc(d_done[2 * st.c.pair + r], 1)
                            elif k == "m_gate" or k == "gate2":
                                act.wait_ge(unit_done, st.c.u + 1)
                                if st.scaled:
                                    act.wait_ge(scaled, st.scaled)
                                if st.of == "hm":
                                    act.wait_ge(conv_out, 8)
                                for r in range(R):
                                    act.activation(b[st.which][:, st.j, r, :], DB[2 * st.c.pair + r][:, :], ACT.Tanh,
                                                   scale=root[:, 2 + r:3 + r] if st.scaled else 0.5).then_inc(d_done[2 * st.c.pair + r], 1)
                            elif k == "m_arow":
                                act.wait_ge(maxed, AH + st.h + 1)
                                for r in (1, 0):
                                    part = b["Pn"][:, st.h, 0:256] if r else b["Pn"][:, st.h, 256:384]
                                    last = act.activation(part, part, ACT.Exp, bias=nmx2[:, 4 * r + st.h:4 * r + st.h + 1])
                                last.then_inc(soft, 1)
                            elif k == "m_floor":
                                act.wait_ge(floored, 1)
                                act.activation(fl, fl, ACT.Exp).then_inc(floored, 1)
                            elif k == "m_pv":
                                act.wait_ge(o_ready, st.o + 1)
                                act.wait_ge(rec_done, st.h + 1)
                                for r in range(R):
                                    scale = rec2[:, 4 * r + st.h:4 * r + st.h + 1]
                                    link(act.activation(b["junk2"][:, :], OB[:, r * MDH:(r + 1) * MDH], ACT.Square, scale=scale,
                                                        accum_out=ss2[:, 2 * st.h + r:2 * st.h + r + 1]))
                                for r in range(R):
                                    scale = rec2[:, 4 * r + st.h:4 * r + st.h + 1]
                                    last = act.activation(b["m_o"][:, r, st.h * MDH:(st.h + 1) * MDH],
                                                          OB[:, r * MDH:(r + 1) * MDH], ACT.Identity, scale=scale)
                                last.then_inc(o_done, 1)
                            elif k == "m_fin":
                                act.wait_ge(rows, st.rows)
                                act.dma_start(b["gain"][:, 0, :], row("gain_ffn2")).then_inc(p_gain[0], 16)
                            elif k == "a_turn":
                                act.wait_ge(t_ready[st.t % 2], st.t // 2 + 1)
                                dst = b["akT"][:, :, :] if st.half == 2 else b["aqT"][:, 4 * st.half:4 * st.half + 4, :]
                                act.activation(dst[:, :, st.tile * P:st.tile * P + P],
                                               TB[st.t % 2][:, :].rearrange("p (k n) -> p k n", k=4), ACT.Copy)\
                                   .then_inc(t_done[st.t % 2], 1)
                            elif k == "aa_s":
                                act.wait_ge(maxed, st.h + 1)
                                for r in (1, 0):
                                    part = b["Pn"][:, st.h % 4, 0:256] if r else b["Pn"][:, st.h % 4, 256:384]
                                    at = 16 * r + st.h
                                    last = act.activation(part, part, ACT.Exp, bias=nmx2[:, at:at + 1],
                                                          accum_out=sm2[:, at:at + 1])
                                if st.h % 4 == 3:
                                    last = act.activation(es, es, ACT.Exp)
                                last.then_inc(soft, 1)
                            elif k == "swiglu":
                                act.wait_ge(unit_done, st.c.u + 1)
                                if st.scaled:
                                    act.wait_ge(scaled, st.scaled)
                                for r in range(R):
                                    act.activation(b["ffn_s"][:, st.i % 2, r, 0:st.width], DB[2 * st.c.pair + r][:, 0:st.width],
                                                   ACT.Silu, scale=root[:, r:r + 1] if st.scaled else 1.0).then_inc(silu, 1)

                    @block.vector
                    def _(dve):
                        chain = [0]

                        def link(ins):
                            chain[0] += 1
                            ins.then_inc(dve_chain, 1)
                            dve.wait_ge(dve_chain, chain[0])

                        def split_low(u):
                            used = plan.units[u][2] * plan.units[u][3]
                            dve.wait_ge(hi_done, u + 1)
                            dve.tensor_tensor(wl[:, u % NS, 0:used], raw[:, u % NRAW, 0:used],
                                              wh[:, u % NS, 0:used].bitcast(F32), ALU.subtract).then_inc(lo_done, 1)

                        def rsqrt(n, x_in, scale, eps, out=None):
                            vv, yy, tt = v[:, 0:n], y[:, 0:n], tn[:, 0:n]
                            link(dve.tensor_scalar(vv, x_in, scale, eps, ALU.mult, ALU.add))
                            link(dve.tensor_scalar(yy.bitcast(I32), vv.bitcast(I32), 1, None, ALU.arith_shift_right))
                            link(dve.tensor_scalar(yy.bitcast(I32), yy.bitcast(I32), -1.0, float(0x5f3759df),
                                                   ALU.mult, ALU.add))
                            factor = 1.0
                            for _ in range(3):
                                if n == 1:
                                    link(dve.scalar_tensor_tensor(tt, yy, vv, yy, ALU.mult, ALU.mult))
                                else:
                                    link(dve.tensor_tensor(tt, yy, yy, ALU.mult))
                                    link(dve.tensor_tensor(tt, tt, vv, ALU.mult))
                                link(dve.scalar_tensor_tensor(yy, tt, -3.0 * factor * factor, yy, ALU.add, ALU.mult))
                                factor *= -2.0 * factor * factor
                            out = yy if out is None else out
                            link(dve.tensor_scalar(out, yy, 1.0 / factor, None, ALU.mult))
                            return out

                        split_low(0)
                        low = 1
                        for st in steps:
                            k = st.kind
                            if k == "first_tile":
                                if low <= st.end:
                                    split_low(low)
                                    low += 1
                            elif k == "unit":
                                if low < min(st.u + NS, U):
                                    split_low(low)
                                    low += 1
                            elif k in ("split", "split_act"):
                                dve.wait_ge(t_hi, st.n)
                                bank = TB[st.t % 2][:, :].rearrange("p (k n) -> p k n", k=4 if k == "split" else 2)
                                if k == "split":
                                    h, lo = [w[:, st.kg:st.kg + 4, st.tile * P:st.tile * P + P] for w in split_of[st.dst]]
                                else:
                                    h, lo = [w[:, 2 * st.i:2 * st.i + 2, :] for w in split_of["act"]]
                                if k == "split" and st.scale != 1.0:
                                    ins = dve.scalar_tensor_tensor(lo, bank, st.scale, h.bitcast(F32), ALU.mult, ALU.subtract)
                                else:
                                    ins = dve.tensor_tensor(lo, bank, h.bitcast(F32), ALU.subtract)
                                ins.then_inc(t_done[st.t % 2], 1)
                            elif k == "lambda":
                                dve.wait_ge(p_vec, 16)
                                for i in range(2):
                                    at = LAMBDA_DOT + 128 * i
                                    last = dve.tensor_tensor_reduce(b["junk"][:, 64 * i:64 * i + 64], b["vec"][:, at:at + 64],
                                                                    b["vec"][:, at + 64:at + 128], 1.0, 0.0, ALU.mult,
                                                                    ALU.add, lamv[:, i:i + 1])
                                last.then_inc(lam_dot, 1)
                                dve.wait_ge(lam_exp, 1)
                                link(dve.scalar_tensor_tensor(lamv[:, 4:5], lamv[:, 2:3], lamv[:, 3:4],
                                                              b["vec"][:, LAM_INIT:LAM_INIT + 1], ALU.subtract, ALU.add))
                            elif k == "ret_gate":
                                for r in range(R):
                                    bank = 2 * st.c.pair + r
                                    dve.wait_ge(tanh_done, 2 * st.j + r + 1)
                                    dst = b["rg"][:, r, st.j * 512:(st.j + 1) * 512]
                                    dve.scalar_tensor_tensor(dst, b["gt"][:, st.j, r, :], 1.0, DB[bank][:, :], ALU.add,
                                                             ALU.mult).then_inc(d_done[bank], 1)
                                    dve.wait_ge(d_done[bank], st.c.nth + 1)
                                    d3 = dst.rearrange("p (h n) -> p h n", h=2)
                                    link(dve.tensor_tensor(d3, d3, b["vec"][:, G_RET:G_RET + RDV].unsqueeze(1)
                                                           .broadcast_to([P, 2, RDV]), ALU.mult))
                            elif k == "ret_s":
                                dve.wait_ge(s_ready, st.s + 1)
                                dve.wait_ge(c_loaded, 48)
                                dve.tensor_tensor(b["Pn"][:, st.h % 4, :], SB[:, 0:384], b["decay"][:, st.h, :], ALU.mult)\
                                   .then_inc(s_done, 1)
                            elif k == "ret_fin":
                                dve.wait_ge(o_done, st.o + 1)
                                rs = rsqrt(8, ss[:, 0:8], 1.0 / RDV, LN_EPS)
                                link(dve.tensor_scalar(rs, rs, 0.5, None, ALU.mult))
                                for h in range(RH):
                                    for r in range(R):
                                        part = b["rg"][:, r, h * RDV:(h + 1) * RDV]
                                        last = dve.scalar_tensor_tensor(part, b["ret_o"][:, r, h * RDV:(h + 1) * RDV],
                                                                        rs[:, 2 * h + r:2 * h + r + 1], part,
                                                                        ALU.mult, ALU.mult)
                                last.then_inc(rows, 1)
                            elif k in ("ca_s", "da_s"):
                                n = st.h if k == "ca_s" else st.g
                                dve.wait_ge(s_ready, st.s + 1)
                                if k == "ca_s":
                                    dve.wait_ge(bias_up, 1)
                                add = b["bias"][:, n, :] if k == "ca_s" else b["dmask"][:, :]
                                dve.tensor_tensor_reduce(b["Pn"][:, n % 4, 0:256], SB[:, 0:256], add, 0.125, -3e38,
                                                         ALU.add, ALU.max, mx[:, 2 * (n % 8) + 1:2 * (n % 8) + 2])
                                dve.tensor_tensor_reduce(b["Pn"][:, n % 4, 256:384], SB[:, 256:384], add[:, 128:256],
                                                         0.125, -3e38, ALU.add, ALU.max, mx[:, 2 * (n % 8):2 * (n % 8) + 1])\
                                   .then_inc(s_done, 1)
                                dve.wait_ge(s_done, st.s + 1)
                                dve.tensor_scalar(nmx[:, 2 * (n % 8):2 * (n % 8) + 2], mx[:, 2 * (n % 8):2 * (n % 8) + 2],
                                                  -1.0, None, ALU.mult).then_inc(maxed, 1)
                            elif k == "ca_out":
                                dve.wait_ge(o_ready, st.o + 1)
                                g = st.h // 4
                                for r in range(R):
                                    link(dve.reciprocal(rc[:, 4 * r:4 * r + 4], sm[:, r * CH + 4 * g:r * CH + 4 * g + 4]))
                                for r in range(R):
                                    dst = b["cq"][:, r, 256 * g:256 * g + 256].rearrange("p (h n) -> p h n", h=4)
                                    last = dve.tensor_tensor(dst, OB[:, 256 * r:256 * r + 256].rearrange("p (h n) -> p h n", h=4),
                                                             rc[:, 4 * r:4 * r + 4].unsqueeze(2).broadcast_to([P, 4, CDH]),
                                                             ALU.mult)
                                last.then_inc(o_done, 1)
                            elif k == "da_mix":
                                dve.wait_ge(soft, CH + 2 * st.h + 2)
                                if st.n > 1:
                                    dve.wait_ge(mixed, st.n - 1)
                                link(dve.reciprocal(rc[:, 0:4], sm[:, 4 * st.h:4 * st.h + 4]))
                                link(dve.tensor_scalar(c1[:, 0:2], rc[:, 2:4], lamv[:, 4:5], None, ALU.mult))
                                s0, s1 = (2 * st.h) % 4, (2 * st.h + 1) % 4
                                for r in range(R):
                                    cols = slice(0, 256) if r else slice(256, 384)
                                    link(dve.tensor_scalar(b["Pn"][:, s1, cols], b["Pn"][:, s1, cols], c1[:, r:r + 1], None,
                                                           ALU.mult))
                                    last = dve.scalar_tensor_tensor(b["Pn"][:, s0, cols], b["Pn"][:, s0, cols],
                                                                    rc[:, r:r + 1], b["Pn"][:, s1, cols], ALU.mult,
                                                                    ALU.subtract)
                                last.then_inc(mixed, 1)
                            elif k == "da_fin":
                                dve.wait_ge(o_done, st.o + 1)
                                rs = rsqrt(8, ss[:, 0:8], 1.0 / P, LN_EPS)
                                link(dve.tensor_scalar(rs, rs, b["vec"][:, LAM_INIT + 1:LAM_INIT + 2], None, ALU.mult))
                                for h in range(DH):
                                    for r in range(R):
                                        part = b["dq"][:, r, h * P:(h + 1) * P]
                                        last = dve.scalar_tensor_tensor(part, part, rs[:, 2 * h + r:2 * h + r + 1],
                                                                        b["vec"][:, G_DA:G_DA + P], ALU.mult, ALU.mult)
                                last.then_inc(rows, 1)
                            elif k == "gate":
                                dve.wait_ge(unit_done, st.c.u + 1)
                                dve.wait_ge(p_gate, 16)
                                at = st.b * D + st.j * 512
                                for r in range(R):
                                    bank = 2 * st.c.pair + r
                                    dve.tensor_tensor(b["gt_c" if st.b == 2 else "gt"][:, st.j, r, :], DB[bank][:, :], b["b_merge"][:, at:at + 512],
                                                      ALU.add).then_inc(d_done[bank], 1)
                            elif k == "merge":
                                if st.early:
                                    dve.wait_ge(first_done, st.early)
                                else:
                                    dve.wait_ge(unit_done, st.c.u + 1)
                                dve.wait_ge(gates, st.n)
                                for r in range(R) if st.tile is None else (st.tile,):
                                    bank = 2 * st.c.pair + r
                                    g = b["gt_c" if st.b == 2 else "gt"][:, st.j, r, :]
                                    m = b["merged"][:, r, st.j * 512:(st.j + 1) * 512]
                                    dve.scalar_tensor_tensor(m if st.b == 0 else g, g, 1.0, DB[bank][:, :], ALU.add,
                                                             ALU.mult).then_inc(d_done[bank], 1)
                                    if st.b:
                                        dve.wait_ge(d_done[bank], st.c.nth + 1)
                                        last = dve.tensor_tensor(m, m, g, ALU.add)
                                        if st.rows:
                                            last.then_inc(rows, 1)
                            elif k == "resid":
                                if st.early:
                                    dve.wait_ge(first_done, st.early)
                                else:
                                    dve.wait_ge(unit_done, st.c.u + 1)
                                for r in range(R) if st.tile is None else (st.tile,):
                                    bank = 2 * st.c.pair + r
                                    xs = x[:, r, 512 * st.n:512 * st.n + 512]
                                    if st.new == 1.0:
                                        ins = dve.scalar_tensor_tensor(xs, xs, st.old, DB[bank][:, :], ALU.mult, ALU.add)
                                    else:
                                        ins = dve.scalar_tensor_tensor(xs, DB[bank][:, :], st.new, xs, ALU.mult, ALU.add)
                                    ins.then_inc(d_done[bank], 1)
                            elif k == "norm":
                                r = st.tile
                                for j in range(2):
                                    dve.wait_ge(d_done[2 * j + r], st.last_chunks[j] + 1)
                                dve.wait_ge(p_norm, 16 * (st.which + 1))
                                for j in range(2):
                                    last = dve.bn_stats(bst[:, r, j, :], x[:, r, 512 * j:512 * j + 512])
                                link(last)
                                link(dve.bn_aggr(bmv[:, r, :], bst[:, r, :, :].rearrange("p a b -> p (a b)")))
                                rs = rsqrt(1, bmv[:, r, 1:2], 1.0, LN_EPS)
                                link(dve.tensor_scalar(x[:, r, :], x[:, r, :], bmv[:, r, 0:1], rs[:, 0:1],
                                                       ALU.subtract, ALU.mult))
                                left, right = x[:, r, 0:HALF], x[:, r, HALF:D]
                                dve.tensor_tensor(right, right, b["ln"][:, 0, HALF:D], ALU.mult).then_inc(gained, 1)
                                link(dve.tensor_tensor(left, left, b["ln"][:, 0, 0:HALF], ALU.mult))
                                dve.tensor_tensor(left, left, b["ln"][:, 1, 0:HALF], ALU.add).then_inc(fed_left, 1)
                            elif k == "rms":
                                r = st.tile
                                slot, count = GAIN[st.which]
                                dve.wait_ge(p_gain[slot], 16 * count)
                                if st.which:
                                    for j in range(2):
                                        dve.wait_ge(d_done[2 * j + r], st.last_chunks[j] + 1)
                                dve.tensor_tensor(b["merged"][:, r, 0:HALF], x[:, r, 0:HALF], b["gain"][:, slot, 0:HALF],
                                                  ALU.mult).then_inc(fed_left, 1)
                            elif k == "root":
                                dve.wait_ge(sumsq, st.n)
                                if st.apply:
                                    r = st.tile
                                    rsqrt(1, ss2[:, r:r + 1], 1.0 / D, EPS, root[:, r:r + 1])
                                    dve.wait_ge(fed, st.n)
                                    dve.wait_ge(fed_left, st.n)
                                    dve.tensor_scalar(b["merged"][:, r, :], b["merged"][:, r, :], root[:, r:r + 1], None,
                                                      ALU.mult).then_inc(rows, 1)
                                else:
                                    rsqrt(R, ss2[:, 0:R], 1.0 / D, EPS, root[:, 0:R])
                                    dve.tensor_scalar(root[:, R:2 * R], root[:, 0:R], 0.5, None, ALU.mult).then_inc(scaled, 1)
                            elif k == "p_split":
                                dve.wait_ge(p_ready, 1)
                                dve.tensor_tensor(b["p_l"][:, :, :], b["p_raw"][:, :, :], b["p_h"][:, :, :].bitcast(F32),
                                                  ALU.subtract).then_inc(p_ready, 1)
                            elif k == "m_log":
                                dve.wait_ge(unit_done, st.c.u + 1)
                                dve.wait_ge(p_vec, 16)
                                for r in range(R):
                                    bank = 2 * st.c.pair + r
                                    dve.tensor_tensor(ifv[:, 8 * r:8 * r + 8], DB[bank][:, 0:8], b["vec2"][:, 144:152], ALU.add)\
                                       .then_inc(d_done[bank], 1)
                                for r in range(R):
                                    dve.wait_ge(d_done[2 * st.c.pair + r], st.c.nth + 1)
                                f = ifv.rearrange("p (r g) -> p r g", r=R)[:, :, MH:2 * MH]
                                dve.scalar_tensor_tensor(absf.rearrange("p (r h) -> p r h", r=R), f, -1.0, f, ALU.mult, ALU.max)\
                                   .then_inc(logs, 1)
                                l3 = lf.rearrange("p (r h) -> p r h", r=R)
                                link(dve.tensor_scalar(l3, f, 0.0, None, ALU.min))
                                dve.wait_ge(logs, 3)
                                dve.tensor_tensor(lf, lf, lnf, ALU.subtract).then_inc(logs, 1)
                            elif k == "conv":
                                dve.wait_ge(unit_done, st.c.u + 1)
                                dve.wait_ge(p_conv, 16)
                                for ct in range(2):
                                    c = 2 * st.i + ct
                                    bank = 2 * st.c.pair + ct
                                    t, w = b["mT"][:, c, :], b["convw"][:, c, :]
                                    dve.wait_ge(tapped, c + 1)
                                    for back in (1, 2, 3):
                                        ins = dve.scalar_tensor_tensor(t[:, back:S], DB[bank][:, 0:S - back],
                                                                       w[:, 3 - back:4 - back], t[:, back:S], ALU.mult, ALU.add)
                                        if back < 3:
                                            link(ins)
                                    ins.then_inc(d_done[bank], 1)
                            elif k == "conv_silu":
                                dve.wait_ge(conv_tanh, st.i + 1)
                                t = b["mT"][:, 2 * st.i:2 * st.i + 2, :]
                                last = dve.scalar_tensor_tensor(t, b["gt"][:, st.i % 2, :, 0:256], 1.0, t, ALU.add, ALU.mult)
                                last.then_inc(conv_out, 1)
                            elif k == "a_sum":
                                r = st.tile
                                dve.wait_ge(squared, r + 1)
                                dve.tensor_reduce(ssq[:, 20 * r:20 * r + 20], b["sq"][:, :].rearrange(
                                    "p (h k) -> p h k", h=AH + AKV), AXX, ALU.add).then_inc(summed, 1)
                                if r == R - 1:
                                    dve.wait_ge(summed, R)
                                    rs = rsqrt(40, ssq, 1.0 / ADH, EPS)
                                    dve.tensor_copy(rq2, rs).then_inc(summed, 1)
                            elif k == "m_gate":
                                dve.wait_ge(p_gain[0], 32)
                                for r in range(R):
                                    dve.wait_ge(d_done[2 * st.c.pair + r], st.c.nth + 1)
                                    link(dve.scalar_tensor_tensor(b["mo"][:, r, 512 * st.j:512 * st.j + 512], b["gt_a"][:, st.j, r, :],
                                                                  1.0, b["gain"][:, 0, 512 * st.j:512 * st.j + 512], ALU.add,
                                                                  ALU.mult))
                            elif k == "m_arow":
                                dve.wait_ge(s_ready, st.s + 1)
                                dve.wait_ge(p_bias, 16)
                                h = st.h
                                if h == 0:
                                    dve.tensor_copy(nb, SB[:, 256:264])
                                dve.tensor_tensor_reduce(b["Pn"][:, h, 0:256], SB[:, 0:256], b["masks"][:, 0, :], 1.0, 0.0,
                                                         ALU.add, ALU.max, mx2[:, 4 + h:5 + h])
                                dve.tensor_tensor_reduce(b["Pn"][:, h, 256:384], SB[:, 0:128], b["masks"][:, 0, 128:256], 1.0,
                                                         0.0, ALU.add, ALU.max, mx2[:, h:h + 1]).then_inc(s_done, 1)
                                dve.wait_ge(s_done, st.s + 1)
                                dve.tensor_scalar(nmx2[:, h:h + 5:4], mx2[:, h:h + 5:4], -1.0, None, ALU.mult).then_inc(maxed, 1)
                            elif k == "m_floor":
                                dve.wait_ge(maxed, AH + MH)
                                dve.tensor_tensor(fl, nb, nmx2[:, 0:8], ALU.add).then_inc(floored, 1)
                            elif k == "m_s":
                                dve.wait_ge(s_ready, st.s + 1)
                                dve.wait_ge(soft, AH + st.h + 1)
                                h = st.h
                                for r in (1, 0):
                                    part = slice(0, 256) if r else slice(256, 384)
                                    ins = dve.tensor_tensor_reduce(b["Pn"][:, h, part], SB[:, part], b["Pn"][:, h, part],
                                                                   0.25 * MDH ** -0.5, 0.0, ALU.mult, ALU.add,
                                                                   den[:, 4 * r + h:4 * r + h + 1])
                                ins.then_inc(s_done, 1)
                                dve.wait_ge(s_done, st.s + 1)
                                dve.wait_ge(floored, 2)
                                d2 = rec2[:, h:h + 5:4]
                                link(dve.scalar_tensor_tensor(d2, den[:, h:h + 5:4], -1.0, den[:, h:h + 5:4], ALU.mult, ALU.max))
                                link(dve.tensor_tensor(d2, d2, fl[:, h:h + 5:4], ALU.max))
                                dve.reciprocal(d2, d2).then_inc(rec_done, 1)
                            elif k == "m_fin":
                                dve.wait_ge(o_done, st.o + 1)
                                rs = rsqrt(8, ss2[:, 0:8], 1.0 / MDH, EPS)
                                link(dve.tensor_scalar(rs, rs, 0.5, None, ALU.mult))
                                for h in range(MH):
                                    for r in range(R):
                                        part = b["mo"][:, r, h * MDH:(h + 1) * MDH]
                                        last = dve.scalar_tensor_tensor(part, b["m_o"][:, r, h * MDH:(h + 1) * MDH],
                                                                        rs[:, 2 * h + r:2 * h + r + 1], part, ALU.mult, ALU.mult)
                                last.then_inc(rows, 1)
                            elif k == "aa_s":
                                dve.wait_ge(s_ready, st.s + 1)
                                n = st.h
                                if n == 0:
                                    dve.wait_ge(p_bias, 16)
                                sink = b["vec2"][:, 128 + n:129 + n]
                                dve.tensor_tensor_reduce(b["Pn"][:, n % 4, 0:256], SB[:, 0:256], b["masks"][:, 1, :],
                                                         ADH ** -0.5, sink, ALU.add, ALU.max, mx2[:, 16 + n:17 + n])
                                dve.tensor_tensor_reduce(b["Pn"][:, n % 4, 256:384], SB[:, 256:384], b["masks"][:, 1, 128:256],
                                                         ADH ** -0.5, sink, ALU.add, ALU.max, mx2[:, n:n + 1]).then_inc(s_done, 1)
                                dve.wait_ge(s_done, st.s + 1)
                                ins = dve.tensor_scalar(nmx2[:, n:n + 17:16], mx2[:, n:n + 17:16], -1.0, None, ALU.mult)
                                if n % 4 == 3:
                                    link(ins)
                                    g = n - 3
                                    ins = dve.tensor_tensor(es.rearrange("p (r h) -> p r h", r=R),
                                                            nmx2.rearrange("p (r h) -> p r h", r=R)[:, :, g:g + 4],
                                                            b["vec2"][:, 128 + g:132 + g].unsqueeze(1).broadcast_to([P, R, 4]), ALU.add)
                                ins.then_inc(maxed, 1)
                            elif k == "aa_out":
                                dve.wait_ge(o_ready, st.o + 1)
                                g = st.h - 3
                                r3 = rc[:, 0:8].rearrange("p (r h) -> p r h", r=R)
                                dve.wait_ge(soft, st.h + 1)
                                link(dve.tensor_tensor(r3, sm2.rearrange("p (r h) -> p r h", r=R)[:, :, g:g + 4],
                                                       es.rearrange("p (r h) -> p r h", r=R), ALU.add))
                                link(dve.reciprocal(rc[:, 0:8], rc[:, 0:8]))
                                for r in range(R):
                                    dst = b["aqk"][:, r, ADH * g:ADH * g + 256].rearrange("p (h n) -> p h n", h=4)
                                    last = dve.tensor_tensor(dst, OB[:, 256 * r:256 * r + 256].rearrange("p (h n) -> p h n", h=4),
                                                             rc[:, 4 * r:4 * r + 4].unsqueeze(2).broadcast_to([P, 4, ADH]), ALU.mult)
                                last.then_inc(o_done, 1)
                            elif k in ("merge2", "ple"):
                                if st.early:
                                    dve.wait_ge(first_done, st.early)
                                else:
                                    dve.wait_ge(unit_done, st.c.u + 1)
                                for r in range(R):
                                    dve.wait_ge(d_done[2 * st.gate.pair + r], st.gate.nth + 1)
                                for r in range(R) if st.tile is None else (st.tile,):
                                    bank = 2 * st.c.pair + r
                                    g = b[st.which][:, st.j, r, :]
                                    cols = slice(st.j * 512, (st.j + 1) * 512)
                                    first = st.first
                                    dve.scalar_tensor_tensor(b["merged"][:, r, cols] if first else g, g, 1.0, DB[bank][:, :],
                                                             ALU.add, ALU.mult).then_inc(d_done[bank], 1)
                                    dve.wait_ge(d_done[bank], st.c.nth + 1)
                                    if k == "ple":
                                        link(dve.scalar_tensor_tensor(x[:, r, cols], g, 0.5, x[:, r, cols], ALU.mult, ALU.add))
                                    elif not first:
                                        last = dve.tensor_tensor(b["merged"][:, r, cols], b["merged"][:, r, cols], g, ALU.add)
                                        if st.rows:
                                            last.then_inc(rows, 1)
                                        else:
                                            link(last)
                            elif k == "swiglu":
                                for r in range(R):
                                    bank = 2 * st.c.pair + r
                                    dve.wait_ge(silu, 2 * st.m + r + 1)
                                    if st.width < 256:
                                        dve.memset(b["ffn_a"][:, st.i % 2, r, st.width:256], 0.0)
                                    dst, s_in = [b[name][:, st.i % 2, r, 0:st.width] for name in ("ffn_a", "ffn_s")]
                                    up = DB[bank][:, st.width:2 * st.width]
                                    if st.scaled:
                                        ins = dve.scalar_tensor_tensor(dst, up, root[:, r:r + 1], s_in, ALU.mult, ALU.mult)
                                    else:
                                        ins = dve.tensor_tensor(dst, s_in, up, ALU.mult)
                                    ins.then_inc(d_done[bank], 1)

                    @block.tensor
                    def _(pe):
                        def turned(t):
                            pe.wait_ge(t_done[t % 2], t // 2 + 1)
                            if t:
                                pe.wait_ge(t_done[(t - 1) % 2], (t - 1) // 2 + 1)

                        for st in steps:
                            k = st.kind
                            if k in ("unit", "first_tile"):
                                tiles = st.tiles or range(R)
                                if st.first and st.nth:
                                    for r in tiles:
                                        pe.wait_ge(d_done[2 * st.pair + r], st.nth)
                                if st.after_t is not None:
                                    turned(st.after_t)
                                pe.wait_ge(lo_done, st.u + 1)
                                if st.lhs == "p":
                                    pe.wait_ge(p_ready, 2)
                                lh, ll = split_of[st.lhs]
                                s = st.u % NS
                                if st.form == "features":
                                    for ct in range(2):
                                        out = DB[2 * st.pair + ct][:, 0:S]
                                        for i in range(st.nk):
                                            kt, at = st.kt0 + i, i * st.n + ct * P
                                            w_h, w_l = wh[:, s, at:at + P], wl[:, s, at:at + P]
                                            pe.matmul(out, w_h, lh[:, kt, :], start=st.first and i == 0, stop=False)
                                            pe.matmul(out, w_h, ll[:, kt, :], start=False, stop=False)
                                            last = pe.matmul(out, w_l, lh[:, kt, :], start=False,
                                                             stop=st.last and i == st.nk - 1)
                                    last.then_inc(unit_done, 1)
                                    continue
                                for r in tiles:
                                    out = DB[2 * st.pair + r][:, 0:st.n]
                                    for i in range(st.nk):
                                        kt = st.kt0 + i
                                        h, lo = lh[:, kt, r * P:r * P + P], ll[:, kt, r * P:r * P + P]
                                        w_h, w_l = wh[:, s, i * st.n:(i + 1) * st.n], wl[:, s, i * st.n:(i + 1) * st.n]
                                        pe.matmul(out, h, w_h, start=st.first and i == 0, stop=False)
                                        pe.matmul(out, h, w_l, start=False, stop=False)
                                        last = pe.matmul(out, lo, w_h, start=False, stop=st.last and i == st.nk - 1)
                                last.then_inc(first_done if k == "first_tile" else unit_done, 1)
                            elif k in ("split", "split_act", "turn", "a_turn", "probs_T"):
                                bank = TB[st.t % 2]
                                if st.t >= 2:
                                    pe.wait_ge(t_done[st.t % 2], st.t // 2)
                                if k == "split":
                                    if st.t == 0:
                                        pe.wait_ge(x_loaded, 32)
                                    if st.rows:
                                        pe.wait_ge(rows, st.rows)
                                    if st.fed:
                                        pe.wait_ge(fed if st.kg else fed_left, st.fed)
                                    if st.after_o:
                                        pe.wait_ge(o_done, st.after_o)
                                    src = [b[st.src][:, st.tile, (st.kg + i) * P:(st.kg + i + 1) * P] for i in range(4)]
                                elif k == "split_act":
                                    for r in range(R):
                                        pe.wait_ge(d_done[2 * st.made.pair + r], st.made.nth + 1)
                                    src = [b["ffn_a"][:, st.i % 2, r, i * P:(i + 1) * P] for i in range(2) for r in range(R)]
                                elif k == "a_turn":
                                    pe.wait_ge(a_normed, st.tile + 1)
                                    if st.half == 2:
                                        src = [b["akd"][:, st.tile, i, :, :].rearrange("p a k -> p (a k)") for i in range(AKV)]
                                    else:
                                        src = [b["aqk"][:, st.tile, (4 * st.half + i) * P:(4 * st.half + i + 1) * P] for i in range(4)]
                                elif k == "turn":
                                    if st.roped:
                                        pe.wait_ge(roped, st.roped)
                                    else:
                                        for r in range(R):
                                            pe.wait_ge(d_done[2 * st.kept.c.pair + r], st.kept.c.nth + 1)
                                    src = [b[st.src][:, st.tile, i * P:(i + 1) * P] for i in range(4)]
                                else:
                                    if st.of == "ca" or st.of == "aa":
                                        pe.wait_ge(soft, st.n)
                                    elif st.of == "da":
                                        pe.wait_ge(mixed, st.n)
                                    else:
                                        pe.wait_ge(s_done, st.n)
                                    pn = b["Pn"][:, st.slot, :]
                                    src = [pn[:, 256:384], pn[:, 0:128], pn[:, 128:256]]
                                for i, piece in enumerate(src):
                                    last = pe.transpose(bank[:, i * P:(i + 1) * P], piece, ident[:, :])
                                last.then_inc(t_ready[st.t % 2], 1)
                            elif k == "ret_s":
                                if st.s:
                                    pe.wait_ge(s_done, st.s)
                                turned(st.after_t)
                                h = st.h
                                pe.matmul(SB[:, 0:256], b["kT"][:, h, 0:P], b["qT"][:, h, :], start=True, stop=True)
                                pe.matmul(SB[:, 256:384], b["kT"][:, h, P:S], b["qT"][:, h, P:S], start=True, stop=True)\
                                  .then_inc(s_ready, 1)
                            elif k in ("ca_s", "da_s"):
                                if st.s:
                                    pe.wait_ge(s_done, st.s)
                                turned(st.after_t)
                                n = st.h if k == "ca_s" else st.g
                                p0 = 64 * (n % 2)
                                qT, kT = b["qT"][p0:p0 + 64, n // 2, :], b["kT"][p0:p0 + 64, n // 2, :]
                                pe.matmul(SB[:, 0:256], qT[:, P:S], kT, start=True, stop=True)
                                pe.matmul(SB[:, 256:384], qT[:, 0:P], kT[:, 0:P], start=True, stop=True)\
                                  .then_inc(s_ready, 1)
                            elif k == "m_arow":
                                if st.s:
                                    pe.wait_ge(s_done, st.s)
                                pe.wait_ge(spread_out, 2)
                                pe.wait_ge(p_bias, 16)
                                h, tri = st.h, b["masks"][:, 2, :]
                                lb, ib = b["lfb"], b["ib"]
                                if h == 0:
                                    pe.matmul(SB[:, 256:260], tri[:, 0:P], lf[:, 0:MH], start=True, stop=True)
                                    pe.matmul(SB[:, 260:264], tri[:, P:S], lf[:, 0:MH], start=True, stop=False)
                                    pe.matmul(SB[:, 260:264], tri[:, 0:P], lf[:, MH:2 * MH], start=False, stop=True)
                                pe.matmul(SB[:, 0:P], lb[:, 0, h, :], tri[:, 0:P], start=True, stop=False)
                                pe.matmul(SB[:, 0:P], ib[:, 0, h, :], ident[:, :], start=False, stop=True)
                                pe.matmul(SB[:, P:S], lb[:, 0, h, :], tri[:, P:S], start=True, stop=False)
                                pe.matmul(SB[:, P:S], lb[:, 1, h, :], tri[:, 0:P], start=False, stop=False)
                                pe.matmul(SB[:, P:S], ib[:, 1, h, :], ident[:, :], start=False, stop=True).then_inc(s_ready, 1)
                            elif k == "m_s":
                                if st.s:
                                    pe.wait_ge(s_done, st.s)
                                pe.wait_ge(conv_out, 8)
                                for r, cols in ((1, slice(0, 256)), (0, slice(256, 384))):
                                    for kk in range(2):
                                        ins = pe.matmul(SB[:, cols], b["mT"][:, 2 * st.h + kk, r * P:r * P + P],
                                                        b["mT"][:, 8 + 2 * st.h + kk, 0:(r + 1) * P], start=kk == 0, stop=kk == 1)
                                ins.then_inc(s_ready, 1)
                            elif k == "m_pv":
                                turned(st.t)
                                if st.o:
                                    pe.wait_ge(o_done, st.o)
                                for kept in st.kept:
                                    for r in range(R):
                                        pe.wait_ge(d_done[2 * kept.c.pair + r], kept.c.nth + 1)
                                pt = b["PT"][:, st.h % 2, :]
                                vs = [b["mv"][:, r, st.h * MDH:(st.h + 1) * MDH] for r in range(R)]
                                pe.matmul(OB[:, 0:MDH], pt[:, 0:P], vs[0], start=True, stop=True)
                                pe.matmul(OB[:, MDH:512], pt[:, P:S], vs[0], start=True, stop=False)
                                pe.matmul(OB[:, MDH:512], pt[:, S:384], vs[1], start=False, stop=True).then_inc(o_ready, 1)
                            elif k == "aa_s":
                                if st.s:
                                    pe.wait_ge(s_done, st.s)
                                turned(st.after_t)
                                p0 = 64 * (st.h % 2)
                                qT, kT = b["aqT"][p0:p0 + 64, st.h // 2, :], b["akT"][p0:p0 + 64, st.h // 4, :]
                                pe.matmul(SB[:, 0:256], qT[:, P:S], kT, start=True, stop=True)
                                pe.matmul(SB[:, 256:384], qT[:, 0:P], kT[:, 0:P], start=True, stop=True).then_inc(s_ready, 1)
                            elif k == "aa_pv":
                                turned(st.t)
                                if st.h % 4 == 0:
                                    if st.o:
                                        pe.wait_ge(o_done, st.o)
                                for r in range(R):
                                    pe.wait_ge(d_done[2 * st.kept.c.pair + r], st.kept.c.nth + 1)
                                pt = b["PT"][:, st.h % 2, :]
                                kv = st.h // 4
                                out = [OB[:, 256 * r + ADH * (st.h % 4):256 * r + ADH * (st.h % 4 + 1)] for r in range(R)]
                                vs = [b["av"][:, r, kv * ADH:(kv + 1) * ADH] for r in range(R)]
                                pe.matmul(out[0], pt[:, 0:P], vs[0], start=True, stop=True)
                                pe.matmul(out[1], pt[:, P:S], vs[0], start=True, stop=False)
                                last = pe.matmul(out[1], pt[:, S:384], vs[1], start=False, stop=True)
                                if st.h % 4 == 3:
                                    last.then_inc(o_ready, 1)
                            elif k == "ret_pv":
                                pe.wait_ge(s_done, st.s + 1)
                                if st.o:
                                    pe.wait_ge(o_done, st.o)
                                for kept in st.kept:
                                    for r in range(R):
                                        pe.wait_ge(d_done[2 * kept.c.pair + r], kept.c.nth + 1)
                                pr = b["Pn"][:, st.h % 4, :]
                                vs = [b["rv"][:, r, st.h * RDV:(st.h + 1) * RDV] for r in range(R)]
                                pe.matmul(OB[:, 0:RDV], pr[:, 0:P], vs[0], start=True, stop=True)
                                pe.matmul(OB[:, RDV:512], pr[:, P:S], vs[0], start=True, stop=False)
                                pe.matmul(OB[:, RDV:512], pr[:, S:384], vs[1], start=False, stop=True).then_inc(o_ready, 1)
                            elif k in ("ca_pv", "da_pv"):
                                turned(st.t)
                                if k == "da_pv" or st.h % 4 == 0:
                                    if st.o:
                                        pe.wait_ge(o_done, st.o)
                                for r in range(R):
                                    pe.wait_ge(d_done[2 * st.kept.c.pair + r], st.kept.c.nth + 1)
                                pt = b["PT"][:, st.h % 2, :]
                                if k == "ca_pv":
                                    out = [OB[:, 256 * r + CDH * (st.h % 4):256 * r + CDH * (st.h % 4 + 1)] for r in range(R)]
                                    vs = [b["cv"][:, r, st.h * CDH:(st.h + 1) * CDH] for r in range(R)]
                                else:
                                    out = [OB[:, r * P:(r + 1) * P] for r in range(R)]
                                    vs = [b["dv"][:, r, st.h * P:(st.h + 1) * P] for r in range(R)]
                                pe.matmul(out[0], pt[:, 0:P], vs[0], start=True, stop=True)
                                pe.matmul(out[1], pt[:, P:S], vs[0], start=True, stop=False)
                                last = pe.matmul(out[1], pt[:, S:384], vs[1], start=False, stop=True)
                                if k == "da_pv" or st.h % 4 == 3:
                                    last.then_inc(o_ready, 1)

                nc.all_engine_barrier(sems_to_clear=range(first_cleared, last_cleared + 1))

        with nc.Block() as block:
            @block.sync
            def _(sp):
                last = 1 if plan2.steps else 0
                for s in range(NRAW):
                    sp.wait_ge(w_loaded[s], 16 * (slot_base[last][s] + DEPTH * cnt[last][s] + 1))
                sp.dma_start(a["out"].rearrange("(r p) d -> p r d", p=P), x[:, :, :]).then_inc(stored, 16)
                sp.wait_ge(stored, 16)


def constants():
    f = np.float32
    n = np.arange(S)
    c = {"ident": np.eye(P, dtype=f)}
    lg = np.log1p(-np.exp2(-5.0 - np.arange(RH)))
    dist = n[None, :] - n[:, None]
    same = n[None, :] // CHUNK == n[:, None] // CHUNK
    seen = n[None, :] // CHUNK > n[:, None] // CHUNK
    dec = np.exp(lg[:, None, None] * np.abs(dist)) * (same | seen) * RDK ** -0.5
    c["decay"] = np.concatenate([dec[:, :P, :], dec[:, P:, P:]], 2).transpose(1, 0, 2).astype(f)
    rope = np.zeros((S, 2, 96), f)
    for d, at in ((RDK, 0), (DDH, RDK // 2)):
        inv = (f(ROPE_THETA) ** (-np.arange(0, d, 2, dtype=f) / f(d))).astype(f)
        ang = (n.astype(f)[:, None] * inv[None, :]).astype(f)
        rope[:, 0, at:at + d // 2], rope[:, 1, at:at + d // 2] = np.cos(ang), np.sin(ang)
    c["rope"] = rope.reshape(R, P, 2, 96).transpose(1, 0, 2, 3)
    m = np.zeros((P, S), f)
    m[:CHUNK, 192:] = NEG * DDH ** 0.5
    c["dmask"] = m
    i, j = np.arange(P)[:, None], np.arange(S)[None, :]
    causal = np.where(j <= P + i, 0.0, NEG)
    window = np.where((j <= P + i) & (P + i - j < WINDOW), 0.0, NEG * ADH ** 0.5)
    tri = np.where((j >= i) | (j >= P), -1.0, 0.0)
    c["masks"] = np.stack([causal, window, tri], 1).astype(f)
    return c


def weight_stream(inputs, plans, suffixes):
    total = sum(DEPTH * len(p.units) for p in plans) + NRAW
    out = np.zeros((total, P, UNIT), np.float32)
    at = 0
    for plan, suffix in zip(plans, suffixes):
        for l in range(DEPTH):
            for (names, cols), kt0, nk, n in plan.units:
                names = (names,) if isinstance(names, str) else names
                mats = [inputs[name + suffix][l] for name in names]
                k0, k1 = kt0 * P, min((kt0 + nk) * P, mats[0].shape[0])
                part = np.concatenate([m[k0:k1, c0:c1] for m in mats for c0, c1 in cols], 1)
                full = np.zeros((nk * P, n), np.float32)
                full[:k1 - k0] = part
                out[at, :, :nk * n] = full.reshape(nk, P, n).transpose(1, 0, 2).reshape(P, nk * n)
                at += 1
    return out


def spread(*vectors):
    v = np.concatenate([np.asarray(x, np.float32).reshape(DEPTH, -1) for x in vectors], 1)
    return np.ascontiguousarray(np.broadcast_to(v[:, None, :], (DEPTH, P, v.shape[1])))


def finish_plan(p):
    n = m = 0
    seen_t = None
    last_chunks = [0, 0]
    o = 0
    p.steps = [st for st in p.steps if st.kind != "pause"]
    for st in p.steps:
        if st.kind in ("split", "split_act"):
            n += 1
            st.n = n
        if st.kind == "resid":
            last_chunks[st.c.pair] = st.c.nth
        if st.kind in ("unit", "first_tile"):
            if st.after_t == seen_t or st.lhs == "p":
                st.after_t = None
            else:
                seen_t = st.after_t
        if st.kind == "swiglu":
            st.m = m
            m += 1
        if st.kind in ("norm", "rms"):
            st.last_chunks = tuple(last_chunks)
        if st.o is not None:
            o = st.o
        if st.kind in ("ret_fin", "da_fin", "m_fin"):
            st.o = o
    return p


def kernel(**inputs):
    import concourse.bacc as bacc
    from concourse.bass_utils import run_bass_kernel_spmd as run
    inputs = {k: np.asarray(v) for k, v in inputs.items()}
    plan1 = finish_plan(plan_block1())
    plan2 = finish_plan(plan_block2())
    f = np.float32
    arrays = dict(constants())
    arrays["x"] = inputs["x"][0]
    arrays["weights"] = weight_stream(inputs, [plan1, plan2], ["", "_2"])
    rb = inputs["ca_rel_bias"]
    idx = 384 + np.arange(P)[:, None] - np.arange(S)[None, :]
    arrays["bias"] = np.ascontiguousarray(rb[:, :, idx].transpose(0, 2, 1, 3)).reshape(DEPTH, P, CH * S)
    li = np.array([[0.8 - 0.6 * math.exp(-0.3 * l), 0.6 * math.exp(-0.3 * l) + 0.2] for l in range(DEPTH)], f)
    arrays["vec"] = spread(inputs["ret_norm_g"], inputs["da_norm_g"], inputs["da_lambda_q1"], inputs["da_lambda_k1"],
                           inputs["da_lambda_q2"], inputs["da_lambda_k2"], li)
    arrays["b_merge"] = spread(inputs["b_merge"])
    arrays["ln1"] = spread(inputs["ln1_g"], inputs["ln1_b"])
    arrays["ln2"] = spread(inputs["ln2_g"], inputs["ln2_b"])
    for key, name in (("gain_ffn1", "ffn1_norm_2"), ("gain_mix", "mix_norm_2"), ("gain_m", "m_out_norm_2"),
                      ("gain_ffn2", "ffn2_norm_2"), ("gain_ple", "ple_norm_2")):
        arrays[key] = spread(inputs[name])
    arrays["vec2"] = spread(inputs["a_q_norm_2"], inputs["a_k_norm_2"], inputs["a_sinks_2"], inputs["m_igate_b_2"],
                            inputs["m_fgate_b_2"])
    taps = np.concatenate([inputs["m_conv_w_2"], inputs["m_conv_b_2"][:, None, :]], 1)
    arrays["convw"] = taps.reshape(DEPTH, CONV_K + 1, 16, P).transpose(0, 3, 2, 1).reshape(DEPTH, P, 16 * (CONV_K + 1))
    pt = inputs["p_2"][:, 0].transpose(0, 2, 1)
    arrays["p"] = pt.reshape(DEPTH, 2, P, S).transpose(0, 2, 1, 3).reshape(DEPTH, P, 2 * S)
    nc = bacc.Bacc("TRN2", target_bir_lowering=False, num_devices=1)
    arrays = {"in_" + k: np.ascontiguousarray(v) for k, v in arrays.items()}
    a = {k[3:]: nc.dram_tensor(k, v.shape, F32, kind="ExternalInput").ap() for k, v in arrays.items()}
    a["out"] = nc.dram_tensor("out", (S, D), F32, kind="ExternalOutput").ap()
    build(nc, plan1, plan2, a)
    r = run(nc, [arrays], core_ids=[0])
    return r.results[0]["out"].reshape(1, S, D)
```
